# Optimizing a Trainium2 kernel written in Bass

```python
import jax, jax.numpy as jnp
from jax import lax
import numpy as np

D_MODEL = 1024
BATCH = 1
SEQ = 512
DEPTH = 2

N_MIXERS = 2
CHUNK = 128
GMLP_WIDTH = D_MODEL
GMLP_GROUPS = 8
GMLP_GROUP_DIM = GMLP_WIDTH // GMLP_GROUPS
RWKV_HEAD = 64
RWKV_HEADS = D_MODEL // RWKV_HEAD
DECAY_LORA = 64
AAA_LORA = 64
MV_LORA = 32
GATE_LORA = 160
D_FF = 4 * D_MODEL
N_A = (DEPTH + 1) // 2
N_B = DEPTH // 2
N_VRES = max(N_B - 1, 0)
ALPHA = (2.0 * DEPTH) ** 0.25
BETA = (8.0 * DEPTH) ** -0.25
LN_EPS = 1e-5
GN_EPS = 64e-5

kernel_name = 'hybrid_gmlp_rwkv7_deepnorm_trunk'

def _layer_norm(x, g, b, eps):
    xf = x.astype(jnp.float32)
    mean = jnp.mean(xf, axis=-1, keepdims=True)
    var = jnp.mean(jnp.square(xf - mean), axis=-1, keepdims=True)
    y = (xf - mean) * lax.rsqrt(var + eps)
    return (y * g.astype(jnp.float32) + b.astype(jnp.float32)).astype(x.dtype)

def _gmlp_mixer(x, w_in, vn_g, vn_b, ws, bs, w_out):
    B, S, _ = x.shape
    z = jax.nn.gelu(x @ w_in, approximate=False)
    u, v = jnp.split(z, 2, axis=-1)
    v = _layer_norm(v, vn_g, vn_b, LN_EPS)
    v = v.reshape(B, S // CHUNK, CHUNK, GMLP_GROUPS, GMLP_GROUP_DIM)
    causal = jnp.tril(jnp.ones((CHUNK, CHUNK), dtype=bool))
    ws_c = jnp.where(causal[None], ws, jnp.zeros_like(ws)).astype(v.dtype)
    mixed = jnp.einsum('gts,bcsgd->bctgd', ws_c, v) + bs.T[None, None, :, :, None]
    gated = u * mixed.reshape(B, S, GMLP_WIDTH)
    return gated @ w_out

def _token_shift(x):
    return jnp.pad(x, ((0, 0), (1, 0), (0, 0)))[:, :-1, :]

def _wkv7(r, decay, k, v, kk, b):
    xs = tuple(jnp.moveaxis(t.astype(jnp.float32), 1, 0) for t in (r, decay, k, v, kk, b))
    Bsz, _, H, N = r.shape

    def step(state, inp):
        r_t, w_t, k_t, v_t, kk_t, b_t = inp
        sa = jnp.einsum('bhij,bhj->bhi', state, -kk_t)
        state = (state * w_t[:, :, None, :] + sa[..., None] * b_t[:, :, None, :]
                 + v_t[..., None] * k_t[:, :, None, :])
        y = jnp.einsum('bhij,bhj->bhi', state, r_t)
        return state, y

    s0 = jnp.zeros((Bsz, H, N, N), jnp.float32)
    _, ys = lax.scan(step, s0, xs)
    return jnp.moveaxis(ys, 0, 1)

def _rwkv7_mixer(x, v_first, mu, w_rkv, w0, w1, w2, a0, a1, a2, g1, g2,
                 k_k, k_a, r_k, gn_g, gn_b, w_o, vres):
    B, S, D = x.shape
    H, N = RWKV_HEADS, RWKV_HEAD
    xx = _token_shift(x) - x
    xr, xw, xk, xv, xa, xg = (x + xx * mu[i] for i in range(6))
    r = xr @ w_rkv[0]
    k = xk @ w_rkv[1]
    v = xv @ w_rkv[2]
    w_log = -jax.nn.softplus(-(w0 + jnp.tanh(xw @ w1) @ w2)) - 0.5
    decay = jnp.exp(-jnp.exp(w_log.astype(jnp.float32)))
    a = jax.nn.sigmoid(a0 + (xa @ a1) @ a2)
    g = jax.nn.sigmoid(xg @ g1) @ g2
    if vres is None:
        v_first = v
    else:
        v0, v1, v2 = vres
        v = v + (v_first - v) * jax.nn.sigmoid(v0 + (xv @ v1) @ v2)
    kk = (k * k_k).reshape(B, S, H, N).astype(jnp.float32)
    kk = kk / jnp.maximum(jnp.sqrt(jnp.sum(kk * kk, axis=-1, keepdims=True)), 1e-12)
    k = k * (1.0 + (a - 1.0) * k_a)
    rh = r.reshape(B, S, H, N)
    kh = k.reshape(B, S, H, N)
    vh = v.reshape(B, S, H, N)
    ah = a.reshape(B, S, H, N).astype(jnp.float32)
    y = _wkv7(rh, decay.reshape(B, S, H, N), kh, vh, kk, kk * ah)
    mean = jnp.mean(y, axis=-1, keepdims=True)
    var = jnp.mean(jnp.square(y - mean), axis=-1, keepdims=True)
    y = ((y - mean) * lax.rsqrt(var + GN_EPS)).reshape(B, S, D)
    y = (y * gn_g.astype(jnp.float32) + gn_b.astype(jnp.float32)).astype(x.dtype)
    bonus = (jnp.sum(rh * kh * r_k, axis=-1, keepdims=True) * vh).reshape(B, S, D)
    return ((y + bonus) * g) @ w_o, v_first

def setup_inputs(seed: int = 0) -> dict:
    key = jax.random.key(seed)
    ks = iter(jax.random.split(key, 40))

    def nrm(shape, scale):
        return jax.random.normal(next(ks), shape, jnp.float32) * scale

    lin = jnp.arange(D_MODEL, dtype=jnp.float32) / (D_MODEL - 1)
    ratio = jnp.arange(N_B, dtype=jnp.float32) / max(N_B - 1, 1)
    decay_speed = -7.0 + 5.0 * lin[None, :] ** (0.85 + ratio[:, None] ** 0.5)
    return {
        'x': nrm((BATCH, SEQ, D_MODEL), 1.0),
        'ln1_g': 1.0 + nrm((DEPTH, D_MODEL), 0.02),
        'ln1_b': nrm((DEPTH, D_MODEL), 0.02),
        'ln2_g': 1.0 + nrm((DEPTH, D_MODEL), 0.02),
        'ln2_b': nrm((DEPTH, D_MODEL), 0.02),
        'ffn_w1': nrm((DEPTH, D_MODEL, D_FF), D_MODEL ** -0.5),
        'ffn_w2': nrm((DEPTH, D_FF, D_MODEL), D_FF ** -0.5 * BETA),
        'gm_w_in': nrm((N_A, D_MODEL, 2 * GMLP_WIDTH), D_MODEL ** -0.5),
        'gm_vn_g': 1.0 + nrm((N_A, GMLP_WIDTH), 0.02),
        'gm_vn_b': nrm((N_A, GMLP_WIDTH), 0.02),
        'gm_ws': nrm((N_A, GMLP_GROUPS, CHUNK, CHUNK), CHUNK ** -0.5),
        'gm_bs': 1.0 + nrm((N_A, GMLP_GROUPS, CHUNK), 0.1),
        'gm_w_out': nrm((N_A, GMLP_WIDTH, D_MODEL), GMLP_WIDTH ** -0.5 * BETA),
        'rw_mu': jax.random.uniform(next(ks), (N_B, 6, D_MODEL), jnp.float32),
        'rw_w_rkv': nrm((N_B, 3, D_MODEL, D_MODEL), D_MODEL ** -0.5),
        'rw_w0': decay_speed + 0.5 + nrm((N_B, D_MODEL), 0.1),
        'rw_w1': nrm((N_B, D_MODEL, DECAY_LORA), D_MODEL ** -0.5),
        'rw_w2': nrm((N_B, DECAY_LORA, D_MODEL), 0.1 * DECAY_LORA ** -0.5),
        'rw_a0': nrm((N_B, D_MODEL), 0.1),
        'rw_a1': nrm((N_B, D_MODEL, AAA_LORA), D_MODEL ** -0.5),
        'rw_a2': nrm((N_B, AAA_LORA, D_MODEL), 0.1 * AAA_LORA ** -0.5),
        'rw_g1': nrm((N_B, D_MODEL, GATE_LORA), D_MODEL ** -0.5),
        'rw_g2': nrm((N_B, GATE_LORA, D_MODEL), GATE_LORA ** -0.5),
        'rw_k_k': 0.85 + nrm((N_B, D_MODEL), 0.05),
        'rw_k_a': 1.0 + nrm((N_B, D_MODEL), 0.05),
        'rw_r_k': -0.04 + nrm((N_B, RWKV_HEADS, RWKV_HEAD), 0.1),
        'rw_gn_g': 1.0 + nrm((N_B, D_MODEL), 0.02),
        'rw_gn_b': nrm((N_B, D_MODEL), 0.02),
        'rw_w_o': nrm((N_B, D_MODEL, D_MODEL), D_MODEL ** -0.5 * BETA),
        'rw_v0': 1.0 + nrm((N_VRES, D_MODEL), 0.1),
        'rw_v1': nrm((N_VRES, D_MODEL, MV_LORA), D_MODEL ** -0.5),
        'rw_v2': nrm((N_VRES, MV_LORA, D_MODEL), 0.1 * MV_LORA ** -0.5),
    }

def reference(x, ln1_g, ln1_b, ln2_g, ln2_b, ffn_w1, ffn_w2,
              gm_w_in, gm_vn_g, gm_vn_b, gm_ws, gm_bs, gm_w_out,
              rw_mu, rw_w_rkv, rw_w0, rw_w1, rw_w2, rw_a0, rw_a1, rw_a2,
              rw_g1, rw_g2, rw_k_k, rw_k_a, rw_r_k, rw_gn_g, rw_gn_b, rw_w_o,
              rw_v0, rw_v1, rw_v2):
    h = x
    v_first = None
    for i in range(DEPTH):
        j = i // N_MIXERS
        if i % N_MIXERS == 0:
            mix = _gmlp_mixer(h, gm_w_in[j], gm_vn_g[j], gm_vn_b[j], gm_ws[j],
                              gm_bs[j], gm_w_out[j])
        else:
            vres = None if j == 0 else (rw_v0[j - 1], rw_v1[j - 1], rw_v2[j - 1])
            mix, v_first = _rwkv7_mixer(h, v_first, rw_mu[j], rw_w_rkv[j], rw_w0[j],
                                        rw_w1[j], rw_w2[j], rw_a0[j], rw_a1[j], rw_a2[j],
                                        rw_g1[j], rw_g2[j], rw_k_k[j], rw_k_a[j],
                                        rw_r_k[j], rw_gn_g[j], rw_gn_b[j], rw_w_o[j], vres)
        h = _layer_norm(ALPHA * h + mix, ln1_g[i], ln1_b[i], LN_EPS)
        f = jnp.square(jax.nn.relu(h @ ffn_w1[i])) @ ffn_w2[i]
        h = _layer_norm(ALPHA * h + f, ln2_g[i], ln2_b[i], LN_EPS)
    return h


_drawn_inputs = setup_inputs


def setup_inputs(seed=0):
    import zlib

    import numpy as np

    out = dict(_drawn_inputs(seed))
    spreads = {}
    factors = {'gm_vn_g': 8.0,
     'gm_vn_b': 8.0,
     'rw_w1': 8.0,
     'rw_w2': 8.0,
     'rw_a0': 6.705,
     'rw_a1': 7.191,
     'rw_a2': 7.186,
     'rw_k_k': 6.154,
     'rw_k_a': 4.955,
     'rw_gn_g': 8.0,
     'rw_gn_b': 8.0}
    for name, (base, spread) in spreads.items():
        noise = np.random.default_rng([zlib.crc32(name.encode()), seed]).standard_normal(out[name].shape)
        drawn = base * np.exp(spread * noise) if base else spread * noise
        out[name] = __import__('jax').numpy.asarray(drawn.astype(out[name].dtype))
    for name, factor in factors.items():
        out[name] = (out[name] * factor).astype(out[name].dtype)
    return out
```

```python
import math
from contextlib import ExitStack

import concourse.bass as bass
from concourse import mybir

P = 128
SLOTS = 4
LN_EPS = 1e-5
GN_EPS = 64e-5
BASE = 8
LEVELS = (8, 16, 32, 64)

ALU = mybir.AluOpType
ACT = mybir.ActivationFunctionType
AX = mybir.AxisListType
F32 = mybir.dt.float32
F32R = mybir.dt.float32r


class Tally:

    def __init__(self, sem):
        self.sem, self.n = sem, 0

    def inc(self, instruction):
        instruction.then_inc(self.sem, 1)
        self.n += 1
        return self.n


def trunk(nc, x, ln1_g, ln1_b, ln2_g, ln2_b, ffn_w1, ffn_w2, gm_w_in, gm_vn_g, gm_vn_b, gm_ws, gm_bs,
          gm_w_out, rw_mu, rw_w_rkv, rw_w0, rw_w1, rw_w2, rw_a0, rw_a1, rw_a2, rw_g1, rw_g2, rw_k_k,
          rw_k_a, rw_r_k, rw_gn_g, rw_gn_b, rw_w_o, out):
    _, S, D = x.shape
    depth, _, FF = ffn_w1.shape
    GROUPS = gm_ws.shape[1]
    TT, KT, FT = S // P, D // P, FF // P
    ALPHA = (2.0 * depth) ** 0.25
    HALF = D // 2
    HEADS, N = rw_r_k.shape[1:]
    LORA, GLORA = rw_w1.shape[2], rw_g1.shape[2]
    HH = HEADS // 2
    PAIRS = HH // 2
    DECAY = -math.exp(-0.5)
    MID = P // 2
    assert (S, D, HALF) == (512, 1024, 512) and GROUPS == KT and HH * N == HALF

    def rows(w, c0=0):
        v = w.rearrange("(k p) n -> k p n", p=P)
        return lambda k: v[k, :, c0:c0 + D]

    def columns(w):
        v = w.rearrange("(k p) (f c) -> f p k c", p=P, c=P)
        return lambda f: v[f]

    stream = [("v", "rows", KT, rows(gm_w_in[0], D)), ("u", "columns", KT, columns(gm_w_in[0][:, 0:D])),
              ("gm_out", "rows", KT, rows(gm_w_out[0])),
              ("up0", "columns", FT, columns(ffn_w1[0])), ("down0", "rows", FT, rows(ffn_w2[0])),
              ("key", "rows", KT, rows(rw_w_rkv[0, 1])), ("receptance", "rows", KT, rows(rw_w_rkv[0, 0])),
              ("value", "rows", KT, rows(rw_w_rkv[0, 2])), ("rw_out", "rows", KT, rows(rw_w_o[0])),
              ("up1", "columns", FT, columns(ffn_w1[1])), ("down1", "rows", FT, rows(ffn_w2[1]))]
    COUNT = {s[0]: s[2] for s in stream}
    row_products = [s[0] for s in stream if s[1] == "rows"]
    SLABS = sum(s[2] for s in stream)
    first_slab, first_act, at, act_at = {}, {}, 0, 0
    for name, kind, count, _ in stream:
        first_slab[name] = at
        at += count
        if kind == "rows":
            first_act[name] = act_at
            act_at += count

    with ExitStack() as ctx:
        here = [(nc.sbuf_base + 31) // 32 * 32]

        def sb(name, shape, dtype=F32, at=None):
            size = 4
            for s in shape[1:]:
                size *= s
            where = here[0] if at is None else at
            if at is None:
                here[0] += (size + 31) // 32 * 32
            place[name] = where
            return nc.alloc_sbuf_tensor_at(name, shape, dtype, offset=where)

        place = {}

        def sem(name):
            return ctx.enter_context(nc.semaphore(name))

        raw = sb("raw", [P, SLOTS, D])
        w_hi = sb("w_hi", [P, SLOTS, D], F32R)
        w_lo = sb("w_lo", [P, SLOTS, D], F32R)
        a_hi = sb("a_hi", [P, SLOTS, S], F32R)
        a_lo = sb("a_lo", [P, SLOTS, S], F32R)
        PAD = 8
        xT = sb("xT", [P, KT, PAD + S])
        x_tok = sb("x_tok", [P, TT, D])
        xT_hi = sb("xT_hi", [P, KT, S], F32R)
        xT_lo = sb("xT_lo", [P, KT, S], F32R)
        big = sb("big", [P, FT, S])
        gains = sb("gains", [P, 2, D])
        ident = sb("ident", [P, P])
        relu = sb("relu", [P, 2, S])
        stats = sb("stats", [P, 2, 6])
        mean_var = sb("mean_var", [P, 2])
        std = sb("std", [P, 1])
        rstd = sb("rstd", [P, 1])
        v_tok = sb("v_tok", [P, TT, D], at=place["big"])
        uT = sb("uT", [P, KT, S], at=place["big"] + 16384)
        gatedT = sb("gatedT", [P, KT, S], at=place["big"] + 32768)
        ws_in = sb("ws_in", [P, GROUPS, P], at=place["big"] + 49152)
        wsT = sb("wsT", [P, GROUPS, P], at=place["big"] + 53248)
        bs_all = sb("bs_all", [P, GROUPS, P], at=place["big"] + 57344)

        cursor = [0, 0]

        def over(name, shape):
            size = 4
            for n in shape[1:]:
                size *= n
            where, cursor[0] = cursor[0], cursor[0] + (size + 31) // 32 * 32
            assert cursor[0] <= cursor[1], name
            return sb(name, shape, at=where)

        cursor[:] = place["big"] + (FT * S - 4 * D) * 4, place["gains"]
        k_k, k_a, r_k = (over(name, [P, D]) for name in ("k_k", "k_a", "r_k"))
        state = over("state", [P, 2, PAIRS, P])
        cursor[:] = place["relu"], place["relu"] + 4 * D
        keep_before = over("keep_before", [P, 2, P])
        keep_block = over("keep_block", [P, P])
        keep_level = [over(f"keep_level{b}", [P, P]) for b in LEVELS]
        cumulate = over("cumulate", [P, P])
        cursor[:] = place["xT_hi"], place["k_k"]
        lw1 = over("lw1", [P, KT, LORA])
        la1 = over("la1", [P, KT, LORA])
        lg1 = over("lg1", [P, KT, GLORA])
        lw2 = over("lw2", [LORA + 1, D])
        la2 = over("la2", [LORA + 1, D])
        lg2 = over("lg2", [P, D])
        lg2b = over("lg2b", [GLORA - P, D])
        assert cursor[0] <= place["big"]
        low_w = over("low_w", [LORA + 1, S])
        low_a = over("low_a", [LORA + 1, S])
        low_g = over("low_g", [P, S])
        low_gb = over("low_gb", [GLORA - P, S])
        xxT = over("xxT", [P, KT, S])
        lora_mix = over("lora_mix", [P, 2, 3, S])
        mix = over("mix", [P, SLOTS, S])
        stage = over("stage", [P, 2, D])
        cursor[:] = place["xT_hi"], place["k_k"]
        given = over("given", [P, 2, 6, HALF])
        SIG, AA, GG, KK, RR, VV = range(6)
        tok = over("tok", [P, 4, HALF])
        A_, R_, B_, K_ = range(4)
        turned4 = over("turned4", [P, PAIRS, 4, P])
        gram = over("gram", [P, HH, 4, P])
        B_A, B_R, K_A, K_R = range(4)
        inv_t = over("inv_t", [P, HH, P])
        prep_at = cursor[0]
        m_full = over("m_full", [P, HH, P])
        n_one = over("n_one", [P, HH, P])
        buf2 = over("buf2", [P, HH, P])
        cursor[0] = prep_at
        kkn, p_mid, p_inv, p_prev, scratch = (over(name, [P, HALF]) for name in
                                              ("kkn", "p_mid", "p_inv", "p_prev", "scratch"))
        cursor[:] = place["a_hi"], place["xT"]
        buf3 = over("buf3", [P, HH, P])
        buf4 = over("buf4", [P, HH, P])
        xs = over("xs", [P, HALF])
        us = over("us", [P, HALF])
        yc = over("yc", [P, HALF])
        start = over("start", [P, PAIRS, P])
        cursor[1] = place["x_tok"]
        y_tok = over("y_tok", [P, TT, D])
        yT = sb("yT", [P, KT, S], at=place["big"])
        gn = sb("gn", [P, 2, D], at=place["gains"])
        rk = sb("rk", [P, HALF], at=place["xs"])
        mu = sb("mu", [P, 6, KT])
        mu_rows = sb("mu_rows", [6 * KT, P])
        halves = sb("halves", [P, 2])
        decays = sb("decays", [P, PAIRS, 2])
        small = sb("small", [P, 8, HH])
        SQ, NORM, RNORM, BONUS, YSUM, YVAR, YSTD, YR = range(8)

        inverse = [("turn", gram, None, m_full, "act"),
                   ("copy", buf2, n_one, buf3, "act"), ("copy", n_one, buf2, buf4, "act"),
                   ("add", buf4, inv_t, inv_t, "dve"), ("copy", buf3, buf4, buf2, "act"),
                   ("add", buf2, inv_t, inv_t, "dve")]
        for b in range(len(LEVELS)):
            inverse += [("turn", inv_t, None, buf4, "act"), ("mask", m_full, inv_t, buf3, "dve"),
                        ("add", buf4, buf3, inv_t, "dve")]
        STAGES = len(inverse)
        ON_ACT = [s for s in range(STAGES) if inverse[s][4] == "act"]
        ON_DVE = [s for s in range(STAGES) if inverse[s][4] == "dve"]

        proj = nc.dram_tensor("proj", (6, TT, P, D), F32, kind="Internal").ap()

        bank = [ctx.enter_context(nc.psum_tensor(f"bank{b}", [P, S], F32)) for b in range(8)]

        raw_in = [sem(f"raw_in{j}") for j in range(SLOTS)]
        w_hi_ready, w_lo_ready, slab_used = sem("w_hi_ready"), sem("w_lo_ready"), sem("slab_used")
        a_hi_ready, a_lo_ready = sem("a_hi_ready"), sem("a_lo_ready")
        tile_summed = sem("tile_summed")
        bank_read = sem("bank_read")
        squared = sem("squared")
        v_read = sem("v_read")
        x_in, gains_in, ws_arrived, bs_arrived = sem("x_in"), sem("gains_in"), sem("ws_arrived"), sem("bs_arrived")
        ident_ready, ws_masked, wsT_summed, wsT_ready = sem("ident_ready"), sem("ws_masked"), sem("wsT_summed"), sem("wsT_ready")
        x_turned, xT_ready, xT_split = sem("x_turned"), sem("xT_ready"), sem("xT_split")
        var_ready, std_ready, x_ready, v_ready = sem("var_ready"), sem("std_ready"), sem("x_ready"), sem("v_ready")
        mixed, gated = sem("mixed"), sem("gated")
        dve_done, pool_done = sem("dve_done"), sem("pool_done")
        stored = sem("stored")
        lora_in, rw_in, gn_in = sem("lora_in"), sem("rw_in"), sem("gn_in")
        lora_mixed, lora_used, lora_summed, low_ready = sem("lora_mixed"), sem("lora_used"), sem("lora_summed"), sem("low_ready")
        bank_projected, proj_read = sem("bank_projected"), sem("proj_read")
        stage_out = [sem("stage_out0"), sem("stage_out1")]
        x_mixed, ones_ready, masks_ready, state_zero = sem("x_mixed"), sem("ones_ready"), sem("masks_ready"), sem("state_zero")
        given_in = [sem("given_in0"), sem("given_in1")]
        given_used = sem("given_used")
        cum_summed, lx_ready, exp_ready = sem("cum_summed"), sem("lx_ready"), sem("exp_ready")
        kk_scaled, kk_squared, ss_ready, norm_ready, k_ready = (
            sem("kk_scaled"), sem("kk_squared"), sem("ss_ready"), sem("norm_ready"), sem("k_ready"))
        tok_ready, rk_ready, turned_summed, turned_ready = sem("tok_ready"), sem("rk_ready"), sem("turned_summed"), sem("turned_ready")
        gram_summed, gram_ready, base_ready = sem("gram_summed"), sem("gram_ready"), sem("base_ready")
        inv_summed, inv_copied, inv_added = sem("inv_summed"), sem("inv_copied"), sem("inv_added")
        start_ready, x_summed, xs_ready, u_summed, us_ready = (
            sem("start_ready"), sem("x_summed"), sem("xs_ready"), sem("u_summed"), sem("us_ready"))
        mu_in, mu_turned, mu_ready = sem("mu_in"), sem("mu_turned"), sem("mu_ready")
        y_summed, s_summed, state_ready = sem("y_summed"), sem("s_summed"), sem("state_ready")
        yc_ready, yq_ready, yvar_ready, ystd_ready, yr_ready, bonus_ready, y_done = (
            sem("yc_ready"), sem("yq_ready"), sem("yvar_ready"), sem("ystd_ready"), sem("yr_ready"),
            sem("bonus_ready"), sem("y_done"))
        step_dve, step_pool, y_turned, yT_ready = sem("step_dve"), sem("step_pool"), sem("y_turned"), sem("yT_ready")
        STEPS = 2 * TT

        def nth(t, half, per_step, k):
            return t * (2 * per_step) + (half * per_step + k)

        block = ctx.enter_context(nc.Block())

        @block.sync
        def _(sp):
            sp.dma_start(x_tok[:], x[0].rearrange("(t p) n -> p t n", p=P)).then_inc(x_in, 16)

            def load(name, source, i, j):
                n0 = first_slab[name]
                if n0 + j >= SLOTS or not isinstance(i, int) or i > 0:
                    sp.wait_ge(w_lo_ready, i * SLOTS + (n0 + j - SLOTS + 1))
                dst = raw[:, j, :]
                if dict((s[0], s[1]) for s in stream)[name] == "columns":
                    dst = dst.rearrange("p (k c) -> p k c", c=P)
                sp.dma_start(dst, source(i * SLOTS + j)).then_inc(raw_in[j], 16)

            def load_given(t, half):
                sp.dma_start(given[:, half, :, :],
                             proj[:, t, :, half * HALF:(half + 1) * HALF].rearrange("u p n -> p u n")
                             ).then_inc(given_in[half], 16)

            for name, _, count, source in stream:
                if count == KT:
                    for i in range(count // SLOTS):
                        if (name, i) == ("rw_out", 1):
                            for s in range(2):
                                sp.wait_ge(stage_out[s], 16 * 6 * TT // 2)
                            sp.wait_ge(slab_used, first_slab["rw_out"])
                            load_given(0, 0)
                            load_given(0, 1)
                            with sp.Fori(1, TT) as t:
                                for half in range(2):
                                    sp.wait_ge(given_used, t * 2 + (half - 1))
                                    load_given(t, half)
                        for j in range(SLOTS):
                            load(name, source, i, j)
                else:
                    with sp.Fori(0, count // SLOTS) as i:
                        for j in range(SLOTS):
                            load(name, source, i, j)
            sp.wait_ge(x_ready, 4 * TT)
            sp.dma_start(out[0].rearrange("(t p) n -> p t n", p=P), x_tok[:]).then_inc(stored, 16)
            sp.wait_ge(stored, 16)

        @block.gpsimd
        def _(pool):
            nc.gpsimd.memset(ident[:], 0.0).then_inc(pool_done, 1)
            pool.wait_ge(pool_done, 1)
            nc.gpsimd.affine_select(out=ident[:], in_=ident[:], compare_op=ALU.not_equal, fill=1.0, base=0,
                                    pattern=[[-1, P]], channel_multiplier=1).then_inc(ident_ready, 1)
            pool.wait_ge(ws_arrived, 16)
            nc.gpsimd.affine_select(out=ws_in[:], in_=ws_in[:], compare_op=ALU.is_ge, fill=0.0, base=0,
                                    pattern=[[0, GROUPS], [-1, P]], channel_multiplier=1).then_inc(ws_masked, 1)

            def low_weights(i, j):
                pool.wait_ge(w_hi_ready, i * SLOTS + (j + 1))
                nc.gpsimd.tensor_tensor(w_lo[:, j, :], raw[:, j, :], w_hi[:, j, :].bitcast(F32),
                                        ALU.subtract).then_inc(w_lo_ready, 1)

            def low_groups(first, end):
                with pool.Fori(first, end) as i:
                    for j in range(SLOTS):
                        low_weights(i, j)

            low_groups(0, first_slab["key"] // SLOTS)
            pool.wait_ge(squared, FT + 2)
            done = Tally(pool_done)
            done.n = 1

            def then(instruction):
                pool.wait_ge(pool_done, done.inc(instruction))

            def keep(out, compare, pattern, base, by_partition):
                then(nc.gpsimd.affine_select(out=out, in_=out, compare_op=compare, fill=0.0, base=base,
                                             pattern=pattern, channel_multiplier=by_partition))
            then(nc.gpsimd.memset(keep_before[:], 1.0))
            keep(keep_before[:, 0, :], ALU.is_gt, [[1, P]], 0, -1)
            keep(keep_before[:, 1, :], ALU.is_ge, [[1, P]], 0, -1)
            then(nc.gpsimd.memset(keep_block[:], 1.0))
            blocks = keep_block[:].rearrange("p (m c) -> p m c", c=BASE)
            keep(blocks, ALU.is_ge, [[-BASE, P // BASE], [0, BASE]], 0, 1)
            keep(blocks, ALU.is_ge, [[BASE, P // BASE], [0, BASE]], BASE - 1, -1)
            for b, level in zip(LEVELS, keep_level):
                then(nc.gpsimd.memset(level[:], 0.0))
                odd = level[:].rearrange("p (m e c) -> p m e c", e=2, c=b)[:, :, 1, :]
                then(nc.gpsimd.memset(odd, 1.0))
                keep(odd, ALU.is_ge, [[-2 * b, P // (2 * b)], [0, b]], 0, 1)
                keep(odd, ALU.is_ge, [[2 * b, P // (2 * b)], [0, b]], b - 1, -1)
            then(nc.gpsimd.memset(cumulate[0:MID, :], -DECAY))
            then(nc.gpsimd.memset(cumulate[MID:P, :], DECAY))
            keep(cumulate[0:MID, :], ALU.is_gt, [[-1, P]], 0, 1)
            keep(cumulate[MID:P, :], ALU.is_ge, [[1, P]], -MID, -1)
            then(nc.gpsimd.memset(halves[:], 0.0))
            then(nc.gpsimd.memset(halves[0:MID, 0:1], DECAY))
            nc.gpsimd.memset(halves[MID:P, 1:2], DECAY).then_inc(masks_ready, 1)
            pool.wait_ge(masks_ready, 1)

            low_groups(first_slab["key"] // SLOTS, first_slab["rw_out"] // SLOTS)
            low_weights(first_slab["rw_out"] // SLOTS, 0)
            low_weights(first_slab["rw_out"] // SLOTS, 1)
            pool.wait_ge(gn_in, 32)
            pool.wait_ge(rw_in, 48)
            with pool.Fori(0, TT) as t:
                for half in range(2):
                    LINKS = 6
                    links = [0]
                    col = slice(half * HALF, (half + 1) * HALF)

                    def link(instruction):
                        instruction.then_inc(step_pool, 1)
                        links[0] += 1
                        pool.wait_ge(step_pool, nth(t, half, LINKS, links[0]))

                    def heads(ap):
                        return ap.rearrange("p (h n) -> p h n", n=N)

                    def per_head(k):
                        return small[:, k, :].unsqueeze(2).broadcast_to([P, HH, N])

                    pool.wait_ge(given_in[half], t * 16 + 16)
                    pool.wait_ge(k_ready, nth(t, half, 1, 1))
                    link(nc.gpsimd.tensor_tensor(rk[:], given[:, half, RR, :], given[:, half, KK, :], ALU.mult))
                    nc.gpsimd.tensor_tensor(rk[:], rk[:], r_k[:, col], ALU.mult).then_inc(rk_ready, 1)
                    y = y_tok[:, t, col]
                    pool.wait_ge(yr_ready, nth(t, half, 1, 1))
                    link(nc.gpsimd.tensor_tensor(heads(yc[:]), heads(yc[:]), per_head(YR), ALU.mult))
                    link(nc.gpsimd.tensor_tensor(yc[:], yc[:], gn[:, 0, col], ALU.mult))
                    link(nc.gpsimd.tensor_tensor(yc[:], yc[:], gn[:, 1, col], ALU.add))
                    pool.wait_ge(bonus_ready, nth(t, half, 1, 1))
                    link(nc.gpsimd.tensor_tensor(heads(us[:]), heads(given[:, half, VV, :]), per_head(BONUS), ALU.mult))
                    link(nc.gpsimd.tensor_tensor(yc[:], yc[:], us[:], ALU.add))
                    nc.gpsimd.tensor_tensor(y, yc[:], given[:, half, GG, :], ALU.mult).then_inc(given_used, 1)
                    assert links[0] == LINKS

            low_weights(first_slab["rw_out"] // SLOTS, 2)
            low_weights(first_slab["rw_out"] // SLOTS, 3)
            low_groups(first_slab["rw_out"] // SLOTS + 1, SLABS // SLOTS)

        @block.scalar
        def _(act):
            nc.scalar.dma_start(ws_in[:], gm_ws[0].rearrange("g t s -> t g s")).then_inc(ws_arrived, 16)
            nc.scalar.dma_start(mu_rows[:], rw_mu[0].rearrange("m (k p) -> (m k) p", p=P)).then_inc(mu_in, 16)
            nc.scalar.dma_start(bs_all[:], gm_bs.partition_broadcast(P).rearrange("p a g t -> p (a g) t")
                                ).then_inc(bs_arrived, 16)

            def load_gains(q, g, b):
                if q:
                    act.wait_ge(x_ready if q > 1 else v_ready, max(q - 1, 1) * TT)
                nc.scalar.dma_start(gains[:, 0, :], g.partition_broadcast(P).rearrange("p a n -> p (a n)")
                                    ).then_inc(gains_in, 16)
                nc.scalar.dma_start(gains[:, 1, :], b.partition_broadcast(P).rearrange("p a n -> p (a n)")
                                    ).then_inc(gains_in, 16)

            def round_weights(i, j, n0):
                n0, j = n0 + j // SLOTS * SLOTS, j % SLOTS
                act.wait_ge(raw_in[j], i * 16 + 16 * (n0 // SLOTS + 1))
                if not isinstance(i, int) or n0 + i * SLOTS >= SLOTS:
                    act.wait_ge(slab_used, i * SLOTS + (n0 + j - SLOTS + 1))
                nc.scalar.activation(w_hi[:, j, :], raw[:, j, :], ACT.Copy).then_inc(w_hi_ready, 1)

            AHEAD = 2

            def ahead(i, j, n0):
                if isinstance(i, int) and n0 + i * SLOTS + j + AHEAD >= SLABS:
                    return
                round_weights(i, j + AHEAD, n0)

            def row_product(name, count, source, wait_source=None):
                n0 = first_slab[name]

                def group(i, aheads):
                    for j in range(SLOTS):
                        if j < aheads:
                            ahead(i, j, n0)
                        if wait_source is not None:
                            wait_source(i * SLOTS + j)
                        nc.scalar.activation(a_hi[:, j, :], source(i * SLOTS + j), ACT.Copy).then_inc(a_hi_ready, 1)
                if count == KT:
                    group(0, SLOTS)
                else:
                    with act.Fori(0, count // SLOTS - 1) as i:
                        group(i, SLOTS)
                group(count // SLOTS - 1, AHEAD)

            def next_weights(name, count):
                for j in range(AHEAD, SLOTS):
                    ahead(count // SLOTS - 1, j, first_slab[name])

            def turned(times, t):
                for h in range(2):
                    b = 2 * t + h
                    act.wait_ge(x_turned, times * 2 * TT + b + 1)
                    nc.scalar.activation(xT[:, 4 * h:4 * h + 4, PAD + t * P:PAD + (t + 1) * P],
                                         bank[b][:].rearrange("p (k t) -> p k t", t=P), ACT.Copy
                                         ).then_inc(xT_ready, 1)

            def std_of(norm, t):
                act.wait_ge(var_ready, norm * TT + t + 1)
                nc.scalar.activation(std[:], mean_var[:, 1:2], ACT.Sqrt).then_inc(std_ready, 1)

            def finish_norm(name, count, norm, times):
                for t in range(TT):
                    if t == TT - 1:
                        next_weights(name, count)
                    std_of(norm, t)
                    if times is not None and t == 2:
                        turned(times, 0)
                if times is not None:
                    for t in range(1, TT):
                        turned(times, t)

            load_gains(0, gm_vn_g, gm_vn_b)
            round_weights(0, 0, 0)
            round_weights(0, 1, 0)
            for t in range(TT):
                turned(0, t)
            for h in range(2):
                act.wait_ge(wsT_summed, h + 1)
                nc.scalar.activation(wsT[:, 4 * h:4 * h + 4, :], bank[6 + h][:].rearrange("p (g t) -> p g t", t=P),
                                     ACT.Copy).then_inc(wsT_ready, 1)
            act.wait_ge(mu_turned, 1)
            nc.scalar.activation(mu[:].rearrange("p m k -> p (m k)"), bank[5][:, 0:6 * KT], ACT.Copy
                                 ).then_inc(mu_ready, 1)
            act.wait_ge(xT_ready, 2 * TT)
            row_product("v", KT, lambda k: xT[:, k, PAD:])
            for t in range(TT):
                if t < TT - 1:
                    act.wait_ge(tile_summed, t + 1)
                else:
                    next_weights("v", KT)
                    act.wait_ge(slab_used, first_slab["u"])
                for h in range(2):
                    nc.scalar.activation(v_tok[:, t, h * HALF:(h + 1) * HALF], bank[2 * t + h][:], ACT.Gelu
                                         ).then_inc(v_read, 1)

            for f in range(KT):
                n0 = first_slab["u"]
                ahead(f // SLOTS, f % SLOTS, n0)
                if f in (1, 2, 3, 4):
                    std_of(0, f - 1)
                act.wait_ge(slab_used, n0 + f + 1)
                nc.scalar.activation(uT[:, f, :], bank[f % SLOTS][:], ACT.Gelu).then_inc(bank_read, 1)
            load_gains(1, ln1_g[0:1], ln1_b[0:1])
            row_product("gm_out", KT, lambda k: gatedT[:, k, :], lambda k: act.wait_ge(gated, 2 * k + 2))
            finish_norm("gm_out", KT, 1, 1)

            def load_small():
                for dst, source in ((lw1[:], rw_w1[0].rearrange("(k p) n -> p k n", p=P)),
                                    (la1[:], rw_a1[0].rearrange("(k p) n -> p k n", p=P)),
                                    (lg1[:], rw_g1[0].rearrange("(k p) n -> p k n", p=P)),
                                    (lw2[0:LORA, :], rw_w2[0]), (lw2[LORA:LORA + 1, :], rw_w0),
                                    (la2[0:LORA, :], rw_a2[0]), (la2[LORA:LORA + 1, :], rw_a0),
                                    (lg2[:], rw_g2[0, 0:P]), (lg2b[:], rw_g2[0, P:GLORA])):
                    nc.scalar.dma_start(dst, source).then_inc(lora_in, 16)

            def mlp(layer, up_before, loads_between=False):
                n0 = first_slab[f"up{layer}"]

                def up_body(i, j):
                    ahead(i, j, n0)
                    act.wait_ge(slab_used, i * SLOTS + (n0 + j + 1))
                    if layer or not (isinstance(i, int) and i == 0 and j < 2):
                        act.wait_ge(squared, i * SLOTS + (FT * layer + j + 1))
                    nc.scalar.activation(relu[:, j % 2, :], bank[j][:], ACT.Relu).then_inc(bank_read, 1)
                with act.Fori(0, FT // SLOTS) as i:
                    for j in range(SLOTS):
                        up_body(i, j)
                act.wait_ge(squared, FT * (layer + 1) + 2)
                if loads_between:
                    load_small()
                row_product(f"down{layer}", FT, lambda k: big[:, k, :])

            load_gains(2, ln2_g[0:1], ln2_b[0:1])
            mlp(0, KT, loads_between=True)
            finish_norm("down0", FT, 2, 2)

            for row, source in ((k_k, rw_k_k), (k_a, rw_k_a), (r_k, rw_r_k.rearrange("a h n -> a (h n)"))):
                nc.scalar.dma_start(row[:], source.partition_broadcast(P).rearrange("p a n -> p (a n)")
                                    ).then_inc(rw_in, 16)
            act.wait_ge(x_ready, 2 * TT)
            for g, source in enumerate((rw_gn_g, rw_gn_b)):
                nc.scalar.dma_start(gn[:, g, :], source.partition_broadcast(P).rearrange("p a n -> p (a n)")
                                    ).then_inc(gn_in, 16)
            act.wait_ge(lora_summed, 1)
            nc.scalar.activation(low_w[0:LORA, :], bank[0][0:LORA, :], ACT.Tanh).then_inc(low_ready, 1)
            nc.scalar.activation(low_a[0:LORA, :], bank[1][0:LORA, :], ACT.Copy).then_inc(low_ready, 1)
            nc.scalar.activation(low_g[:], bank[2][:], ACT.Sigmoid).then_inc(low_ready, 1)
            nc.scalar.activation(low_gb[:], bank[3][0:GLORA - P, :], ACT.Sigmoid).then_inc(low_ready, 1)

            def projected(u, t, function, weights=None):
                z = u * TT + t
                if z >= 2:
                    act.wait_ge(stage_out[z % 2], 16 * (z // 2))
                for h in range(2):
                    nc.scalar.activation(stage[:, z % 2, h * HALF:(h + 1) * HALF], bank[2 * t + h][:], function
                                         ).then_inc(proj_read, 1)
                act.wait_ge(proj_read, 2 * z + 2)
                nc.scalar.dma_start(proj[u, t], stage[:, z % 2, :]).then_inc(stage_out[z % 2], 16)

            for u in range(3):
                for t in range(TT):
                    act.wait_ge(bank_projected, TT * u + t + 1)
                    projected(u, t, ACT.Copy if u == 2 else ACT.Sigmoid)
            for u, name in enumerate(("key", "receptance", "value")):
                row_product(name, KT, lambda k: mix[:, k % SLOTS, :],
                            lambda k: act.wait_ge(x_mixed, u * KT + k + 1))
                for t in range(TT):
                    if t < TT - 1:
                        act.wait_ge(tile_summed, row_products.index(name) * (TT - 1) + t + 1)
                    else:
                        next_weights(name, KT)
                        act.wait_ge(slab_used, first_slab[name] + KT)
                    projected(3 + u, t, ACT.Copy)

            with act.Fori(0, TT) as t:
                for half in range(2):
                    def due(semaphore, per_step, k):
                        act.wait_ge(semaphore, nth(t, half, per_step, k))

                    due(kk_scaled, 1, 1)
                    nc.scalar.activation(scratch[:], kkn[:], ACT.Square).then_inc(kk_squared, 1)
                    due(ss_ready, 1, 1)
                    nc.scalar.activation(small[:, NORM, :], small[:, SQ, :], ACT.Sqrt).then_inc(norm_ready, 1)
                    due(lx_ready, 1, 1)
                    nc.scalar.activation(decays[:], bank[5][:, 0:2 * PAIRS].rearrange("p (a b) -> p a b", b=2),
                                         ACT.Exp).then_inc(exp_ready, 1)
                    nc.scalar.activation(p_prev[:], p_prev[:], ACT.Exp).then_inc(exp_ready, 1)
                    nc.scalar.activation(p_inv[:], bank[4][:], ACT.Exp, scale=-1.0).then_inc(exp_ready, 1)
                    nc.scalar.activation(p_mid[:], bank[4][:], ACT.Exp).then_inc(exp_ready, 1)
                    for p in range(PAIRS):
                        due(turned_summed, PAIRS, p + 1)
                        nc.scalar.activation(turned4[:, p, :, :].rearrange("p a t -> p (a t)"), bank[4 + p][:],
                                             ACT.Copy).then_inc(turned_ready, 1)
                    for s in ON_ACT:
                        for g in range(2):
                            due(inv_summed, 2 * STAGES, 2 * s + g + 1)
                            nc.scalar.activation(inverse[s][3][:, 4 * g:4 * g + 4, :].rearrange("p h t -> p (h t)"),
                                                 bank[2 * (s % 2) + g][:], ACT.Copy).then_inc(inv_copied, 1)
                    due(x_summed, 1, 1)
                    nc.scalar.activation(xs[:], bank[0][:], ACT.Copy).then_inc(xs_ready, 1)
                    due(u_summed, 1, 1)
                    nc.scalar.activation(us[:], bank[1][:], ACT.Copy).then_inc(us_ready, 1)
                    due(yc_ready, 1, 1)
                    nc.scalar.activation(xs[:], yc[:], ACT.Square).then_inc(yq_ready, 1)
                    due(yvar_ready, 1, 1)
                    nc.scalar.activation(small[:, YSTD, :], small[:, YVAR, :], ACT.Sqrt).then_inc(ystd_ready, 1)

            act.wait_ge(given_used, STEPS)
            load_gains(3, ln1_g[1:2], ln1_b[1:2])
            for t in range(TT):
                for h in range(2):
                    act.wait_ge(y_turned, 2 * t + h + 1)
                    nc.scalar.activation(yT[:, 4 * h:4 * h + 4, t * P:(t + 1) * P],
                                         bank[2 * t + h][:].rearrange("p (k t) -> p k t", t=P), ACT.Copy
                                         ).then_inc(yT_ready, 1)
            act.wait_ge(yT_ready, 2 * TT)
            row_product("rw_out", KT, lambda k: yT[:, k, :])
            finish_norm("rw_out", KT, 3, 3)
            load_gains(4, ln2_g[1:2], ln2_b[1:2])
            mlp(1, KT + FT)
            finish_norm("down1", FT, 4, None)

        @block.vector
        def _(dve):
            done = Tally(dve_done)

            def then(instruction):
                dve.wait_ge(dve_done, done.inc(instruction))

            then(nc.vector.memset(xT[:, :, 0:PAD], 0.0))
            then(nc.vector.memset(relu[:], 0.0))
            nc.vector.memset(stats[:, 0, :], 0.0).then_inc(squared, 1)
            nc.vector.memset(stats[:, 1, :], 0.0).then_inc(squared, 1)

            def low_of(i, j, m0, source):
                dve.wait_ge(a_hi_ready, i * SLOTS + (m0 + j + 1))
                nc.vector.tensor_tensor(a_lo[:, j, :], source(i * SLOTS + j), a_hi[:, j, :].bitcast(F32),
                                        ALU.subtract).then_inc(a_lo_ready, 1)

            def groups(count, body):
                if count == KT:
                    for i in range(count // SLOTS):
                        for j in range(SLOTS):
                            body(i, j)
                else:
                    with dve.Fori(0, count // SLOTS) as i:
                        for j in range(SLOTS):
                            body(i, j)

            def normalise(y, var_before, result):
                for h in range(2):
                    last = done.inc(nc.vector.bn_stats(stats[:, h, :], y[:, h * HALF:(h + 1) * HALF]))
                dve.wait_ge(dve_done, last)
                then(nc.vector.bn_aggr(mean_var[:], stats[:].rearrange("p h s -> p (h s)")))
                nc.vector.tensor_scalar(mean_var[:, 1:2], mean_var[:, 1:2], LN_EPS, None, ALU.add
                                        ).then_inc(var_ready, 1)
                dve.wait_ge(std_ready, var_before + 1)
                then(nc.vector.reciprocal(rstd[:], std[:]))
                then(nc.vector.scalar_tensor_tensor(y, y, mean_var[:, 0:1], gains[:, 0, :],
                                                    ALU.subtract, ALU.mult))
                nc.vector.scalar_tensor_tensor(y, y, rstd[:, 0:1], gains[:, 1, :],
                                               ALU.mult, ALU.add).then_inc(result, 1)

            def residual_norm(name, which, times, split=True):
                dve.wait_ge(gains_in, 32 * (which + 2))
                product = [s[0] for s in stream if s[1] == "rows"].index(name)
                for t in range(TT):
                    if t < TT - 1:
                        dve.wait_ge(tile_summed, product * (TT - 1) + t + 1)
                    else:
                        dve.wait_ge(slab_used, first_slab[name] + dict((s[0], s[2]) for s in stream)[name])
                    for h in range(2):
                        y = x_tok[:, t, h * HALF:(h + 1) * HALF]
                        last = done.inc(nc.vector.scalar_tensor_tensor(y, y, ALPHA, bank[2 * t + h][:],
                                                                       ALU.mult, ALU.add))
                    dve.wait_ge(dve_done, last)
                    normalise(x_tok[:, t, :], (which + 1) * TT + t, x_ready)
                    if t == 2 and times is not None and split:
                        split_x(0, times)
                if times is not None and split:
                    for t in range(1, TT):
                        split_x(t, times)

            def split_x(t, times):
                dve.wait_ge(xT_ready, times * 2 * TT + 2 * (t + 1))
                here = slice(t * P, (t + 1) * P)
                src = xT[:, :, PAD + t * P:PAD + (t + 1) * P]
                then(nc.vector.tensor_copy(xT_hi[:, :, here], src))
                nc.vector.tensor_tensor(xT_lo[:, :, here], src, xT_hi[:, :, here].bitcast(F32), ALU.subtract
                                        ).then_inc(xT_split, 1)

            for t in range(TT):
                split_x(t, 0)
            groups(KT, lambda i, j: low_of(i, j, first_act["v"], lambda k: xT[:, k, PAD:]))
            dve.wait_ge(gains_in, 32)
            for t in range(TT):
                dve.wait_ge(v_read, 2 * t + 2)
                normalise(v_tok[:, t, :], t, v_ready)
            dve.wait_ge(bs_arrived, 16)
            for g in range(GROUPS):
                dve.wait_ge(mixed, g + 1)
                chunk = gatedT[:, g, :].rearrange("p (c t) -> p c t", t=P)
                dve.wait_ge(bank_read, g + 1)
                nc.vector.tensor_tensor(chunk, bank[4 + g % 4][:].rearrange("p (c t) -> p c t", t=P),
                                        bs_all[:, g:g + 1, :].broadcast_to([P, TT, P]), ALU.add
                                        ).then_inc(gated, 1)
                dve.wait_ge(gated, 2 * g + 1)
                nc.vector.tensor_tensor(gatedT[:, g, :], gatedT[:, g, :], uT[:, g, :], ALU.mult
                                        ).then_inc(gated, 1)
            groups(KT, lambda i, j: low_of(i, j, first_act["gm_out"], lambda k: gatedT[:, k, :]))
            residual_norm("gm_out", 0, 1)

            def mlp(layer, up_before):
                def square(i, j):
                    dve.wait_ge(bank_read, i * SLOTS + (up_before + j + 1))
                    nc.vector.tensor_tensor(big[:, i * SLOTS + j, :], relu[:, j % 2, :], relu[:, j % 2, :],
                                            ALU.mult).then_inc(squared, 1)
                groups(FT, square)
                groups(FT, lambda i, j: low_of(i, j, first_act[f"down{layer}"], lambda k: big[:, k, :]))
            mlp(0, KT)
            residual_norm("down0", 1, 2, False)

            then(nc.vector.memset(low_w[LORA:LORA + 1, :], 1.0))
            nc.vector.memset(low_a[LORA:LORA + 1, :], 1.0).then_inc(ones_ready, 1)
            dve.wait_ge(mu_ready, 1)
            dve.wait_ge(xT_ready, 3 * 2 * TT)
            R_MIX, W_MIX, K_MIX, V_MIX, A_MIX, G_MIX = range(6)

            def mix_into(dst, k, m):
                return nc.vector.scalar_tensor_tensor(dst, xxT[:, k, :], mu[:, m, k:k + 1], xT[:, k, PAD:],
                                                      ALU.mult, ALU.add)
            for k in range(KT):
                then(nc.vector.tensor_tensor(xxT[:, k, :], xT[:, k, PAD - 1:PAD - 1 + S], xT[:, k, PAD:],
                                             ALU.subtract))
                if k >= 2:
                    dve.wait_ge(lora_used, k - 1)
                for m, which in enumerate((W_MIX, A_MIX, G_MIX)):
                    mix_into(lora_mix[:, k % 2, m, :], k, which).then_inc(lora_mixed, 1)
            for u, (name, which) in enumerate((("key", K_MIX), ("receptance", R_MIX), ("value", V_MIX))):
                m0 = first_act[name]

                def mix_slab(k):
                    if u * KT + k >= SLOTS:
                        dve.wait_ge(a_lo_ready, m0 + k - SLOTS + 1)
                    mix_into(mix[:, k % SLOTS, :], k, which).then_inc(x_mixed, 1)
                mix_slab(0)
                mix_slab(1)
                for k in range(KT):
                    low_of(k // SLOTS, k % SLOTS, m0, lambda k: mix[:, k % SLOTS, :])
                    if k + 2 < KT:
                        mix_slab(k + 2)

            dve.wait_ge(slab_used, first_slab["rw_out"])
            then(nc.vector.memset(state[:], 0.0))
            then(nc.vector.memset(start[:], 0.0))
            dve.wait_ge(rw_in, 48)
            dve.wait_ge(masks_ready, 1)

            def by_head(ap):
                return ap.rearrange("p (h n) -> p h n", n=N)

            with dve.Fori(0, TT) as t:
                for half in range(2):
                    LINKS = 10
                    links = [0]
                    col = slice(half * HALF, (half + 1) * HALF)
                    from_proj = [given[:, half, u, :] for u in range(6)]

                    def link(instruction):
                        instruction.then_inc(step_dve, 1)
                        links[0] += 1
                        dve.wait_ge(step_dve, nth(t, half, LINKS, links[0]))

                    def due(semaphore, per_step, k):
                        dve.wait_ge(semaphore, nth(t, half, per_step, k))

                    def per_head(k):
                        return small[:, k, :].unsqueeze(2).broadcast_to([P, HH, N])

                    dve.wait_ge(given_in[half], t * 16 + 16)
                    nc.vector.tensor_tensor(kkn[:], from_proj[KK], k_k[:, col], ALU.mult).then_inc(kk_scaled, 1)
                    due(kk_scaled, 1, 1)
                    due(cum_summed, 1, 1)
                    nc.vector.scalar_tensor_tensor(p_prev[:], from_proj[SIG], -DECAY, bank[4][:],
                                                   ALU.mult, ALU.add).then_inc(lx_ready, 1)
                    due(kk_squared, 1, 1)
                    nc.vector.tensor_reduce(small[:, SQ, :], by_head(scratch[:]), AX.X, ALU.add).then_inc(ss_ready, 1)
                    due(norm_ready, 1, 1)
                    link(nc.vector.tensor_scalar(small[:, NORM, :], small[:, NORM, :], 1e-12, None, ALU.max))
                    link(nc.vector.reciprocal(small[:, RNORM, :], small[:, NORM, :]))
                    link(nc.vector.tensor_tensor(by_head(kkn[:]), by_head(kkn[:]), per_head(RNORM), ALU.mult))
                    link(nc.vector.scalar_tensor_tensor(scratch[:], from_proj[AA], -1.0, k_a[:, col],
                                                        ALU.add, ALU.mult))
                    nc.vector.scalar_tensor_tensor(from_proj[KK], scratch[:], 1.0, from_proj[KK],
                                                   ALU.add, ALU.mult).then_inc(k_ready, 1)
                    due(k_ready, 1, 1)
                    link(nc.vector.scalar_tensor_tensor(scratch[:], kkn[:], -1.0, from_proj[AA], ALU.mult, ALU.mult))
                    due(exp_ready, 4, 2)
                    nc.vector.tensor_tensor(tok[:, A_, :], kkn[:], p_prev[:], ALU.mult).then_inc(tok_ready, 1)
                    due(exp_ready, 4, 3)
                    nc.vector.tensor_tensor(tok[:, B_, :], scratch[:], p_inv[:], ALU.mult).then_inc(tok_ready, 1)
                    nc.vector.tensor_tensor(tok[:, K_, :], from_proj[KK], p_inv[:], ALU.mult).then_inc(tok_ready, 1)
                    due(exp_ready, 4, 4)
                    nc.vector.tensor_tensor(tok[:, R_, :], from_proj[RR], p_mid[:], ALU.mult).then_inc(tok_ready, 1)
                    due(rk_ready, 1, 1)
                    nc.vector.tensor_reduce(small[:, BONUS, :], by_head(rk[:]), AX.X, ALU.add).then_inc(bonus_ready, 1)
                    for e in range(2):
                        rows_, cols_ = slice(e * N, (e + 1) * N), slice(e * N, (e + 1) * N)
                        nc.vector.tensor_tensor(start[rows_, :, cols_], state[rows_, half, :, cols_],
                                                decays[rows_, :, 0:1].broadcast_to([N, PAIRS, N]), ALU.mult
                                                ).then_inc(start_ready, 1)
                    for h in range(HH):
                        due(gram_summed, HH, h + 1)
                        nc.vector.tensor_tensor(gram[:, h, :, :].rearrange("p (g a) t -> p g a t", a=2),
                                                bank[4 + h % 4][:].rearrange("p (g a t) -> p g a t", g=2, a=2),
                                                keep_before[:].unsqueeze(1).broadcast_to([P, 2, 2, P]),
                                                ALU.mult).then_inc(gram_ready, 1)
                    due(gram_ready, HH, HH)
                    block_mask = keep_block[:].unsqueeze(1).broadcast_to([P, HH, P])
                    nc.vector.tensor_tensor(n_one[:], gram[:, :, B_A, :], block_mask, ALU.mult).then_inc(base_ready, 1)
                    due(base_ready, 3, 1)
                    nc.vector.tensor_tensor(inv_t[:], n_one[:], ident[:].unsqueeze(1).broadcast_to([P, HH, P]),
                                            ALU.add).then_inc(base_ready, 1)
                    due(inv_copied, 2 * len(ON_ACT), 2)
                    nc.vector.tensor_tensor(buf2[:], m_full[:], block_mask, ALU.mult).then_inc(base_ready, 1)
                    for s in ON_DVE:
                        what, _, _, result, _ = inverse[s]
                        for g in range(2):
                            due(inv_summed, 2 * STAGES, 2 * s + g + 1)
                            four = slice(4 * g, 4 * g + 4)
                            product = bank[2 * (s % 2) + g][:].rearrange("p (h t) -> p h t", t=P)
                            if what == "mask":
                                other = keep_level[(s - 7) // 3][:].unsqueeze(1).broadcast_to([P, 4, P])
                            else:
                                other = result[:, four, :]
                            nc.vector.tensor_tensor(result[:, four, :], product, other,
                                                    ALU.mult if what == "mask" else ALU.add).then_inc(inv_added, 1)
                    due(s_summed, 1, 1)
                    for e in range(2):
                        rows_, cols_ = slice(e * N, (e + 1) * N), slice(e * N, (e + 1) * N)
                        now = state[rows_, half, :, cols_]
                        link(nc.vector.tensor_tensor(now, bank[3][rows_, :].rearrange("p (a v) -> p a v", v=P)[:, :, cols_],
                                                     start[rows_, :, cols_], ALU.add))
                        nc.vector.tensor_tensor(now, now, decays[rows_, :, 1:2].broadcast_to([N, PAIRS, N]), ALU.mult
                                                ).then_inc(state_ready, 1)
                    due(y_summed, 1, 1)
                    link(nc.vector.tensor_reduce(small[:, YSUM, :], by_head(bank[2][:]), AX.X, ALU.add))
                    link(nc.vector.tensor_scalar(small[:, YSUM, :], small[:, YSUM, :], 1.0 / N, None, ALU.mult))
                    nc.vector.tensor_tensor(by_head(yc[:]), by_head(bank[2][:]), per_head(YSUM), ALU.subtract
                                            ).then_inc(yc_ready, 1)
                    due(yq_ready, 1, 1)
                    link(nc.vector.tensor_reduce(small[:, YVAR, :], by_head(xs[:]), AX.X, ALU.add))
                    nc.vector.tensor_scalar(small[:, YVAR, :], small[:, YVAR, :], 1.0 / N, GN_EPS, ALU.mult, ALU.add
                                            ).then_inc(yvar_ready, 1)
                    due(ystd_ready, 1, 1)
                    nc.vector.reciprocal(small[:, YR, :], small[:, YSTD, :]).then_inc(yr_ready, 1)
                    dve.wait_ge(given_used, t * 2 + half + 1)
                    assert links[0] == LINKS, links

            groups(KT, lambda i, j: low_of(i, j, first_act["rw_out"], lambda k: yT[:, k, :]))
            residual_norm("rw_out", 2, 3)
            mlp(1, KT + FT)
            residual_norm("down1", 3, None)

        @block.tensor
        def _(pe):
            def slab_arrived(n):
                pe.wait_ge(w_hi_ready, n + 1)
                pe.wait_ge(w_lo_ready, n + 1)

            def row_tile(j, t, start, stop):
                tok = slice(t * P, (t + 1) * P)
                for a, ws in ((a_hi, (w_hi, w_lo)), (a_lo, (w_hi,))):
                    for w in ws:
                        for h in range(2):
                            last = nc.tensor.matmul(bank[2 * t + h][:], a[:, j, tok], w[:, j, h * HALF:(h + 1) * HALF],
                                                    start=start and a is a_hi and w is w_hi,
                                                    stop=stop and a is a_lo)
                return last

            def row_product(name, count, turning=None, bank_free=None):
                n0, m0 = first_slab[name], first_act[name]

                def arrived(i, j):
                    pe.wait_ge(w_hi_ready, i * SLOTS + (n0 + j + 1))
                    pe.wait_ge(w_lo_ready, i * SLOTS + (n0 + j + 1))
                    pe.wait_ge(a_hi_ready, i * SLOTS + (m0 + j + 1))
                    pe.wait_ge(a_lo_ready, i * SLOTS + (m0 + j + 1))

                def group(i, start):
                    for j in range(SLOTS):
                        arrived(i, j)
                        for t in range(TT):
                            if start and j == 0 and bank_free is not None:
                                bank_free(t)
                            last = row_tile(j, t, start and j == 0, False)
                        last.then_inc(slab_used, 1)
                group(0, True)
                if count > 2 * SLOTS:
                    with pe.Fori(1, count // SLOTS - 1) as i:
                        group(i, False)
                for t in range(TT):
                    for j in range(SLOTS):
                        if t == 0:
                            arrived(count // SLOTS - 1, j)
                        last = row_tile(j, t, False, j == SLOTS - 1)
                        if t == TT - 1:
                            last.then_inc(slab_used, 1)
                    if t < TT - 1:
                        last.then_inc(tile_summed, 1)
                    if turning is not None and t >= 2:
                        turn_x(turning, t - 2)
                if turning is not None:
                    for t in range(2, TT):
                        turn_x(turning, t)

            def column_slab(i, j, n0):
                pe.wait_ge(w_hi_ready, i * SLOTS + (n0 + j + 1))
                pe.wait_ge(w_lo_ready, i * SLOTS + (n0 + j + 1))
                for k in range(KT):
                    col = slice(k * P, (k + 1) * P)
                    nc.tensor.matmul(bank[j][:], w_hi[:, j, col], xT_hi[:, k, :], start=k == 0, stop=False)
                    nc.tensor.matmul(bank[j][:], w_hi[:, j, col], xT_lo[:, k, :], start=False, stop=False)
                    last = nc.tensor.matmul(bank[j][:], w_lo[:, j, col], xT_hi[:, k, :], start=False,
                                            stop=k == KT - 1)
                last.then_inc(slab_used, 1)

            def turn_x(norms, t):
                if norms is not None:
                    pe.wait_ge(x_ready, norms * TT + t + 1)
                for h in range(2):
                    for k in range(4):
                        last = nc.tensor.transpose(bank[2 * t + h][:, k * P:(k + 1) * P],
                                                   x_tok[:, t, (4 * h + k) * P:(4 * h + k + 1) * P], ident[:])
                    last.then_inc(x_turned, 1)

            pe.wait_ge(x_in, 16)
            pe.wait_ge(ident_ready, 1)
            for t in range(TT):
                turn_x(None, t)
            pe.wait_ge(ws_masked, 1)
            for h in range(2):
                pe.wait_ge(xT_ready, 7 + h)
                for g in range(4):
                    last = nc.tensor.transpose(bank[6 + h][:, g * P:(g + 1) * P], ws_in[:, 4 * h + g, :], ident[:])
                last.then_inc(wsT_summed, 1)
            pe.wait_ge(xT_ready, 2 * TT)
            pe.wait_ge(mu_in, 16)
            nc.tensor.transpose(bank[5][:, 0:6 * KT], mu_rows[:], ident[0:6 * KT, 0:6 * KT]).then_inc(mu_turned, 1)
            pe.wait_ge(wsT_ready, 2)
            pe.wait_ge(mu_ready, 1)
            row_product("v", KT)
            pe.wait_ge(xT_split, TT)
            for f in range(KT):
                if f < 4:
                    pe.wait_ge(v_read, f + 1)
                else:
                    pe.wait_ge(bank_read, f - 3)
                column_slab(f // SLOTS, f % SLOTS, first_slab["u"])
            pe.wait_ge(v_ready, TT)
            for g in range(GROUPS):
                if g >= 4:
                    pe.wait_ge(gated, 2 * (g - 4) + 1)
                for c in range(TT):
                    last = nc.tensor.matmul(bank[4 + g % 4][:, c * P:(c + 1) * P], v_tok[:, c, g * P:(g + 1) * P],
                                            wsT[:, g, :], start=True, stop=True)
                last.then_inc(mixed, 1)
            pe.wait_ge(bank_read, KT)
            pe.wait_ge(gated, 2 * GROUPS)
            row_product("gm_out", KT, 0)

            def mlp(layer, splits, up_before, turning):
                n0 = first_slab[f"up{layer}"]
                pe.wait_ge(xT_split, splits)
                for f in range(SLOTS):
                    column_slab(0, f, n0)
                with pe.Fori(1, FT // SLOTS) as i:
                    for j in range(SLOTS):
                        pe.wait_ge(bank_read, i * SLOTS + (up_before + j - SLOTS + 1))
                        column_slab(i, j, n0)
                pe.wait_ge(bank_read, up_before + FT)
                row_product(f"down{layer}", FT, turning)
            mlp(0, 2 * TT, KT, 1)

            pe.wait_ge(xT_ready, 3 * 2 * TT)
            pe.wait_ge(lora_in, 16 * 9)
            for k in range(KT):
                for m, products in enumerate((((0, lw1[:, k, :]),), ((1, la1[:, k, :]),),
                                              ((2, lg1[:, k, 0:P]), (3, lg1[:, k, P:GLORA])))):
                    pe.wait_ge(lora_mixed, 3 * k + m + 1)
                    for b, w in products:
                        last = nc.tensor.matmul(bank[b][0:w.shape[1], :], w, lora_mix[:, k % 2, m, :],
                                                start=k == 0, stop=k == KT - 1)
                if k < KT - 1:
                    last.then_inc(lora_used, 1)
                else:
                    last.then_inc(lora_summed, 1)
            pe.wait_ge(ones_ready, 1)
            pe.wait_ge(low_ready, 4)
            for u, terms in enumerate((((low_w, lw2),), ((low_a, la2),), ((low_g, lg2), (low_gb, lg2b)))):
                for t in range(TT):
                    for h in range(2):
                        if u:
                            pe.wait_ge(proj_read, 8 * (u - 1) + 2 * t + h + 1)
                        for n, (a, w) in enumerate(terms):
                            last = nc.tensor.matmul(bank[2 * t + h][:], a[:, t * P:(t + 1) * P],
                                                    w[:, h * HALF:(h + 1) * HALF], start=n == 0,
                                                    stop=n == len(terms) - 1)
                    last.then_inc(bank_projected, 1)
            for u, name in enumerate(("key", "receptance", "value")):
                row_product(name, KT, None, lambda t: pe.wait_ge(proj_read, 8 * (u + 2) + 2 * t + 2))

            pe.wait_ge(proj_read, 8 * 6)
            pe.wait_ge(masks_ready, 1)
            with pe.Fori(0, TT) as t:
                for half in range(2):
                    def due(semaphore, per_step, k):
                        pe.wait_ge(semaphore, nth(t, half, per_step, k))

                    def head(ap, h):
                        return ap[:, h * N:(h + 1) * N]

                    v = given[:, half, VV, :]
                    pe.wait_ge(given_in[half], t * 16 + 16)
                    nc.tensor.matmul(bank[4][:], cumulate[:], given[:, half, SIG, :], start=True, stop=True)
                    for p in range(PAIRS):
                        last = nc.tensor.matmul(bank[5][:, 2 * p:2 * p + 2], given[:, half, SIG, p * P:(p + 1) * P],
                                                halves[:], start=True, stop=True)
                    last.then_inc(cum_summed, 1)
                    due(exp_ready, 4, 4)
                    due(tok_ready, 4, 4)
                    for p in range(PAIRS):
                        for a in range(4):
                            last = nc.tensor.transpose(bank[4 + p][:, a * P:(a + 1) * P],
                                                       tok[:, a, p * P:(p + 1) * P], ident[:])
                        last.then_inc(turned_summed, 1)
                    for p in range(PAIRS):
                        due(turned_ready, PAIRS, p + 1)
                        for e in range(2):
                            h = 2 * p + e
                            due(turned_ready, PAIRS, h % 4 + 1)
                            if h >= 4:
                                due(gram_ready, HH, h - 3)
                            r = slice(e * N, (e + 1) * N)
                            for g, left in enumerate((B_, K_)):
                                last = nc.tensor.matmul(bank[4 + h % 4][:, g * 2 * P:(g + 1) * 2 * P],
                                                        turned4[r, p, left, :],
                                                        turned4[r, p, 0:2, :].rearrange("p a t -> p (a t)"),
                                                        start=True, stop=True)
                            last.then_inc(gram_summed, 1)

                    def evacuated(s, g):
                        if s in ON_ACT:
                            due(inv_copied, 2 * len(ON_ACT), 2 * ON_ACT.index(s) + g + 1)
                        else:
                            due(inv_added, 2 * len(ON_DVE), 2 * ON_DVE.index(s) + g + 1)
                    for s, (what, left, right, _, _) in enumerate(inverse):
                        for g in range(2):
                            if s == 0:
                                due(gram_ready, HH, 4 * g + 4)
                            elif s == 1:
                                due(base_ready, 3, 3)
                            if s >= 1:
                                evacuated(s - 1, g)
                            if s >= 2:
                                evacuated(s - 2, g)
                            for h in range(4 * g, 4 * g + 4):
                                dst = bank[2 * (s % 2) + g][:, (h % 4) * P:(h % 4 + 1) * P]
                                if what == "turn":
                                    src = left[:, h, B_A, :] if left is gram else left[:, h, :]
                                    last = nc.tensor.transpose(dst, src, ident[:])
                                else:
                                    last = nc.tensor.matmul(dst, left[:, h, :], right[:, h, :], start=True, stop=True)
                            last.then_inc(inv_summed, 1)
                    for s in (STAGES - 2, STAGES - 1):
                        evacuated(s, 1)
                    due(start_ready, 2, 2)
                    due(gram_ready, HH, HH)
                    for p in range(PAIRS):
                        nc.tensor.matmul(bank[0][:, p * P:(p + 1) * P], turned4[:, p, A_, :], start[:, p, :],
                                         start=p == 0, stop=False, skip_group_check=True)
                        for h in (2 * p, 2 * p + 1):
                            last = nc.tensor.matmul(head(bank[0], h), gram[:, h, K_A, :], head(v, h), start=False,
                                                    stop=True, skip_group_check=True)
                    last.then_inc(x_summed, 1)
                    due(xs_ready, 1, 1)
                    for h in range(HH):
                        last = nc.tensor.matmul(head(bank[1], h), inv_t[:, h, :], head(xs, h), start=True, stop=True)
                    last.then_inc(u_summed, 1)
                    due(us_ready, 1, 1)
                    for p in range(PAIRS):
                        c = slice(p * P, (p + 1) * P)
                        nc.tensor.matmul(bank[3][:, c], tok[:, B_, c], us[:, c], start=p == 0, stop=False,
                                         skip_group_check=True)
                        last = nc.tensor.matmul(bank[3][:, c], tok[:, K_, c], v[:, c], start=False, stop=True,
                                                skip_group_check=True)
                    last.then_inc(s_summed, 1)
                    for p in range(PAIRS):
                        nc.tensor.matmul(bank[2][:, p * P:(p + 1) * P], turned4[:, p, R_, :], start[:, p, :],
                                         start=p == 0, stop=False, skip_group_check=True)
                        for h in (2 * p, 2 * p + 1):
                            nc.tensor.matmul(head(bank[2], h), gram[:, h, B_R, :], head(us, h), start=False,
                                             stop=False, skip_group_check=True)
                            last = nc.tensor.matmul(head(bank[2], h), gram[:, h, K_R, :], head(v, h), start=False,
                                                    stop=True, skip_group_check=True)
                    last.then_inc(y_summed, 1)
                    due(yc_ready, 1, 1)
                    due(state_ready, 2, 2)

            for t in range(TT):
                pe.wait_ge(given_used, 2 * t + 2)
                for h in range(2):
                    for k in range(4):
                        last = nc.tensor.transpose(bank[2 * t + h][:, k * P:(k + 1) * P],
                                                   y_tok[:, t, (4 * h + k) * P:(4 * h + k + 1) * P], ident[:])
                    last.then_inc(y_turned, 1)
            pe.wait_ge(yT_ready, 2 * TT)
            row_product("rw_out", KT, 2)
            mlp(1, 3 * TT, KT + FT, None)


_INS = ["x", "ln1_g", "ln1_b", "ln2_g", "ln2_b", "ffn_w1", "ffn_w2", "gm_w_in", "gm_vn_g", "gm_vn_b", "gm_ws",
        "gm_bs", "gm_w_out", "rw_mu", "rw_w_rkv", "rw_w0", "rw_w1", "rw_w2", "rw_a0", "rw_a1", "rw_a2", "rw_g1",
        "rw_g2", "rw_k_k", "rw_k_a", "rw_r_k", "rw_gn_g", "rw_gn_b", "rw_w_o"]


def kernel(**inputs):
    import numpy as np
    import concourse.bacc as bacc
    from concourse.bass_utils import run_bass_kernel_spmd

    nc = bacc.Bacc("TRN2", target_bir_lowering=False, num_devices=1)
    arrays, args = {}, []
    for name in _INS:
        a = np.ascontiguousarray(inputs[name])
        arrays[f"in_{name}"] = a
        args.append(nc.dram_tensor(f"in_{name}", a.shape, mybir.dt.from_np(a.dtype), kind="ExternalInput").ap())
    out = nc.dram_tensor("out_0", inputs["x"].shape, F32, kind="ExternalOutput").ap()
    trunk(nc, *args, out)
    r = run_bass_kernel_spmd(nc, [arrays], core_ids=[0])
    return r.results[0]["out_0"]
```

```python
import math
from contextlib import ExitStack

import concourse.bass as bass
from concourse import mybir

P = 128
SLOTS = 4
LN_EPS = 1e-5
GN_EPS = 64e-5
BASE = 8
LEVELS = (8, 16, 32, 64)

ALU = mybir.AluOpType
ACT = mybir.ActivationFunctionType
AX = mybir.AxisListType
F32 = mybir.dt.float32
F32R = mybir.dt.float32r


class Tally:

    def __init__(self, sem):
        self.sem, self.n = sem, 0

    def inc(self, instruction):
        instruction.then_inc(self.sem, 1)
        self.n += 1
        return self.n


class Step:

    def __init__(self, i, c):
        self.i, self.c, self.half = i, c, c % 2
        self.t = i + c // 2 if c >= 2 else i

    def nth(self, per_step, k):
        return self.i * (2 * per_step) + (self.c * per_step + k)

    def loaded(self):
        return self.i * 16 + (self.c // 2 + 1) * 16


def trunk(nc, x, ln1_g, ln1_b, ln2_g, ln2_b, ffn_w1, ffn_w2, gm_w_in, gm_vn_g, gm_vn_b, gm_ws, gm_bs,
          gm_w_out, rw_mu, rw_w_rkv, rw_w0, rw_w1, rw_w2, rw_a0, rw_a1, rw_a2, rw_g1, rw_g2, rw_k_k,
          rw_k_a, rw_r_k, rw_gn_g, rw_gn_b, rw_w_o, out):
    _, S, D = x.shape
    depth, _, FF = ffn_w1.shape
    GROUPS = gm_ws.shape[1]
    TT, KT, FT = S // P, D // P, FF // P
    ALPHA = (2.0 * depth) ** 0.25
    HALF = D // 2
    HEADS, N = rw_r_k.shape[1:]
    LORA, GLORA = rw_w1.shape[2], rw_g1.shape[2]
    HH = HEADS // 2
    PAIRS = HH // 2
    DECAY = -math.exp(-0.5)
    MID = P // 2
    assert (S, D, HALF) == (512, 1024, 512) and GROUPS == KT and HH * N == HALF

    def rows(w, c0=0):
        v = w.rearrange("(k p) n -> k p n", p=P)
        return lambda k: v[k, :, c0:c0 + D]

    def columns(w):
        v = w.rearrange("(k p) (f c) -> f p k c", p=P, c=P)
        return lambda f: v[f]

    stream = [("v", "rows", KT, rows(gm_w_in[0], D)), ("u", "columns", KT, columns(gm_w_in[0][:, 0:D])),
              ("gm_out", "rows", KT, rows(gm_w_out[0])),
              ("up0", "columns", FT, columns(ffn_w1[0])), ("down0", "rows", FT, rows(ffn_w2[0])),
              ("key", "rows", KT, rows(rw_w_rkv[0, 1])), ("receptance", "rows", KT, rows(rw_w_rkv[0, 0])),
              ("value", "rows", KT, rows(rw_w_rkv[0, 2])), ("rw_out", "rows", KT, rows(rw_w_o[0])),
              ("up1", "columns", FT, columns(ffn_w1[1])), ("down1", "rows", FT, rows(ffn_w2[1]))]
    COUNT = {s[0]: s[2] for s in stream}
    row_products = [s[0] for s in stream if s[1] == "rows"]
    SLABS = sum(s[2] for s in stream)
    first_slab, first_act, at, act_at = {}, {}, 0, 0
    for name, kind, count, _ in stream:
        first_slab[name] = at
        at += count
        if kind == "rows":
            first_act[name] = act_at
            act_at += count

    with ExitStack() as ctx:
        here = [(nc.sbuf_base + 31) // 32 * 32]

        def sb(name, shape, dtype=F32, at=None):
            size = 4
            for s in shape[1:]:
                size *= s
            where = here[0] if at is None else at
            if at is None:
                here[0] += (size + 31) // 32 * 32
            place[name] = where
            return nc.alloc_sbuf_tensor_at(name, shape, dtype, offset=where)

        place = {}

        def sem(name):
            return ctx.enter_context(nc.semaphore(name))

        raw = sb("raw", [P, SLOTS, D])
        w_hi = sb("w_hi", [P, SLOTS, D], F32R)
        w_lo = sb("w_lo", [P, SLOTS, D], F32R)
        a_hi = sb("a_hi", [P, SLOTS, S], F32R)
        a_lo = sb("a_lo", [P, SLOTS, S], F32R)
        PAD = 8
        xT = sb("xT", [P, KT, PAD + S])
        x_tok = sb("x_tok", [P, TT, D])
        xT_hi = sb("xT_hi", [P, KT, S], F32R)
        xT_lo = sb("xT_lo", [P, KT, S], F32R)
        big = sb("big", [P, FT, S])
        gains = sb("gains", [P, 2, D])
        ident = sb("ident", [P, P])
        relu = sb("relu", [P, 2, S])
        stats = sb("stats", [P, 2, 6])
        mean_var = sb("mean_var", [P, 2])
        std = sb("std", [P, 1])
        rstd = sb("rstd", [P, 1])
        v_tok = sb("v_tok", [P, TT, D], at=place["big"])
        uT = sb("uT", [P, KT, S], at=place["big"] + 16384)
        gatedT = sb("gatedT", [P, KT, S], at=place["big"] + 32768)
        ws_in = sb("ws_in", [P, GROUPS, P], at=place["big"] + 49152)
        wsT = sb("wsT", [P, GROUPS, P], at=place["big"] + 53248)
        bs_all = sb("bs_all", [P, GROUPS, P], at=place["big"] + 57344)

        cursor = [0, 0]

        def over(name, shape):
            size = 4
            for n in shape[1:]:
                size *= n
            where, cursor[0] = cursor[0], cursor[0] + (size + 31) // 32 * 32
            assert cursor[0] <= cursor[1], name
            return sb(name, shape, at=where)

        cursor[:] = place["big"] + (FT * S - 4 * D) * 4, place["gains"]
        k_k, k_a, r_k = (over(name, [P, D]) for name in ("k_k", "k_a", "r_k"))
        state = over("state", [P, 2, PAIRS, P])
        cursor[:] = place["relu"], place["relu"] + 4 * D
        keep_before = over("keep_before", [P, 2, P])
        keep_block = over("keep_block", [P, P])
        keep_level = [over(f"keep_level{b}", [P, P]) for b in LEVELS]
        cumulate = over("cumulate", [P, P])
        cursor[:] = place["xT_hi"], place["k_k"]
        lw1 = over("lw1", [P, KT, LORA])
        la1 = over("la1", [P, KT, LORA])
        lg1 = over("lg1", [P, KT, GLORA])
        lw2 = over("lw2", [LORA + 1, D])
        la2 = over("la2", [LORA + 1, D])
        lg2 = over("lg2", [P, D])
        lg2b = over("lg2b", [GLORA - P, D])
        assert cursor[0] <= place["big"]
        low_w = over("low_w", [LORA + 1, S])
        low_a = over("low_a", [LORA + 1, S])
        low_g = over("low_g", [P, S])
        low_gb = over("low_gb", [GLORA - P, S])
        xxT = over("xxT", [P, KT, S])
        lora_mix = over("lora_mix", [P, 2, 3, S])
        mix = over("mix", [P, SLOTS, S])
        stage = over("stage", [P, 2, D])
        cursor[:] = place["xT_hi"], place["k_k"]
        early = over("early", [P, 2, 4, HALF])
        late = over("late", [P, 2, 2, HALF])
        SIG, AA, KK, RR = range(4)
        GG, VV = range(2)
        tok_ar = over("tok_ar", [P, 2, HALF])
        tok_bk = over("tok_bk", [P, 2, 2, HALF])
        A_, R_, B_, K_ = range(4)
        turned4 = over("turned4", [P, 2, PAIRS, 4, P])
        kkn, p_mid, p_inv, p_prev, scratch, rk = (over(name, [P, HALF]) for name in
                                                  ("kkn", "p_mid", "p_inv", "p_prev", "scratch", "rk"))
        m_full, n_one, buf2, buf3 = (over(name, [P, HH, P]) for name in ("m_full", "n_one", "buf2", "buf3"))
        cursor[:] = place["raw"] + 2 * D * 4, place["x_tok"]
        gram = over("gram", [P, 2, HH, 4, P])
        B_A, B_R, K_A, K_R = range(4)
        inv_t = over("inv_t", [P, 2, HH, P])
        buf4 = over("buf4", [P, HH, P])
        xs, us, yc, bonus_v = (over(name, [P, HALF]) for name in ("xs", "us", "yc", "bonus_v"))
        start = over("start", [P, PAIRS, P])
        y_tok = over("y_tok", [P, TT, D])
        yT = sb("yT", [P, KT, S], at=place["big"])
        gn = sb("gn", [P, 2, D], at=place["gains"])
        mu = sb("mu", [P, 6, KT])
        mu_rows = sb("mu_rows", [6 * KT, P])
        halves = sb("halves", [P, 2])
        decays = sb("decays", [P, 2, PAIRS, 2])
        small = sb("small", [P, 9, HH])
        SQ, NORM, RNORM, YSUM, YVAR, YSTD, YR, BONUS = range(8)

        def inverse_of(half):
            inv = inv_t[:, half]
            stages = [("turn", gram[:, half, :, B_A, :], None, m_full, "act"),
                      ("copy", buf2, n_one, buf3, "act"), ("copy", n_one, buf2, buf4, "act"),
                      ("add", buf4, inv, inv, "dve"), ("copy", buf3, buf4, buf2, "act"),
                      ("add", buf2, inv, inv, "dve")]
            for _ in LEVELS:
                stages += [("turn", inv, None, buf4, "act"), ("mask", m_full, inv, buf3, "dve"),
                           ("add", buf4, buf3, inv, "dve")]
            return stages
        inverse = [inverse_of(half) for half in range(2)]
        STAGES = len(inverse[0])
        ON_ACT = [s for s in range(STAGES) if inverse[0][s][4] == "act"]
        ON_DVE = [s for s in range(STAGES) if inverse[0][s][4] == "dve"]

        proj = nc.dram_tensor("proj", (6, TT, P, D), F32, kind="Internal").ap()

        bank = [ctx.enter_context(nc.psum_tensor(f"bank{b}", [P, S], F32)) for b in range(8)]

        raw_in = [sem(f"raw_in{j}") for j in range(SLOTS)]
        w_hi_ready, w_lo_ready, slab_used = sem("w_hi_ready"), sem("w_lo_ready"), sem("slab_used")
        a_hi_ready, a_lo_ready = sem("a_hi_ready"), sem("a_lo_ready")
        tile_summed = sem("tile_summed")
        bank_read = sem("bank_read")
        squared = sem("squared")
        v_read = sem("v_read")
        x_in, gains_in, ws_arrived, bs_arrived = sem("x_in"), sem("gains_in"), sem("ws_arrived"), sem("bs_arrived")
        ident_ready, ws_masked, wsT_summed, wsT_ready = sem("ident_ready"), sem("ws_masked"), sem("wsT_summed"), sem("wsT_ready")
        x_turned, xT_ready, xT_split = sem("x_turned"), sem("xT_ready"), sem("xT_split")
        var_ready, std_ready, x_ready, v_ready = sem("var_ready"), sem("std_ready"), sem("x_ready"), sem("v_ready")
        mixed, gated = sem("mixed"), sem("gated")
        dve_done, pool_done = sem("dve_done"), sem("pool_done")
        stored = sem("stored")
        lora_in, rw_in, gn_in = sem("lora_in"), sem("rw_in"), sem("gn_in")
        lora_mixed, lora_used, lora_summed, low_ready = sem("lora_mixed"), sem("lora_used"), sem("lora_summed"), sem("low_ready")
        bank_projected, proj_read = sem("bank_projected"), sem("proj_read")
        stage_out = [sem("stage_out0"), sem("stage_out1")]
        x_mixed, ones_ready, masks_ready, state_zero = sem("x_mixed"), sem("ones_ready"), sem("masks_ready"), sem("state_zero")
        early_in, late_in = [sem("early_in0"), sem("early_in1")], [sem("late_in0"), sem("late_in1")]
        late_used = sem("late_used")
        cum_summed, lx_ready, exp_ready = sem("cum_summed"), sem("lx_ready"), sem("exp_ready")
        kk_scaled, kk_squared, ss_ready, norm_ready, k_ready = (
            sem("kk_scaled"), sem("kk_squared"), sem("ss_ready"), sem("norm_ready"), sem("k_ready"))
        tok_ready, rk_ready, turned_summed, turned_ready = sem("tok_ready"), sem("rk_ready"), sem("turned_summed"), sem("turned_ready")
        gram_summed, gram_ready, base_ready = sem("gram_summed"), sem("gram_ready"), sem("base_ready")
        inv_summed, inv_copied, inv_added = sem("inv_summed"), sem("inv_copied"), sem("inv_added")
        start_ready, x_summed, xs_ready, u_summed, us_ready = (
            sem("start_ready"), sem("x_summed"), sem("xs_ready"), sem("u_summed"), sem("us_ready"))
        mu_in, mu_turned, mu_ready = sem("mu_in"), sem("mu_turned"), sem("mu_ready")
        y_summed, s_summed, state_ready = sem("y_summed"), sem("s_summed"), sem("state_ready")
        yc_ready, yq_ready, yvar_ready, ystd_ready, yr_ready, bonus_ready, y_done = (
            sem("yc_ready"), sem("yq_ready"), sem("yvar_ready"), sem("ystd_ready"), sem("yr_ready"),
            sem("bonus_ready"), sem("y_done"))
        prep_linked, end_linked, pool_linked, rk_scaled = (
            sem("prep_linked"), sem("end_linked"), sem("pool_linked"), sem("rk_scaled"))
        y_turned, yT_ready = sem("y_turned"), sem("yT_ready")
        STEPS = 2 * TT

        def steps(engine, iteration):
            iteration(Step(0, 0), None, Step(0, 1))
            with engine.Fori(0, (STEPS - 2) // 2) as i:
                for c in (1, 2):
                    iteration(Step(i, c), Step(i, c - 1), Step(i, c + 1))
            iteration(Step(0, STEPS - 1), Step(0, STEPS - 2), None)

        block = ctx.enter_context(nc.Block())

        @block.sync
        def _(sp):
            sp.dma_start(x_tok[:], x[0].rearrange("(t p) n -> p t n", p=P)).then_inc(x_in, 16)

            def load(name, source, i, j):
                n0 = first_slab[name]
                if n0 + j >= SLOTS or not isinstance(i, int) or i > 0:
                    sp.wait_ge(w_lo_ready, i * SLOTS + (n0 + j - SLOTS + 1))
                dst = raw[:, j, :]
                if dict((s[0], s[1]) for s in stream)[name] == "columns":
                    dst = dst.rearrange("p (k c) -> p k c", c=P)
                sp.dma_start(dst, source(i * SLOTS + j)).then_inc(raw_in[j], 16)

            def load_early(t, half):
                sp.dma_start(early[:, half, :, :],
                             proj[0:4, t, :, half * HALF:(half + 1) * HALF].rearrange("u p n -> p u n")
                             ).then_inc(early_in[half], 16)

            def load_late(t, half):
                sp.dma_start(late[:, half, :, :],
                             proj[4:6, t, :, half * HALF:(half + 1) * HALF].rearrange("u p n -> p u n")
                             ).then_inc(late_in[half], 16)

            for name, _, count, source in stream:
                if count == KT:
                    for i in range(count // SLOTS):
                        for j in range(SLOTS):
                            if (name, i, j) == ("rw_out", 0, 2):
                                for z in range(2):
                                    sp.wait_ge(stage_out[z], 16 * 5 * TT // 2)
                                load_early(0, 0)
                                load_early(0, 1)
                                for z in range(2):
                                    sp.wait_ge(stage_out[z], 16 * 6 * TT // 2)
                                load_late(0, 0)
                                load_late(0, 1)
                                with sp.Fori(1, TT) as t:
                                    for half in range(2):
                                        sp.wait_ge(bonus_ready, t * 2 + (half - 1))
                                        load_early(t, half)
                                        sp.wait_ge(late_used, t * 2 + (half - 1))
                                        load_late(t, half)
                                sp.wait_ge(late_used, STEPS)
                            load(name, source, i, j)
                else:
                    with sp.Fori(0, count // SLOTS) as i:
                        for j in range(SLOTS):
                            load(name, source, i, j)
            sp.wait_ge(x_ready, 4 * TT)
            sp.dma_start(out[0].rearrange("(t p) n -> p t n", p=P), x_tok[:]).then_inc(stored, 16)
            sp.wait_ge(stored, 16)

        @block.gpsimd
        def _(pool):
            nc.gpsimd.memset(ident[:], 0.0).then_inc(pool_done, 1)
            pool.wait_ge(pool_done, 1)
            nc.gpsimd.affine_select(out=ident[:], in_=ident[:], compare_op=ALU.not_equal, fill=1.0, base=0,
                                    pattern=[[-1, P]], channel_multiplier=1).then_inc(ident_ready, 1)
            pool.wait_ge(ws_arrived, 16)
            nc.gpsimd.affine_select(out=ws_in[:], in_=ws_in[:], compare_op=ALU.is_ge, fill=0.0, base=0,
                                    pattern=[[0, GROUPS], [-1, P]], channel_multiplier=1).then_inc(ws_masked, 1)

            def low_weights(i, j):
                pool.wait_ge(w_hi_ready, i * SLOTS + (j + 1))
                nc.gpsimd.tensor_tensor(w_lo[:, j, :], raw[:, j, :], w_hi[:, j, :].bitcast(F32),
                                        ALU.subtract).then_inc(w_lo_ready, 1)

            def low_groups(first, end):
                with pool.Fori(first, end) as i:
                    for j in range(SLOTS):
                        low_weights(i, j)

            low_groups(0, first_slab["key"] // SLOTS)
            pool.wait_ge(squared, FT + 2)
            done = Tally(pool_done)
            done.n = 1

            def then(instruction):
                pool.wait_ge(pool_done, done.inc(instruction))

            def keep(out, compare, pattern, base, by_partition):
                then(nc.gpsimd.affine_select(out=out, in_=out, compare_op=compare, fill=0.0, base=base,
                                             pattern=pattern, channel_multiplier=by_partition))
            then(nc.gpsimd.memset(keep_before[:], 1.0))
            keep(keep_before[:, 0, :], ALU.is_gt, [[1, P]], 0, -1)
            keep(keep_before[:, 1, :], ALU.is_ge, [[1, P]], 0, -1)
            then(nc.gpsimd.memset(keep_block[:], 1.0))
            blocks = keep_block[:].rearrange("p (m c) -> p m c", c=BASE)
            keep(blocks, ALU.is_ge, [[-BASE, P // BASE], [0, BASE]], 0, 1)
            keep(blocks, ALU.is_ge, [[BASE, P // BASE], [0, BASE]], BASE - 1, -1)
            for b, level in zip(LEVELS, keep_level):
                then(nc.gpsimd.memset(level[:], 0.0))
                odd = level[:].rearrange("p (m e c) -> p m e c", e=2, c=b)[:, :, 1, :]
                then(nc.gpsimd.memset(odd, 1.0))
                keep(odd, ALU.is_ge, [[-2 * b, P // (2 * b)], [0, b]], 0, 1)
                keep(odd, ALU.is_ge, [[2 * b, P // (2 * b)], [0, b]], b - 1, -1)
            then(nc.gpsimd.memset(cumulate[0:MID, :], -DECAY))
            then(nc.gpsimd.memset(cumulate[MID:P, :], DECAY))
            keep(cumulate[0:MID, :], ALU.is_gt, [[-1, P]], 0, 1)
            keep(cumulate[MID:P, :], ALU.is_ge, [[1, P]], -MID, -1)
            then(nc.gpsimd.memset(halves[:], 0.0))
            then(nc.gpsimd.memset(halves[0:MID, 0:1], DECAY))
            nc.gpsimd.memset(halves[MID:P, 1:2], DECAY).then_inc(masks_ready, 1)
            pool.wait_ge(masks_ready, 1)

            low_groups(first_slab["key"] // SLOTS, first_slab["rw_out"] // SLOTS)
            pool.wait_ge(gn_in, 32)
            pool.wait_ge(rw_in, 48)

            def bonus_terms(n):
                half, col = n.half, slice(n.half * HALF, (n.half + 1) * HALF)
                pool.wait_ge(early_in[half], n.loaded())
                pool.wait_ge(k_ready, n.nth(1, 1))
                nc.gpsimd.tensor_tensor(rk[:], early[:, half, RR, :], early[:, half, KK, :], ALU.mult
                                        ).then_inc(rk_scaled, 1)
                pool.wait_ge(rk_scaled, n.nth(1, 1))
                nc.gpsimd.tensor_tensor(rk[:], rk[:], r_k[:, col], ALU.mult).then_inc(rk_ready, 1)

            def finish(s):
                half, col = s.half, slice(s.half * HALF, (s.half + 1) * HALF)

                def link(k, instruction):
                    instruction.then_inc(pool_linked, 1)
                    pool.wait_ge(pool_linked, s.nth(5, k))

                def heads(ap):
                    return ap.rearrange("p (h n) -> p h n", n=N)

                def per_head(k):
                    return small[:, k, :].unsqueeze(2).broadcast_to([P, HH, N])
                pool.wait_ge(late_in[half], s.loaded())
                pool.wait_ge(bonus_ready, s.nth(1, 1))
                link(1, nc.gpsimd.tensor_tensor(heads(bonus_v[:]), heads(late[:, half, VV, :]),
                                                per_head(BONUS + half), ALU.mult))
                pool.wait_ge(yr_ready, s.nth(1, 1))
                link(2, nc.gpsimd.tensor_tensor(heads(yc[:]), heads(yc[:]), per_head(YR), ALU.mult))
                link(3, nc.gpsimd.tensor_tensor(yc[:], yc[:], gn[:, 0, col], ALU.mult))
                link(4, nc.gpsimd.tensor_tensor(yc[:], yc[:], gn[:, 1, col], ALU.add))
                link(5, nc.gpsimd.tensor_tensor(yc[:], yc[:], bonus_v[:], ALU.add))
                nc.gpsimd.tensor_tensor(y_tok[:, s.t, col], yc[:], late[:, half, GG, :], ALU.mult
                                        ).then_inc(late_used, 1)

            def iteration(q, s, n):
                if s:
                    finish(s)
                if n:
                    bonus_terms(n)
            bonus_terms(Step(0, 0))
            steps(pool, iteration)
            finish(Step(0, STEPS - 1))
            low_groups(first_slab["rw_out"] // SLOTS, SLABS // SLOTS)

        @block.scalar
        def _(act):
            nc.scalar.dma_start(ws_in[:], gm_ws[0].rearrange("g t s -> t g s")).then_inc(ws_arrived, 16)
            nc.scalar.dma_start(mu_rows[:], rw_mu[0].rearrange("m (k p) -> (m k) p", p=P)).then_inc(mu_in, 16)
            nc.scalar.dma_start(bs_all[:], gm_bs.partition_broadcast(P).rearrange("p a g t -> p (a g) t")
                                ).then_inc(bs_arrived, 16)

            def load_gains(q, g, b):
                if q:
                    act.wait_ge(x_ready if q > 1 else v_ready, max(q - 1, 1) * TT)
                nc.scalar.dma_start(gains[:, 0, :], g.partition_broadcast(P).rearrange("p a n -> p (a n)")
                                    ).then_inc(gains_in, 16)
                nc.scalar.dma_start(gains[:, 1, :], b.partition_broadcast(P).rearrange("p a n -> p (a n)")
                                    ).then_inc(gains_in, 16)

            def round_weights(i, j, n0):
                n0, j = n0 + j // SLOTS * SLOTS, j % SLOTS
                act.wait_ge(raw_in[j], i * 16 + 16 * (n0 // SLOTS + 1))
                if not isinstance(i, int) or n0 + i * SLOTS >= SLOTS:
                    act.wait_ge(slab_used, i * SLOTS + (n0 + j - SLOTS + 1))
                nc.scalar.activation(w_hi[:, j, :], raw[:, j, :], ACT.Copy).then_inc(w_hi_ready, 1)

            AHEAD = 2

            def ahead(i, j, n0):
                if isinstance(i, int) and n0 + i * SLOTS + j + AHEAD >= SLABS:
                    return
                round_weights(i, j + AHEAD, n0)

            def row_product(name, count, source, wait_source=None):
                n0 = first_slab[name]

                def group(i, aheads):
                    for j in range(SLOTS):
                        if j < aheads:
                            ahead(i, j, n0)
                        if wait_source is not None:
                            wait_source(i * SLOTS + j)
                        nc.scalar.activation(a_hi[:, j, :], source(i * SLOTS + j), ACT.Copy).then_inc(a_hi_ready, 1)
                if count == KT:
                    group(0, SLOTS)
                else:
                    with act.Fori(0, count // SLOTS - 1) as i:
                        group(i, SLOTS)
                group(count // SLOTS - 1, AHEAD)

            def next_weights(name, count):
                for j in range(AHEAD, SLOTS):
                    ahead(count // SLOTS - 1, j, first_slab[name])

            def turned(times, t):
                for h in range(2):
                    b = 2 * t + h
                    act.wait_ge(x_turned, times * 2 * TT + b + 1)
                    nc.scalar.activation(xT[:, 4 * h:4 * h + 4, PAD + t * P:PAD + (t + 1) * P],
                                         bank[b][:].rearrange("p (k t) -> p k t", t=P), ACT.Copy
                                         ).then_inc(xT_ready, 1)

            def std_of(norm, t):
                act.wait_ge(var_ready, norm * TT + t + 1)
                nc.scalar.activation(std[:], mean_var[:, 1:2], ACT.Sqrt).then_inc(std_ready, 1)

            def finish_norm(name, count, norm, times):
                for t in range(TT):
                    if t == TT - 1:
                        next_weights(name, count)
                    std_of(norm, t)
                    if times is not None and t == 2:
                        turned(times, 0)
                if times is not None:
                    for t in range(1, TT):
                        turned(times, t)

            load_gains(0, gm_vn_g, gm_vn_b)
            round_weights(0, 0, 0)
            round_weights(0, 1, 0)
            for t in range(TT):
                turned(0, t)
            for h in range(2):
                act.wait_ge(wsT_summed, h + 1)
                nc.scalar.activation(wsT[:, 4 * h:4 * h + 4, :], bank[6 + h][:].rearrange("p (g t) -> p g t", t=P),
                                     ACT.Copy).then_inc(wsT_ready, 1)
            act.wait_ge(mu_turned, 1)
            nc.scalar.activation(mu[:].rearrange("p m k -> p (m k)"), bank[5][:, 0:6 * KT], ACT.Copy
                                 ).then_inc(mu_ready, 1)
            act.wait_ge(xT_ready, 2 * TT)
            row_product("v", KT, lambda k: xT[:, k, PAD:])
            for t in range(TT):
                if t < TT - 1:
                    act.wait_ge(tile_summed, t + 1)
                else:
                    next_weights("v", KT)
                    act.wait_ge(slab_used, first_slab["u"])
                for h in range(2):
                    nc.scalar.activation(v_tok[:, t, h * HALF:(h + 1) * HALF], bank[2 * t + h][:], ACT.Gelu
                                         ).then_inc(v_read, 1)

            for f in range(KT):
                n0 = first_slab["u"]
                ahead(f // SLOTS, f % SLOTS, n0)
                if f in (1, 2, 3, 4):
                    std_of(0, f - 1)
                act.wait_ge(slab_used, n0 + f + 1)
                nc.scalar.activation(uT[:, f, :], bank[f % SLOTS][:], ACT.Gelu).then_inc(bank_read, 1)
            load_gains(1, ln1_g[0:1], ln1_b[0:1])
            row_product("gm_out", KT, lambda k: gatedT[:, k, :], lambda k: act.wait_ge(gated, 2 * k + 2))
            finish_norm("gm_out", KT, 1, 1)

            def load_small():
                for dst, source in ((lw1[:], rw_w1[0].rearrange("(k p) n -> p k n", p=P)),
                                    (la1[:], rw_a1[0].rearrange("(k p) n -> p k n", p=P)),
                                    (lg1[:], rw_g1[0].rearrange("(k p) n -> p k n", p=P)),
                                    (lw2[0:LORA, :], rw_w2[0]), (lw2[LORA:LORA + 1, :], rw_w0),
                                    (la2[0:LORA, :], rw_a2[0]), (la2[LORA:LORA + 1, :], rw_a0),
                                    (lg2[:], rw_g2[0, 0:P]), (lg2b[:], rw_g2[0, P:GLORA])):
                    nc.scalar.dma_start(dst, source).then_inc(lora_in, 16)

            def mlp(layer, up_before, loads_between=False):
                n0 = first_slab[f"up{layer}"]

                def up_body(i, j):
                    ahead(i, j, n0)
                    act.wait_ge(slab_used, i * SLOTS + (n0 + j + 1))
                    if layer or not (isinstance(i, int) and i == 0 and j < 2):
                        act.wait_ge(squared, i * SLOTS + (FT * layer + j + 1))
                    nc.scalar.activation(relu[:, j % 2, :], bank[j][:], ACT.Relu).then_inc(bank_read, 1)
                with act.Fori(0, FT // SLOTS) as i:
                    for j in range(SLOTS):
                        up_body(i, j)
                act.wait_ge(squared, FT * (layer + 1) + 2)
                if loads_between:
                    load_small()
                row_product(f"down{layer}", FT, lambda k: big[:, k, :])

            load_gains(2, ln2_g[0:1], ln2_b[0:1])
            mlp(0, KT, loads_between=True)
            finish_norm("down0", FT, 2, 2)

            for row, source in ((k_k, rw_k_k), (k_a, rw_k_a), (r_k, rw_r_k.rearrange("a h n -> a (h n)"))):
                nc.scalar.dma_start(row[:], source.partition_broadcast(P).rearrange("p a n -> p (a n)")
                                    ).then_inc(rw_in, 16)
            act.wait_ge(x_ready, 2 * TT)
            for g, source in enumerate((rw_gn_g, rw_gn_b)):
                nc.scalar.dma_start(gn[:, g, :], source.partition_broadcast(P).rearrange("p a n -> p (a n)")
                                    ).then_inc(gn_in, 16)
            act.wait_ge(lora_summed, 1)
            nc.scalar.activation(low_w[0:LORA, :], bank[0][0:LORA, :], ACT.Tanh).then_inc(low_ready, 1)
            nc.scalar.activation(low_a[0:LORA, :], bank[1][0:LORA, :], ACT.Copy).then_inc(low_ready, 1)
            nc.scalar.activation(low_g[:], bank[2][:], ACT.Sigmoid).then_inc(low_ready, 1)
            nc.scalar.activation(low_gb[:], bank[3][0:GLORA - P, :], ACT.Sigmoid).then_inc(low_ready, 1)

            def projected(u, t, function, weights=None):
                z = u * TT + t
                if z >= 2:
                    act.wait_ge(stage_out[z % 2], 16 * (z // 2))
                for h in range(2):
                    nc.scalar.activation(stage[:, z % 2, h * HALF:(h + 1) * HALF], bank[2 * t + h][:], function
                                         ).then_inc(proj_read, 1)
                act.wait_ge(proj_read, 2 * z + 2)
                nc.scalar.dma_start(proj[(SIG, AA, 4 + GG, KK, RR, 4 + VV)[u], t], stage[:, z % 2, :]).then_inc(stage_out[z % 2], 16)

            for u, function in enumerate((ACT.Sigmoid, ACT.Sigmoid, ACT.Copy)):
                for t in range(TT):
                    act.wait_ge(bank_projected, TT * u + t + 1)
                    projected(u, t, function)
            for u, name in enumerate(("key", "receptance", "value")):
                row_product(name, KT, lambda k: mix[:, k % SLOTS, :],
                            lambda k: act.wait_ge(x_mixed, u * KT + k + 1))
                for t in range(TT):
                    if t < TT - 1:
                        act.wait_ge(tile_summed, row_products.index(name) * (TT - 1) + t + 1)
                    else:
                        if name != "value":
                            next_weights(name, KT)
                        act.wait_ge(slab_used, first_slab[name] + KT)
                    projected(3 + u, t, ACT.Copy)

            def square_kk(n):
                act.wait_ge(kk_scaled, n.nth(1, 1))
                nc.scalar.activation(scratch[:], kkn[:], ACT.Square).then_inc(kk_squared, 1)

            def norm_of(n):
                act.wait_ge(ss_ready, n.nth(1, 1))
                nc.scalar.activation(small[:, NORM, :], small[:, SQ, :], ACT.Sqrt).then_inc(norm_ready, 1)

            def decays_of(n):
                act.wait_ge(lx_ready, n.nth(1, 1))
                nc.scalar.activation(decays[:, n.half], bank[5][:, 0:2 * PAIRS].rearrange("p (a b) -> p a b", b=2),
                                     ACT.Exp).then_inc(exp_ready, 1)
                nc.scalar.activation(p_prev[:], p_prev[:], ACT.Exp).then_inc(exp_ready, 1)
                nc.scalar.activation(p_inv[:], bank[4][:], ACT.Exp, scale=-1.0).then_inc(exp_ready, 1)
                nc.scalar.activation(p_mid[:], bank[4][:], ACT.Exp).then_inc(exp_ready, 1)

            def copy_x(s):
                act.wait_ge(x_summed, s.nth(1, 1))
                nc.scalar.activation(xs[:], bank[4][:], ACT.Copy).then_inc(xs_ready, 1)

            def copy_u(s):
                act.wait_ge(u_summed, s.nth(1, 1))
                nc.scalar.activation(us[:], bank[5][:], ACT.Copy).then_inc(us_ready, 1)

            def square_y(s):
                act.wait_ge(yc_ready, s.nth(1, 1))
                nc.scalar.activation(xs[:], yc[:], ACT.Square).then_inc(yq_ready, 1)

            def std_y(s):
                act.wait_ge(yvar_ready, s.nth(1, 1))
                nc.scalar.activation(small[:, YSTD, :], small[:, YVAR, :], ACT.Sqrt).then_inc(ystd_ready, 1)

            def iteration(q, s, n):
                for p in range(PAIRS):
                    act.wait_ge(turned_summed, q.nth(PAIRS, p + 1))
                    nc.scalar.activation(turned4[:, q.half, p].rearrange("p a t -> p (a t)"), bank[4 + p][:],
                                         ACT.Copy).then_inc(turned_ready, 1)
                for z in range(STAGES):
                    if z in ON_ACT:
                        for g in range(2):
                            act.wait_ge(inv_summed, q.nth(2 * STAGES, 2 * z + g + 1))
                            nc.scalar.activation(inverse[q.half][z][3][:, 4 * g:4 * g + 4, :],
                                                 bank[2 * (z % 2) + g][:].rearrange("p (h t) -> p h t", t=P), ACT.Copy
                                                 ).then_inc(inv_copied, 1)
                    if s and z == 0:
                        copy_x(s)
                    if s and z == 2:
                        copy_u(s)
                    if n and z == 6:
                        square_kk(n)
                    if s and z == 6:
                        square_y(s)
                    if n and z == 9:
                        norm_of(n)
                    if s and z == 9:
                        std_y(s)
                    if n and z == 12:
                        decays_of(n)
            square_kk(Step(0, 0))
            norm_of(Step(0, 0))
            decays_of(Step(0, 0))
            for z in range(2):
                act.wait_ge(stage_out[z], 16 * 6 * TT // 2)
            steps(act, iteration)
            last_step = Step(0, STEPS - 1)
            copy_x(last_step)
            copy_u(last_step)
            square_y(last_step)
            std_y(last_step)

            act.wait_ge(late_used, STEPS)
            next_weights("value", KT)
            load_gains(3, ln1_g[1:2], ln1_b[1:2])
            for t in range(TT):
                for h in range(2):
                    act.wait_ge(y_turned, 2 * t + h + 1)
                    nc.scalar.activation(yT[:, 4 * h:4 * h + 4, t * P:(t + 1) * P],
                                         bank[2 * t + h][:].rearrange("p (k t) -> p k t", t=P), ACT.Copy
                                         ).then_inc(yT_ready, 1)
            act.wait_ge(yT_ready, 2 * TT)
            row_product("rw_out", KT, lambda k: yT[:, k, :])
            finish_norm("rw_out", KT, 3, 3)
            load_gains(4, ln2_g[1:2], ln2_b[1:2])
            mlp(1, KT + FT)
            finish_norm("down1", FT, 4, None)

        @block.vector
        def _(dve):
            done = Tally(dve_done)

            def then(instruction):
                dve.wait_ge(dve_done, done.inc(instruction))

            then(nc.vector.memset(xT[:, :, 0:PAD], 0.0))
            then(nc.vector.memset(relu[:], 0.0))
            nc.vector.memset(stats[:, 0, :], 0.0).then_inc(squared, 1)
            nc.vector.memset(stats[:, 1, :], 0.0).then_inc(squared, 1)

            def low_of(i, j, m0, source):
                dve.wait_ge(a_hi_ready, i * SLOTS + (m0 + j + 1))
                nc.vector.tensor_tensor(a_lo[:, j, :], source(i * SLOTS + j), a_hi[:, j, :].bitcast(F32),
                                        ALU.subtract).then_inc(a_lo_ready, 1)

            def groups(count, body):
                if count == KT:
                    for i in range(count // SLOTS):
                        for j in range(SLOTS):
                            body(i, j)
                else:
                    with dve.Fori(0, count // SLOTS) as i:
                        for j in range(SLOTS):
                            body(i, j)

            def normalise(y, var_before, result):
                for h in range(2):
                    last = done.inc(nc.vector.bn_stats(stats[:, h, :], y[:, h * HALF:(h + 1) * HALF]))
                dve.wait_ge(dve_done, last)
                then(nc.vector.bn_aggr(mean_var[:], stats[:].rearrange("p h s -> p (h s)")))
                nc.vector.tensor_scalar(mean_var[:, 1:2], mean_var[:, 1:2], LN_EPS, None, ALU.add
                                        ).then_inc(var_ready, 1)
                dve.wait_ge(std_ready, var_before + 1)
                then(nc.vector.reciprocal(rstd[:], std[:]))
                then(nc.vector.scalar_tensor_tensor(y, y, mean_var[:, 0:1], gains[:, 0, :],
                                                    ALU.subtract, ALU.mult))
                nc.vector.scalar_tensor_tensor(y, y, rstd[:, 0:1], gains[:, 1, :],
                                               ALU.mult, ALU.add).then_inc(result, 1)

            def residual_norm(name, which, times, split=True):
                dve.wait_ge(gains_in, 32 * (which + 2))
                product = [s[0] for s in stream if s[1] == "rows"].index(name)
                for t in range(TT):
                    if t < TT - 1:
                        dve.wait_ge(tile_summed, product * (TT - 1) + t + 1)
                    else:
                        dve.wait_ge(slab_used, first_slab[name] + dict((s[0], s[2]) for s in stream)[name])
                    for h in range(2):
                        y = x_tok[:, t, h * HALF:(h + 1) * HALF]
                        last = done.inc(nc.vector.scalar_tensor_tensor(y, y, ALPHA, bank[2 * t + h][:],
                                                                       ALU.mult, ALU.add))
                    dve.wait_ge(dve_done, last)
                    normalise(x_tok[:, t, :], (which + 1) * TT + t, x_ready)
                    if t == 2 and times is not None and split:
                        split_x(0, times)
                if times is not None and split:
                    for t in range(1, TT):
                        split_x(t, times)

            def split_x(t, times):
                dve.wait_ge(xT_ready, times * 2 * TT + 2 * (t + 1))
                here = slice(t * P, (t + 1) * P)
                src = xT[:, :, PAD + t * P:PAD + (t + 1) * P]
                then(nc.vector.tensor_copy(xT_hi[:, :, here], src))
                nc.vector.tensor_tensor(xT_lo[:, :, here], src, xT_hi[:, :, here].bitcast(F32), ALU.subtract
                                        ).then_inc(xT_split, 1)

            for t in range(TT):
                split_x(t, 0)
            groups(KT, lambda i, j: low_of(i, j, first_act["v"], lambda k: xT[:, k, PAD:]))
            dve.wait_ge(gains_in, 32)
            for t in range(TT):
                dve.wait_ge(v_read, 2 * t + 2)
                normalise(v_tok[:, t, :], t, v_ready)
            dve.wait_ge(bs_arrived, 16)
            for g in range(GROUPS):
                dve.wait_ge(mixed, g + 1)
                chunk = gatedT[:, g, :].rearrange("p (c t) -> p c t", t=P)
                dve.wait_ge(bank_read, g + 1)
                nc.vector.tensor_tensor(chunk, bank[4 + g % 4][:].rearrange("p (c t) -> p c t", t=P),
                                        bs_all[:, g:g + 1, :].broadcast_to([P, TT, P]), ALU.add
                                        ).then_inc(gated, 1)
                dve.wait_ge(gated, 2 * g + 1)
                nc.vector.tensor_tensor(gatedT[:, g, :], gatedT[:, g, :], uT[:, g, :], ALU.mult
                                        ).then_inc(gated, 1)
            groups(KT, lambda i, j: low_of(i, j, first_act["gm_out"], lambda k: gatedT[:, k, :]))
            residual_norm("gm_out", 0, 1)

            def mlp(layer, up_before):
                def square(i, j):
                    dve.wait_ge(bank_read, i * SLOTS + (up_before + j + 1))
                    nc.vector.tensor_tensor(big[:, i * SLOTS + j, :], relu[:, j % 2, :], relu[:, j % 2, :],
                                            ALU.mult).then_inc(squared, 1)
                groups(FT, square)
                groups(FT, lambda i, j: low_of(i, j, first_act[f"down{layer}"], lambda k: big[:, k, :]))
            mlp(0, KT)
            residual_norm("down0", 1, 2, False)

            then(nc.vector.memset(low_w[LORA:LORA + 1, :], 1.0))
            nc.vector.memset(low_a[LORA:LORA + 1, :], 1.0).then_inc(ones_ready, 1)
            dve.wait_ge(mu_ready, 1)
            dve.wait_ge(xT_ready, 3 * 2 * TT)
            R_MIX, W_MIX, K_MIX, V_MIX, A_MIX, G_MIX = range(6)

            def mix_into(dst, k, m):
                return nc.vector.scalar_tensor_tensor(dst, xxT[:, k, :], mu[:, m, k:k + 1], xT[:, k, PAD:],
                                                      ALU.mult, ALU.add)
            for k in range(KT):
                then(nc.vector.tensor_tensor(xxT[:, k, :], xT[:, k, PAD - 1:PAD - 1 + S], xT[:, k, PAD:],
                                             ALU.subtract))
                if k >= 2:
                    dve.wait_ge(lora_used, k - 1)
                for m, which in enumerate((W_MIX, A_MIX, G_MIX)):
                    mix_into(lora_mix[:, k % 2, m, :], k, which).then_inc(lora_mixed, 1)
            for u, (name, which) in enumerate((("key", K_MIX), ("receptance", R_MIX), ("value", V_MIX))):
                m0 = first_act[name]

                def mix_slab(k):
                    if u * KT + k >= SLOTS:
                        dve.wait_ge(a_lo_ready, m0 + k - SLOTS + 1)
                    mix_into(mix[:, k % SLOTS, :], k, which).then_inc(x_mixed, 1)
                mix_slab(0)
                mix_slab(1)
                for k in range(KT):
                    low_of(k // SLOTS, k % SLOTS, m0, lambda k: mix[:, k % SLOTS, :])
                    if k + 2 < KT:
                        mix_slab(k + 2)

            dve.wait_ge(slab_used, first_slab["rw_out"])
            then(nc.vector.memset(state[:], 0.0))
            then(nc.vector.memset(start[:], 0.0))
            dve.wait_ge(rw_in, 48)
            dve.wait_ge(masks_ready, 1)

            def by_head(ap):
                return ap.rearrange("p (h n) -> p h n", n=N)

            def per_head(k):
                return small[:, k, :].unsqueeze(2).broadcast_to([P, HH, N])

            def prep_link(n, k, instruction):
                instruction.then_inc(prep_linked, 1)
                dve.wait_ge(prep_linked, n.nth(5, k))

            def end_link(s, k, instruction):
                instruction.then_inc(end_linked, 1)
                dve.wait_ge(end_linked, s.nth(5, k))

            def scale_kk(n):
                dve.wait_ge(early_in[n.half], n.loaded())
                nc.vector.tensor_tensor(kkn[:], early[:, n.half, KK, :], k_k[:, n.half * HALF:(n.half + 1) * HALF],
                                        ALU.mult).then_inc(kk_scaled, 1)

            def sum_kk(n):
                dve.wait_ge(kk_squared, n.nth(1, 1))
                nc.vector.tensor_reduce(small[:, SQ, :], by_head(scratch[:]), AX.X, ALU.add).then_inc(ss_ready, 1)

            def decay_before(n):
                dve.wait_ge(cum_summed, n.nth(1, 1))
                nc.vector.scalar_tensor_tensor(p_prev[:], early[:, n.half, SIG, :], -DECAY, bank[4][:],
                                               ALU.mult, ALU.add).then_inc(lx_ready, 1)

            def normalise_kk(n):
                dve.wait_ge(norm_ready, n.nth(1, 1))
                prep_link(n, 1, nc.vector.tensor_scalar(small[:, NORM, :], small[:, NORM, :], 1e-12, None, ALU.max))
                prep_link(n, 2, nc.vector.reciprocal(small[:, RNORM, :], small[:, NORM, :]))
                prep_link(n, 3, nc.vector.tensor_tensor(by_head(kkn[:]), by_head(kkn[:]), per_head(RNORM), ALU.mult))

            def scale_k(n):
                now = early[:, n.half]
                prep_link(n, 4, nc.vector.scalar_tensor_tensor(scratch[:], now[:, AA, :], -1.0,
                                                               k_a[:, n.half * HALF:(n.half + 1) * HALF],
                                                               ALU.add, ALU.mult))
                nc.vector.scalar_tensor_tensor(now[:, KK, :], scratch[:], 1.0, now[:, KK, :],
                                               ALU.add, ALU.mult).then_inc(k_ready, 1)
                dve.wait_ge(k_ready, n.nth(1, 1))
                prep_link(n, 5, nc.vector.scalar_tensor_tensor(scratch[:], kkn[:], -1.0, now[:, AA, :],
                                                               ALU.mult, ALU.mult))

            def decay_ab(n):
                dve.wait_ge(exp_ready, n.nth(4, 2))
                nc.vector.tensor_tensor(tok_ar[:, A_, :], kkn[:], p_prev[:], ALU.mult).then_inc(tok_ready, 1)
                dve.wait_ge(exp_ready, n.nth(4, 3))
                nc.vector.tensor_tensor(tok_bk[:, n.half, 0, :], scratch[:], p_inv[:], ALU.mult).then_inc(tok_ready, 1)

            def decay_kr(n):
                now = early[:, n.half]
                nc.vector.tensor_tensor(tok_bk[:, n.half, 1, :], now[:, KK, :], p_inv[:], ALU.mult).then_inc(tok_ready, 1)
                dve.wait_ge(exp_ready, n.nth(4, 4))
                nc.vector.tensor_tensor(tok_ar[:, R_, :], now[:, RR, :], p_mid[:], ALU.mult).then_inc(tok_ready, 1)

            def sum_bonus(n):
                dve.wait_ge(rk_ready, n.nth(1, 1))
                nc.vector.tensor_reduce(small[:, BONUS + n.half, :], by_head(rk[:]), AX.X, ALU.add
                                        ).then_inc(bonus_ready, 1)

            def start_of(s):
                for e in range(2):
                    rows_, cols_ = slice(e * N, (e + 1) * N), slice(e * N, (e + 1) * N)
                    nc.vector.tensor_tensor(start[rows_, :, cols_], state[rows_, s.half, :, cols_],
                                            decays[rows_, s.half, :, 0:1].broadcast_to([N, PAIRS, N]), ALU.mult
                                            ).then_inc(start_ready, 1)

            def state_behind(s):
                dve.wait_ge(s_summed, s.nth(1, 1))
                for e in range(2):
                    rows_, cols_ = slice(e * N, (e + 1) * N), slice(e * N, (e + 1) * N)
                    now = state[rows_, s.half, :, cols_]
                    end_link(s, e + 1, nc.vector.tensor_tensor(
                        now, bank[6][rows_, :].rearrange("p (a v) -> p a v", v=P)[:, :, cols_],
                        start[rows_, :, cols_], ALU.add))
                    nc.vector.tensor_tensor(now, now, decays[rows_, s.half, :, 1:2].broadcast_to([N, PAIRS, N]),
                                            ALU.mult).then_inc(state_ready, 1)
                dve.wait_ge(state_ready, s.nth(2, 2))

            def centre_y(s):
                dve.wait_ge(y_summed, s.nth(1, 1))
                end_link(s, 3, nc.vector.tensor_reduce(small[:, YSUM, :], by_head(bank[7][:]), AX.X, ALU.add))
                end_link(s, 4, nc.vector.tensor_scalar(small[:, YSUM, :], small[:, YSUM, :], 1.0 / N, None, ALU.mult))
                nc.vector.tensor_tensor(by_head(yc[:]), by_head(bank[7][:]), per_head(YSUM), ALU.subtract
                                        ).then_inc(yc_ready, 1)

            def variance_y(s):
                dve.wait_ge(yq_ready, s.nth(1, 1))
                end_link(s, 5, nc.vector.tensor_reduce(small[:, YVAR, :], by_head(xs[:]), AX.X, ALU.add))
                nc.vector.tensor_scalar(small[:, YVAR, :], small[:, YVAR, :], 1.0 / N, GN_EPS, ALU.mult, ALU.add
                                        ).then_inc(yvar_ready, 1)

            def rstd_y(s):
                dve.wait_ge(ystd_ready, s.nth(1, 1))
                nc.vector.reciprocal(small[:, YR, :], small[:, YSTD, :]).then_inc(yr_ready, 1)

            def four_heads(mask):
                return mask[:].unsqueeze(1).broadcast_to([P, 4, P])

            def iteration(q, s, n):
                if s:
                    start_of(s)
                for h in range(HH):
                    dve.wait_ge(gram_summed, q.nth(HH, h + 1))
                    nc.vector.tensor_tensor(gram[:, q.half, h, :, :].rearrange("p (g a) t -> p g a t", a=2),
                                            bank[4 + h % 4][:].rearrange("p (g a t) -> p g a t", g=2, a=2),
                                            keep_before[:].unsqueeze(1).broadcast_to([P, 2, 2, P]),
                                            ALU.mult).then_inc(gram_ready, 1)
                for g in range(2):
                    four = slice(4 * g, 4 * g + 4)
                    dve.wait_ge(gram_ready, q.nth(HH, 4 * g + 4))
                    nc.vector.tensor_tensor(n_one[:, four, :], gram[:, q.half, four, B_A, :], four_heads(keep_block),
                                            ALU.mult).then_inc(base_ready, 1)
                    dve.wait_ge(inv_copied, q.nth(2 * len(ON_ACT), g + 1))
                    nc.vector.tensor_tensor(buf2[:, four, :], m_full[:, four, :], four_heads(keep_block),
                                            ALU.mult).then_inc(base_ready, 1)
                for g in range(2):
                    four = slice(4 * g, 4 * g + 4)
                    dve.wait_ge(base_ready, q.nth(6, 2 * g + 1))
                    nc.vector.tensor_tensor(inv_t[:, q.half, four, :], n_one[:, four, :], four_heads(ident),
                                            ALU.add).then_inc(base_ready, 1)
                for z in ON_DVE:
                    what, _, _, result, _ = inverse[q.half][z]
                    for g in range(2):
                        dve.wait_ge(inv_summed, q.nth(2 * STAGES, 2 * z + g + 1))
                        four = slice(4 * g, 4 * g + 4)
                        product = bank[2 * (z % 2) + g][:].rearrange("p (h t) -> p h t", t=P)
                        other = four_heads(keep_level[(z - 7) // 3]) if what == "mask" else result[:, four, :]
                        nc.vector.tensor_tensor(result[:, four, :], product, other,
                                                ALU.mult if what == "mask" else ALU.add).then_inc(inv_added, 1)
                    if n and z == 3:
                        scale_kk(n)
                    if s and z == 5:
                        state_behind(s)
                        centre_y(s)
                    if n and z == 8:
                        sum_kk(n)
                    if s and z == 8:
                        variance_y(s)
                    if n and z == 10:
                        decay_before(n)
                    if n and z == 11:
                        normalise_kk(n)
                    if s and z == 11:
                        rstd_y(s)
                    if n and z == 13:
                        scale_k(n)
                    if n and z == 14:
                        decay_ab(n)
                    if n and z == 16:
                        decay_kr(n)
                if n:
                    sum_bonus(n)
            first_step, last_step = Step(0, 0), Step(0, STEPS - 1)
            scale_kk(first_step)
            decay_before(first_step)
            sum_kk(first_step)
            normalise_kk(first_step)
            scale_k(first_step)
            decay_ab(first_step)
            decay_kr(first_step)
            sum_bonus(first_step)
            for z in range(2):
                dve.wait_ge(stage_out[z], 16 * 6 * TT // 2)
            steps(dve, iteration)
            start_of(last_step)
            state_behind(last_step)
            dve.wait_ge(late_used, STEPS - 1)
            centre_y(last_step)
            variance_y(last_step)
            rstd_y(last_step)

            groups(KT, lambda i, j: low_of(i, j, first_act["rw_out"], lambda k: yT[:, k, :]))
            residual_norm("rw_out", 2, 3)
            mlp(1, KT + FT)
            residual_norm("down1", 3, None)

        @block.tensor
        def _(pe):
            def slab_arrived(n):
                pe.wait_ge(w_hi_ready, n + 1)
                pe.wait_ge(w_lo_ready, n + 1)

            def row_tile(j, t, start, stop):
                tok = slice(t * P, (t + 1) * P)
                for a, ws in ((a_hi, (w_hi, w_lo)), (a_lo, (w_hi,))):
                    for w in ws:
                        for h in range(2):
                            last = nc.tensor.matmul(bank[2 * t + h][:], a[:, j, tok], w[:, j, h * HALF:(h + 1) * HALF],
                                                    start=start and a is a_hi and w is w_hi,
                                                    stop=stop and a is a_lo)
                return last

            def row_product(name, count, turning=None, bank_free=None):
                n0, m0 = first_slab[name], first_act[name]

                def arrived(i, j):
                    pe.wait_ge(w_hi_ready, i * SLOTS + (n0 + j + 1))
                    pe.wait_ge(w_lo_ready, i * SLOTS + (n0 + j + 1))
                    pe.wait_ge(a_hi_ready, i * SLOTS + (m0 + j + 1))
                    pe.wait_ge(a_lo_ready, i * SLOTS + (m0 + j + 1))

                def group(i, start):
                    for j in range(SLOTS):
                        arrived(i, j)
                        for t in range(TT):
                            if start and j == 0 and bank_free is not None:
                                bank_free(t)
                            last = row_tile(j, t, start and j == 0, False)
                        last.then_inc(slab_used, 1)
                group(0, True)
                if count > 2 * SLOTS:
                    with pe.Fori(1, count // SLOTS - 1) as i:
                        group(i, False)
                for t in range(TT):
                    for j in range(SLOTS):
                        if t == 0:
                            arrived(count // SLOTS - 1, j)
                        last = row_tile(j, t, False, j == SLOTS - 1)
                        if t == TT - 1:
                            last.then_inc(slab_used, 1)
                    if t < TT - 1:
                        last.then_inc(tile_summed, 1)
                    if turning is not None and t >= 2:
                        turn_x(turning, t - 2)
                if turning is not None:
                    for t in range(2, TT):
                        turn_x(turning, t)

            def column_slab(i, j, n0):
                pe.wait_ge(w_hi_ready, i * SLOTS + (n0 + j + 1))
                pe.wait_ge(w_lo_ready, i * SLOTS + (n0 + j + 1))
                for k in range(KT):
                    col = slice(k * P, (k + 1) * P)
                    nc.tensor.matmul(bank[j][:], w_hi[:, j, col], xT_hi[:, k, :], start=k == 0, stop=False)
                    nc.tensor.matmul(bank[j][:], w_hi[:, j, col], xT_lo[:, k, :], start=False, stop=False)
                    last = nc.tensor.matmul(bank[j][:], w_lo[:, j, col], xT_hi[:, k, :], start=False,
                                            stop=k == KT - 1)
                last.then_inc(slab_used, 1)

            def turn_x(norms, t):
                if norms is not None:
                    pe.wait_ge(x_ready, norms * TT + t + 1)
                for h in range(2):
                    for k in range(4):
                        last = nc.tensor.transpose(bank[2 * t + h][:, k * P:(k + 1) * P],
                                                   x_tok[:, t, (4 * h + k) * P:(4 * h + k + 1) * P], ident[:])
                    last.then_inc(x_turned, 1)

            pe.wait_ge(x_in, 16)
            pe.wait_ge(ident_ready, 1)
            for t in range(TT):
                turn_x(None, t)
            pe.wait_ge(ws_masked, 1)
            for h in range(2):
                pe.wait_ge(xT_ready, 7 + h)
                for g in range(4):
                    last = nc.tensor.transpose(bank[6 + h][:, g * P:(g + 1) * P], ws_in[:, 4 * h + g, :], ident[:])
                last.then_inc(wsT_summed, 1)
            pe.wait_ge(xT_ready, 2 * TT)
            pe.wait_ge(mu_in, 16)
            nc.tensor.transpose(bank[5][:, 0:6 * KT], mu_rows[:], ident[0:6 * KT, 0:6 * KT]).then_inc(mu_turned, 1)
            pe.wait_ge(wsT_ready, 2)
            pe.wait_ge(mu_ready, 1)
            row_product("v", KT)
            pe.wait_ge(xT_split, TT)
            for f in range(KT):
                if f < 4:
                    pe.wait_ge(v_read, f + 1)
                else:
                    pe.wait_ge(bank_read, f - 3)
                column_slab(f // SLOTS, f % SLOTS, first_slab["u"])
            pe.wait_ge(v_ready, TT)
            for g in range(GROUPS):
                if g >= 4:
                    pe.wait_ge(gated, 2 * (g - 4) + 1)
                for c in range(TT):
                    last = nc.tensor.matmul(bank[4 + g % 4][:, c * P:(c + 1) * P], v_tok[:, c, g * P:(g + 1) * P],
                                            wsT[:, g, :], start=True, stop=True)
                last.then_inc(mixed, 1)
            pe.wait_ge(bank_read, KT)
            pe.wait_ge(gated, 2 * GROUPS)
            row_product("gm_out", KT, 0)

            def mlp(layer, splits, up_before, turning):
                n0 = first_slab[f"up{layer}"]
                pe.wait_ge(xT_split, splits)
                for f in range(SLOTS):
                    column_slab(0, f, n0)
                with pe.Fori(1, FT // SLOTS) as i:
                    for j in range(SLOTS):
                        pe.wait_ge(bank_read, i * SLOTS + (up_before + j - SLOTS + 1))
                        column_slab(i, j, n0)
                pe.wait_ge(bank_read, up_before + FT)
                row_product(f"down{layer}", FT, turning)
            mlp(0, 2 * TT, KT, 1)

            pe.wait_ge(xT_ready, 3 * 2 * TT)
            pe.wait_ge(lora_in, 16 * 9)
            for k in range(KT):
                for m, products in enumerate((((0, lw1[:, k, :]),), ((1, la1[:, k, :]),),
                                              ((2, lg1[:, k, 0:P]), (3, lg1[:, k, P:GLORA])))):
                    pe.wait_ge(lora_mixed, 3 * k + m + 1)
                    for b, w in products:
                        last = nc.tensor.matmul(bank[b][0:w.shape[1], :], w, lora_mix[:, k % 2, m, :],
                                                start=k == 0, stop=k == KT - 1)
                if k < KT - 1:
                    last.then_inc(lora_used, 1)
                else:
                    last.then_inc(lora_summed, 1)
            pe.wait_ge(ones_ready, 1)
            pe.wait_ge(low_ready, 4)
            for u, terms in enumerate((((low_w, lw2),), ((low_a, la2),), ((low_g, lg2), (low_gb, lg2b)))):
                for t in range(TT):
                    for h in range(2):
                        if u:
                            pe.wait_ge(proj_read, 8 * (u - 1) + 2 * t + h + 1)
                        for n, (a, w) in enumerate(terms):
                            last = nc.tensor.matmul(bank[2 * t + h][:], a[:, t * P:(t + 1) * P],
                                                    w[:, h * HALF:(h + 1) * HALF], start=n == 0,
                                                    stop=n == len(terms) - 1)
                    last.then_inc(bank_projected, 1)
            for u, name in enumerate(("key", "receptance", "value")):
                row_product(name, KT, None, lambda t: pe.wait_ge(proj_read, 8 * (u + 2) + 2 * t + 2))

            pe.wait_ge(proj_read, 8 * 6)
            pe.wait_ge(masks_ready, 1)
            def head(ap, h):
                return ap[:, h * N:(h + 1) * N]

            def log_decays(n):
                sig = early[:, n.half, SIG, :]
                pe.wait_ge(early_in[n.half], n.loaded())
                nc.tensor.matmul(bank[4][:], cumulate[:], sig, start=True, stop=True)
                for p in range(PAIRS):
                    last = nc.tensor.matmul(bank[5][:, 2 * p:2 * p + 2], sig[:, p * P:(p + 1) * P],
                                            halves[:], start=True, stop=True)
                last.then_inc(cum_summed, 1)

            def interactions(q):
                pe.wait_ge(exp_ready, q.nth(4, 4))
                pe.wait_ge(tok_ready, q.nth(4, 4))
                for p in range(PAIRS):
                    c = slice(p * P, (p + 1) * P)
                    for a, source in enumerate((tok_ar[:, A_, c], tok_ar[:, R_, c],
                                                tok_bk[:, q.half, 0, c], tok_bk[:, q.half, 1, c])):
                        last = nc.tensor.transpose(bank[4 + p][:, a * P:(a + 1) * P], source, ident[:])
                    last.then_inc(turned_summed, 1)
                for p in range(PAIRS):
                    pe.wait_ge(turned_ready, q.nth(PAIRS, p + 1))
                    for e in range(2):
                        h = 2 * p + e
                        pe.wait_ge(turned_ready, q.nth(PAIRS, h % 4 + 1))
                        if h >= 4:
                            pe.wait_ge(gram_ready, q.nth(HH, h - 3))
                        r = slice(e * N, (e + 1) * N)
                        for g, left in enumerate((B_, K_)):
                            last = nc.tensor.matmul(bank[4 + h % 4][:, g * 2 * P:(g + 1) * 2 * P],
                                                    turned4[r, q.half, p, left, :],
                                                    turned4[r, q.half, p, 0:2, :].rearrange("p a t -> p (a t)"),
                                                    start=True, stop=True)
                        last.then_inc(gram_summed, 1)

            def evacuated(q, z, g):
                if z in ON_ACT:
                    pe.wait_ge(inv_copied, q.nth(2 * len(ON_ACT), 2 * ON_ACT.index(z) + g + 1))
                else:
                    pe.wait_ge(inv_added, q.nth(2 * len(ON_DVE), 2 * ON_DVE.index(z) + g + 1))

            def x_product(s):
                pe.wait_ge(start_ready, s.nth(2, 2))
                pe.wait_ge(late_in[s.half], s.loaded())
                for p in range(PAIRS):
                    nc.tensor.matmul(bank[4][:, p * P:(p + 1) * P], turned4[:, s.half, p, A_, :], start[:, p, :],
                                     start=p == 0, stop=False, skip_group_check=True)
                    for h in (2 * p, 2 * p + 1):
                        last = nc.tensor.matmul(head(bank[4], h), gram[:, s.half, h, K_A, :],
                                                head(late[:, s.half, VV, :], h), start=False, stop=True,
                                                skip_group_check=True)
                last.then_inc(x_summed, 1)

            def u_product(s):
                pe.wait_ge(inv_added, s.nth(2 * len(ON_DVE), 2 * len(ON_DVE)))
                pe.wait_ge(xs_ready, s.nth(1, 1))
                for h in range(HH):
                    last = nc.tensor.matmul(head(bank[5], h), inv_t[:, s.half, h, :], head(xs, h),
                                            start=True, stop=True)
                last.then_inc(u_summed, 1)

            def state_change(s):
                pe.wait_ge(us_ready, s.nth(1, 1))
                for p in range(PAIRS):
                    c = slice(p * P, (p + 1) * P)
                    nc.tensor.matmul(bank[6][:, c], tok_bk[:, s.half, 0, c], us[:, c], start=p == 0, stop=False,
                                     skip_group_check=True)
                    last = nc.tensor.matmul(bank[6][:, c], tok_bk[:, s.half, 1, c], late[:, s.half, VV, c],
                                            start=False, stop=True, skip_group_check=True)
                last.then_inc(s_summed, 1)

            def y_product(s):
                for p in range(PAIRS):
                    nc.tensor.matmul(bank[7][:, p * P:(p + 1) * P], turned4[:, s.half, p, R_, :], start[:, p, :],
                                     start=p == 0, stop=False, skip_group_check=True)
                    for h in (2 * p, 2 * p + 1):
                        nc.tensor.matmul(head(bank[7], h), gram[:, s.half, h, B_R, :], head(us, h), start=False,
                                         stop=False, skip_group_check=True)
                        last = nc.tensor.matmul(head(bank[7], h), gram[:, s.half, h, K_R, :],
                                                head(late[:, s.half, VV, :], h), start=False,
                                                stop=True, skip_group_check=True)
                last.then_inc(y_summed, 1)

            def iteration(q, s, n):
                interactions(q)
                for z, (what, left, right, _, _) in enumerate(inverse[q.half]):
                    for g in range(2):
                        if z == 0:
                            pe.wait_ge(gram_ready, q.nth(HH, 4 * g + 4))
                        elif z == 1:
                            pe.wait_ge(base_ready, q.nth(6, 2 * g + 2))
                        elif z == 3:
                            pe.wait_ge(base_ready, q.nth(6, 5 + g))
                        if z >= 1:
                            evacuated(q, z - 1, g)
                        if z >= 2:
                            evacuated(q, z - 2, g)
                        elif s:
                            pe.wait_ge(inv_added, q.nth(2 * len(ON_DVE), 0))
                        for h in range(4 * g, 4 * g + 4):
                            dst = bank[2 * (z % 2) + g][:, (h % 4) * P:(h % 4 + 1) * P]
                            if what == "turn":
                                last = nc.tensor.transpose(dst, left[:, h, :], ident[:])
                            else:
                                last = nc.tensor.matmul(dst, left[:, h, :], right[:, h, :], start=True, stop=True)
                        last.then_inc(inv_summed, 1)
                    if s and z == 0:
                        x_product(s)
                    if s and z == 2:
                        u_product(s)
                    if s and z == 4:
                        state_change(s)
                    if s and z == 5:
                        y_product(s)
                    if n and z == 7:
                        log_decays(n)
            log_decays(Step(0, 0))
            steps(pe, iteration)
            last_step = Step(0, STEPS - 1)
            x_product(last_step)
            u_product(last_step)
            state_change(last_step)
            y_product(last_step)

            for t in range(TT):
                pe.wait_ge(late_used, 2 * t + 2)
                for h in range(2):
                    for k in range(4):
                        last = nc.tensor.transpose(bank[2 * t + h][:, k * P:(k + 1) * P],
                                                   y_tok[:, t, (4 * h + k) * P:(4 * h + k + 1) * P], ident[:])
                    last.then_inc(y_turned, 1)
            pe.wait_ge(yT_ready, 2 * TT)
            row_product("rw_out", KT, 2)
            mlp(1, 3 * TT, KT + FT, None)


_INS = ["x", "ln1_g", "ln1_b", "ln2_g", "ln2_b", "ffn_w1", "ffn_w2", "gm_w_in", "gm_vn_g", "gm_vn_b", "gm_ws",
        "gm_bs", "gm_w_out", "rw_mu", "rw_w_rkv", "rw_w0", "rw_w1", "rw_w2", "rw_a0", "rw_a1", "rw_a2", "rw_g1",
        "rw_g2", "rw_k_k", "rw_k_a", "rw_r_k", "rw_gn_g", "rw_gn_b", "rw_w_o"]


def kernel(**inputs):
    import numpy as np
    import concourse.bacc as bacc
    from concourse.bass_utils import run_bass_kernel_spmd

    nc = bacc.Bacc("TRN2", target_bir_lowering=False, num_devices=1)
    arrays, args = {}, []
    for name in _INS:
        a = np.ascontiguousarray(inputs[name])
        arrays[f"in_{name}"] = a
        args.append(nc.dram_tensor(f"in_{name}", a.shape, mybir.dt.from_np(a.dtype), kind="ExternalInput").ap())
    out = nc.dram_tensor("out_0", inputs["x"].shape, F32, kind="ExternalOutput").ap()
    trunk(nc, *args, out)
    r = run_bass_kernel_spmd(nc, [arrays], core_ids=[0])
    return r.results[0]["out_0"]
```

```python
import math
from contextlib import ExitStack

import concourse.bass as bass
from concourse import mybir

P = 128
SLOTS = 4
LN_EPS = 1e-5
GN_EPS = 64e-5
BASE = 8
LEVELS = (8, 16, 32, 64)

ALU = mybir.AluOpType
ACT = mybir.ActivationFunctionType
AX = mybir.AxisListType
F32 = mybir.dt.float32
F32R = mybir.dt.float32r


class Tally:

    def __init__(self, sem):
        self.sem, self.n = sem, 0

    def inc(self, instruction):
        instruction.then_inc(self.sem, 1)
        self.n += 1
        return self.n


class Step:

    def __init__(self, i, c):
        self.i, self.c, self.half = i, c, c % 2
        self.t = i + c // 2 if c >= 2 else i

    def nth(self, per_step, k):
        return self.i * (2 * per_step) + (self.c * per_step + k)

    def loaded(self):
        return self.i * 16 + (self.c // 2 + 1) * 16


def trunk(nc, x, ln1_g, ln1_b, ln2_g, ln2_b, ffn_w1, ffn_w2, gm_w_in, gm_vn_g, gm_vn_b, gm_ws, gm_bs,
          gm_w_out, rw_mu, rw_w_rkv, rw_w0, rw_w1, rw_w2, rw_a0, rw_a1, rw_a2, rw_g1, rw_g2, rw_k_k,
          rw_k_a, rw_r_k, rw_gn_g, rw_gn_b, rw_w_o, out):
    _, S, D = x.shape
    depth, _, FF = ffn_w1.shape
    GROUPS = gm_ws.shape[1]
    TT, KT, FT = S // P, D // P, FF // P
    ALPHA = (2.0 * depth) ** 0.25
    HALF = D // 2
    HEADS, N = rw_r_k.shape[1:]
    LORA, GLORA = rw_w1.shape[2], rw_g1.shape[2]
    HH = HEADS // 2
    PAIRS = HH // 2
    DECAY = -math.exp(-0.5)
    MID = P // 2
    assert (S, D, HALF) == (512, 1024, 512) and GROUPS == KT and HH * N == HALF

    def rows(w, c0=0):
        v = w.rearrange("(k p) n -> k p n", p=P)
        return lambda k: v[k, :, c0:c0 + D]

    def columns(w):
        v = w.rearrange("(k p) (f c) -> f p k c", p=P, c=P)
        return lambda f: v[f]

    stream = [("v", "rows", KT, rows(gm_w_in[0], D)), ("u", "columns", KT, columns(gm_w_in[0][:, 0:D])),
              ("gm_out", "rows", KT, rows(gm_w_out[0])),
              ("up0", "columns", FT, columns(ffn_w1[0])), ("down0", "rows", FT, rows(ffn_w2[0])),
              ("key", "rows", KT, rows(rw_w_rkv[0, 1])), ("receptance", "rows", KT, rows(rw_w_rkv[0, 0])),
              ("value", "rows", KT, rows(rw_w_rkv[0, 2])), ("rw_out", "rows", KT, rows(rw_w_o[0])),
              ("up1", "columns", FT, columns(ffn_w1[1])), ("down1", "rows", FT, rows(ffn_w2[1]))]
    KIND, COUNT = {s[0]: s[1] for s in stream}, {s[0]: s[2] for s in stream}
    row_products = [s[0] for s in stream if s[1] == "rows"]
    SLABS = sum(s[2] for s in stream)
    first_slab, first_act, at, act_at = {}, {}, 0, 0
    for name, kind, count, _ in stream:
        first_slab[name] = at
        at += count
        if kind == "rows":
            first_act[name] = act_at
            act_at += count

    with ExitStack() as ctx:
        here = [(nc.sbuf_base + 31) // 32 * 32]

        def sb(name, shape, dtype=F32, at=None):
            size = 4
            for s in shape[1:]:
                size *= s
            where = here[0] if at is None else at
            if at is None:
                here[0] += (size + 31) // 32 * 32
            place[name] = where
            return nc.alloc_sbuf_tensor_at(name, shape, dtype, offset=where)

        place = {}

        def sem(name):
            return ctx.enter_context(nc.semaphore(name))

        raw = sb("raw", [P, SLOTS, D])
        w_hi = sb("w_hi", [P, SLOTS, D], F32R)
        w_lo = sb("w_lo", [P, SLOTS, D], F32R)
        a_hi = sb("a_hi", [P, SLOTS, S], F32R)
        a_lo = sb("a_lo", [P, SLOTS, S], F32R)
        PAD = 8
        xT = sb("xT", [P, KT, PAD + S])
        x_tok = sb("x_tok", [P, TT, D])
        xT_hi = sb("xT_hi", [P, KT, S], F32R)
        xT_lo = sb("xT_lo", [P, KT, S], F32R)
        big = sb("big", [P, FT, S])
        gains = sb("gains", [P, 2, D])
        ident = sb("ident", [P, P])
        relu = sb("relu", [P, 2, S])
        stats = sb("stats", [P, 2, 6])
        mean_var = sb("mean_var", [P, 2])
        std = sb("std", [P, 1])
        rstd = sb("rstd", [P, 1])
        v_tok = sb("v_tok", [P, TT, D], at=place["big"])
        uT = sb("uT", [P, KT, S], at=place["big"] + 16384)
        gatedT = sb("gatedT", [P, KT, S], at=place["big"] + 32768)
        ws_in = sb("ws_in", [P, GROUPS, P], at=place["big"] + 49152)
        wsT = sb("wsT", [P, GROUPS, P], at=place["big"] + 53248)
        bs_all = sb("bs_all", [P, GROUPS, P], at=place["big"] + 57344)

        cursor = [0, 0]

        def over(name, shape):
            size = 4
            for n in shape[1:]:
                size *= n
            where, cursor[0] = cursor[0], cursor[0] + (size + 31) // 32 * 32
            assert cursor[0] <= cursor[1], name
            return sb(name, shape, at=where)

        cursor[:] = place["big"] + (FT * S - 4 * D) * 4, place["gains"]
        k_k, k_a, r_k = (over(name, [P, D]) for name in ("k_k", "k_a", "r_k"))
        state = over("state", [P, 2, PAIRS, P])
        cursor[:] = place["relu"], place["relu"] + 4 * D
        keep_before = over("keep_before", [P, 2, P])
        keep_block = over("keep_block", [P, P])
        keep_level = [over(f"keep_level{b}", [P, P]) for b in LEVELS]
        cumulate = over("cumulate", [P, P])
        cursor[:] = place["xT_hi"], place["k_k"]
        lw1 = over("lw1", [P, KT, LORA])
        la1 = over("la1", [P, KT, LORA])
        lg1 = over("lg1", [P, KT, GLORA])
        lw2 = over("lw2", [LORA + 1, D])
        la2 = over("la2", [LORA + 1, D])
        lg2 = over("lg2", [P, D])
        lg2b = over("lg2b", [GLORA - P, D])
        assert cursor[0] <= place["big"]
        low_w = over("low_w", [LORA + 1, S])
        low_a = over("low_a", [LORA + 1, S])
        low_g = over("low_g", [P, S])
        low_gb = over("low_gb", [GLORA - P, S])
        xxT = over("xxT", [P, KT, S])
        lora_mix = over("lora_mix", [P, 2, 3, S])
        mix = over("mix", [P, SLOTS, S])
        stage = over("stage", [P, 2, D])
        cursor[:] = place["xT_hi"], place["k_k"]
        early = over("early", [P, 2, 4, HALF])
        late = over("late", [P, 2, 2, HALF])
        SIG, AA, KK, RR = range(4)
        GG, VV = range(2)
        tok_ar = over("tok_ar", [P, 2, HALF])
        tok_bk = over("tok_bk", [P, 2, 2, HALF])
        A_, R_, B_, K_ = range(4)
        turned4 = over("turned4", [P, 2, PAIRS, 4, P])
        kkn, p_mid, p_inv, p_prev, scratch, k_gain = (over(name, [P, HALF]) for name in
                                                  ("kkn", "p_mid", "p_inv", "p_prev", "scratch", "k_gain"))
        gram_t = over("gram_t", [P, HH, P])
        in_block = over("in_block", [P, HH, P])
        block_n = over("block_n", [P, HH, BASE])
        xs, yc, bonus_v = (over(name, [P, HALF]) for name in ("xs", "yc", "bonus_v"))
        rk = bonus_v
        cursor[:] = place["raw"] + D * 4, place["x_tok"]
        gram = over("gram", [P, 2, HH, 4, P])
        B_A, B_R, K_A, K_R = range(4)
        inv_t = over("inv_t", [P, 2, HH, P])
        inv = over("inv", [P, HH, P])
        level_n = [over("level_n", [P, HH, P]), in_block]
        block_inv = over("block_inv", [P, HH, BASE])
        terms = over("terms", [P, HH, BASE, BASE])
        left_inv = over("left_inv", [P, HH, P])
        spread = over("spread", [P, BASE, HH, BASE])
        us = over("us", [P, HALF])
        start = over("start", [P, PAIRS, P])
        y_tok = over("y_tok", [P, TT, D])
        yT = sb("yT", [P, KT, S], at=place["early"])
        gn = sb("gn", [P, 2, D], at=place["gains"])
        mu = sb("mu", [P, 6, KT])
        mu_rows = sb("mu_rows", [6 * KT, P])
        halves = sb("halves", [P, 2])
        select = sb("select", [P, BASE])
        decays = sb("decays", [P, 2, PAIRS, 2])
        small = sb("small", [P, 9, HH])
        SQ, NORM, RNORM, YSUM, YVAR, YSTD, YR, BONUS = range(8)

        def inverse_of(half):
            growing = inv_t[:, half]
            stages = [("turn", gram[:, half, :, B_A, :], None, gram_t, "act", False)]
            for level in range(len(LEVELS)):
                stages += [("turn", growing, None, inv, "act", True),
                           ("left", level_n[level % 2], growing, left_inv, "act", False),
                           ("add", inv, left_inv, growing, "dve", True)]
            return stages
        inverse = [inverse_of(half) for half in range(2)]
        STAGES = len(inverse[0])
        LEFT = [2 + 3 * level for level in range(len(LEVELS))]
        ON_ACT = [s for s in range(STAGES) if inverse[0][s][4] == "act"]
        ON_DVE = [s for s in range(STAGES) if inverse[0][s][4] == "dve"]

        proj = nc.dram_tensor("proj", (6, TT, P, D), F32, kind="Internal").ap()

        bank = [ctx.enter_context(nc.psum_tensor(f"bank{b}", [P, S], F32)) for b in range(8)]

        raw_in = [sem(f"raw_in{j}") for j in range(SLOTS)]
        w_hi_ready, w_lo_ready, slab_used = sem("w_hi_ready"), sem("w_lo_ready"), sem("slab_used")
        a_hi_ready, a_lo_ready = sem("a_hi_ready"), sem("a_lo_ready")
        tile_summed = sem("tile_summed")
        bank_read = sem("bank_read")
        squared = sem("squared")
        v_read = sem("v_read")
        x_in = [sem(f"x_in{t}") for t in range(TT)]
        gains_in, ws_arrived, bs_arrived = sem("gains_in"), sem("ws_arrived"), sem("bs_arrived")
        ident_ready, ws_masked, wsT_summed, wsT_ready = sem("ident_ready"), sem("ws_masked"), sem("wsT_summed"), sem("wsT_ready")
        x_turned, xT_ready, xT_split = sem("x_turned"), sem("xT_ready"), sem("xT_split")
        var_ready, std_ready, x_ready, v_ready = sem("var_ready"), sem("std_ready"), sem("x_ready"), sem("v_ready")
        mixed, gated = sem("mixed"), sem("gated")
        dve_done, pool_done = sem("dve_done"), sem("pool_done")
        stored = sem("stored")
        lora_in, rw_in, gn_in = sem("lora_in"), sem("rw_in"), sem("gn_in")
        lora_mixed, lora_used, lora_summed, low_ready = sem("lora_mixed"), sem("lora_used"), sem("lora_summed"), sem("low_ready")
        bank_projected, proj_read = sem("bank_projected"), sem("proj_read")
        stage_out = [sem("stage_out0"), sem("stage_out1")]
        x_mixed, ones_ready, masks_ready = sem("x_mixed"), sem("ones_ready"), sem("masks_ready")
        early_in, late_in = [sem("early_in0"), sem("early_in1")], [sem("late_in0"), sem("late_in1")]
        late_used = sem("late_used")
        cum_summed, lx_ready, exp_ready = sem("cum_summed"), sem("lx_ready"), sem("exp_ready")
        kk_scaled, kk_squared, ss_ready, norm_ready, k_ready = (
            sem("kk_scaled"), sem("kk_squared"), sem("ss_ready"), sem("norm_ready"), sem("k_ready"))
        tok_ready, rk_ready, turned_summed, turned_ready = sem("tok_ready"), sem("rk_ready"), sem("turned_summed"), sem("turned_ready")
        gram_summed, gram_ready, base_ready = sem("gram_summed"), sem("gram_ready"), sem("base_ready")
        spread_ready, replicated, base_linked = sem("spread_ready"), sem("replicated"), sem("base_linked")
        state_moved = sem("state_moved")
        level_ready, k_linked = sem("level_ready"), sem("k_linked")
        inv_summed, inv_copied, inv_added = sem("inv_summed"), sem("inv_copied"), sem("inv_added")
        start_ready, x_summed, xs_ready, u_summed, us_ready = (
            sem("start_ready"), sem("x_summed"), sem("xs_ready"), sem("u_summed"), sem("us_ready"))
        mu_in, mu_turned, mu_ready = sem("mu_in"), sem("mu_turned"), sem("mu_ready")
        y_summed, s_summed, state_ready = sem("y_summed"), sem("s_summed"), sem("state_ready")
        yc_ready, yq_ready, yvar_ready, ystd_ready, yr_ready, bonus_ready = (
            sem("yc_ready"), sem("yq_ready"), sem("yvar_ready"), sem("ystd_ready"), sem("yr_ready"),
            sem("bonus_ready"))
        prep_linked, end_linked, pool_linked, rk_scaled = (
            sem("prep_linked"), sem("end_linked"), sem("pool_linked"), sem("rk_scaled"))
        y_turned, yT_ready = [sem("y_turned0"), sem("y_turned1")], [sem("yT_ready0"), sem("yT_ready1")]
        STEPS = 2 * TT

        def steps(engine, iteration):
            iteration(Step(0, 0), None, Step(0, 1))
            with engine.Fori(0, (STEPS - 2) // 2) as i:
                for c in (1, 2):
                    iteration(Step(i, c), Step(i, c - 1), Step(i, c + 1))
            iteration(Step(0, STEPS - 1), Step(0, STEPS - 2), None)

        block = ctx.enter_context(nc.Block())

        @block.sync
        def _(sp):

            def load(name, source, i, j):
                n0 = first_slab[name]
                if n0 + j >= SLOTS or not isinstance(i, int) or i > 0:
                    sp.wait_ge(w_lo_ready, i * SLOTS + (n0 + j - SLOTS + 1))
                dst = raw[:, j, :]
                if KIND[name] == "columns":
                    dst = dst.rearrange("p (k c) -> p k c", c=P)
                sp.dma_start(dst, source(i * SLOTS + j)).then_inc(raw_in[j], 16)

            def load_early(t, half):
                sp.dma_start(early[:, half, :, :],
                             proj[0:4, t, :, half * HALF:(half + 1) * HALF].rearrange("u p n -> p u n")
                             ).then_inc(early_in[half], 16)

            def load_late(t, half):
                sp.dma_start(late[:, half, :, :],
                             proj[4:6, t, :, half * HALF:(half + 1) * HALF].rearrange("u p n -> p u n")
                             ).then_inc(late_in[half], 16)

            for name, _, count, source in stream:
                if count == KT:
                    for i in range(count // SLOTS):
                        for j in range(SLOTS):
                            if (name, i, j) == ("v", 0, 1):
                                for t in range(TT):
                                    sp.dma_start(x_tok[:, t, :], x[0, t * P:(t + 1) * P, :]).then_inc(x_in[t], 16)
                            if (name, i, j) == ("rw_out", 0, 1):
                                for z in range(2):
                                    sp.wait_ge(stage_out[z], 16 * 5 * TT // 2)
                                load_early(0, 0)
                                load_early(0, 1)
                                for z in range(2):
                                    sp.wait_ge(stage_out[z], 16 * 6 * TT // 2)
                                load_late(0, 0)
                                load_late(0, 1)
                                with sp.Fori(1, TT) as t:
                                    for half in range(2):
                                        sp.wait_ge(bonus_ready, t * 2 + (half - 1))
                                        load_early(t, half)
                                        sp.wait_ge(late_used, t * 2 + (half - 1))
                                        load_late(t, half)
                                sp.wait_ge(y_summed, STEPS - 1)
                            load(name, source, i, j)
                        if (name, i) == ("v", 0):
                            sp.dma_start(ws_in[:], gm_ws[0].rearrange("g t s -> t g s")).then_inc(ws_arrived, 16)
                            sp.dma_start(mu_rows[:], rw_mu[0].rearrange("m (k p) -> (m k) p", p=P)).then_inc(mu_in, 16)
                            sp.dma_start(bs_all[:], gm_bs.partition_broadcast(P).rearrange("p a g t -> p (a g) t")
                                         ).then_inc(bs_arrived, 16)
                            for half, vector in enumerate((gm_vn_g, gm_vn_b)):
                                sp.dma_start(gains[:, half, :], vector.partition_broadcast(P).rearrange("p a n -> p (a n)")
                                             ).then_inc(gains_in, 16)
                        if (name, i) == ("key", 0):
                            sp.wait_ge(slab_used, first_slab["key"])
                            for row, vector in ((k_k, rw_k_k), (k_a, rw_k_a),
                                                (r_k, rw_r_k.rearrange("a h n -> a (h n)"))):
                                sp.dma_start(row[:], vector.partition_broadcast(P).rearrange("p a n -> p (a n)")
                                             ).then_inc(rw_in, 16)
                            sp.wait_ge(x_ready, 2 * TT)
                            for g, vector in enumerate((rw_gn_g, rw_gn_b)):
                                sp.dma_start(gn[:, g, :], vector.partition_broadcast(P).rearrange("p a n -> p (a n)")
                                             ).then_inc(gn_in, 16)
                else:
                    for j in range(SLOTS):
                        load(name, source, 0, j)
                    if name == "down0":
                        sp.wait_ge(slab_used, first_slab["down0"])
                        small_loads = ((lw1[:], rw_w1[0].rearrange("(k p) n -> p k n", p=P)),
                                       (la1[:], rw_a1[0].rearrange("(k p) n -> p k n", p=P)),
                                       (lg1[:], rw_g1[0].rearrange("(k p) n -> p k n", p=P)),
                                       (lw2[0:LORA, :], rw_w2[0]), (lw2[LORA:LORA + 1, :], rw_w0),
                                       (la2[0:LORA, :], rw_a2[0]), (la2[LORA:LORA + 1, :], rw_a0),
                                       (lg2[:], rw_g2[0, 0:P]), (lg2b[:], rw_g2[0, P:GLORA]))
                        for i in range(1, count // SLOTS):
                            for j in range(SLOTS):
                                load(name, source, i, j)
                            for dst, small_source in small_loads[2 * (i - 1):2 * i]:
                                sp.dma_start(dst, small_source).then_inc(lora_in, 16)
                    else:
                        with sp.Fori(1, count // SLOTS) as i:
                            for j in range(SLOTS):
                                load(name, source, i, j)
            for t in range(TT):
                sp.wait_ge(x_ready, 3 * TT + t + 1)
                sp.dma_start(out[0, t * P:(t + 1) * P, :], x_tok[:, t, :]).then_inc(stored, 16)
            sp.wait_ge(stored, 16 * TT)

        @block.gpsimd
        def _(pool):
            nc.gpsimd.memset(ident[:], 0.0).then_inc(pool_done, 1)
            pool.wait_ge(pool_done, 1)
            nc.gpsimd.affine_select(out=ident[:], in_=ident[:], compare_op=ALU.not_equal, fill=1.0, base=0,
                                    pattern=[[-1, P]], channel_multiplier=1).then_inc(ident_ready, 1)
            def low_weights(i, j):
                pool.wait_ge(w_hi_ready, i * SLOTS + (j + 1))
                nc.gpsimd.tensor_tensor(w_lo[:, j, :], raw[:, j, :], w_hi[:, j, :].bitcast(F32),
                                        ALU.subtract).then_inc(w_lo_ready, 1)

            def low_groups(first, end):
                with pool.Fori(first, end) as i:
                    for j in range(SLOTS):
                        low_weights(i, j)

            for j in range(SLOTS):
                low_weights(0, j)
            pool.wait_ge(ws_arrived, 16)
            nc.gpsimd.affine_select(out=ws_in[:], in_=ws_in[:], compare_op=ALU.is_ge, fill=0.0, base=0,
                                    pattern=[[0, GROUPS], [-1, P]], channel_multiplier=1).then_inc(ws_masked, 1)
            low_groups(1, first_slab["key"] // SLOTS)
            pool.wait_ge(squared, FT + 2)
            done = Tally(pool_done)
            done.n = 1

            def then(instruction):
                pool.wait_ge(pool_done, done.inc(instruction))

            def keep(out, compare, pattern, base, by_partition):
                then(nc.gpsimd.affine_select(out=out, in_=out, compare_op=compare, fill=0.0, base=base,
                                             pattern=pattern, channel_multiplier=by_partition))
            then(nc.gpsimd.memset(keep_before[:], 1.0))
            keep(keep_before[:, 0, :], ALU.is_gt, [[1, P]], 0, -1)
            keep(keep_before[:, 1, :], ALU.is_ge, [[1, P]], 0, -1)
            then(nc.gpsimd.memset(keep_block[:], 1.0))
            blocks = keep_block[:].rearrange("p (m c) -> p m c", c=BASE)
            keep(blocks, ALU.is_ge, [[-BASE, P // BASE], [0, BASE]], 0, 1)
            keep(blocks, ALU.is_ge, [[BASE, P // BASE], [0, BASE]], BASE - 1, -1)
            for b, level in zip(LEVELS, keep_level):
                then(nc.gpsimd.memset(level[:], 0.0))
                even = level[:].rearrange("p (m e c) -> p m e c", e=2, c=b)[:, :, 0, :]
                then(nc.gpsimd.memset(even, 1.0))
                keep(even, ALU.is_ge, [[-2 * b, P // (2 * b)], [0, b]], -b, 1)
                keep(even, ALU.is_ge, [[2 * b, P // (2 * b)], [0, b]], 2 * b - 1, -1)
            then(nc.gpsimd.memset(cumulate[0:MID, :], -DECAY))
            then(nc.gpsimd.memset(cumulate[MID:P, :], DECAY))
            keep(cumulate[0:MID, :], ALU.is_gt, [[-1, P]], 0, 1)
            keep(cumulate[MID:P, :], ALU.is_ge, [[1, P]], -MID, -1)
            then(nc.gpsimd.memset(halves[:], 0.0))
            then(nc.gpsimd.memset(halves[0:MID, 0:1], DECAY))
            nc.gpsimd.memset(halves[MID:P, 1:2], DECAY).then_inc(masks_ready, 1)
            pool.wait_ge(masks_ready, 1)

            low_groups(first_slab["key"] // SLOTS, first_slab["rw_out"] // SLOTS)
            pool.wait_ge(gn_in, 32)
            pool.wait_ge(rw_in, 48)

            def level_of(q, level):
                if level == 0:
                    pool.wait_ge(base_linked, q.nth(4 + 2 * (BASE - 1), 4))
                for g in range(2):
                    four = slice(4 * g, 4 * g + 4)
                    if level == 0:
                        pool.wait_ge(inv_copied, q.nth(2 * len(ON_ACT), g + 1))
                    elif level >= 2:
                        pool.wait_ge(inv_summed, q.nth(2 * STAGES, 2 * LEFT[level - 2] + g + 1))
                    nc.gpsimd.tensor_tensor(level_n[level % 2][:, four, :], gram_t[:, four, :],
                                            keep_level[level][:].unsqueeze(1).broadcast_to([P, 4, P]), ALU.mult
                                            ).then_inc(level_ready, 1)

            def scale_k(n):
                now, gain = early[:, n.half], k_a[:, n.half * HALF:(n.half + 1) * HALF]

                def link(k, instruction):
                    instruction.then_inc(k_linked, 1)
                    pool.wait_ge(k_linked, n.nth(3, k))
                pool.wait_ge(early_in[n.half], n.loaded())
                link(1, nc.gpsimd.tensor_tensor(k_gain[:], now[:, AA, :], gain, ALU.mult))
                link(2, nc.gpsimd.tensor_tensor(k_gain[:], k_gain[:], gain, ALU.subtract))
                pool.wait_ge(kk_scaled, n.nth(1, 1))
                link(3, nc.gpsimd.tensor_tensor(k_gain[:], k_gain[:], now[:, KK, :], ALU.mult))
                nc.gpsimd.tensor_tensor(now[:, KK, :], now[:, KK, :], k_gain[:], ALU.add).then_inc(k_ready, 1)

            def bonus_terms(n):
                half, col = n.half, slice(n.half * HALF, (n.half + 1) * HALF)
                pool.wait_ge(early_in[half], n.loaded())
                pool.wait_ge(k_ready, n.nth(1, 1))
                nc.gpsimd.tensor_tensor(rk[:], early[:, half, RR, :], early[:, half, KK, :], ALU.mult
                                        ).then_inc(rk_scaled, 1)
                pool.wait_ge(rk_scaled, n.nth(1, 1))
                nc.gpsimd.tensor_tensor(rk[:], rk[:], r_k[:, col], ALU.mult).then_inc(rk_ready, 1)

            def finish(s):
                half, col = s.half, slice(s.half * HALF, (s.half + 1) * HALF)

                def link(k, instruction):
                    instruction.then_inc(pool_linked, 1)
                    pool.wait_ge(pool_linked, s.nth(5, k))

                def heads(ap):
                    return ap.rearrange("p (h n) -> p h n", n=N)

                def per_head(k):
                    return small[:, k, :].unsqueeze(2).broadcast_to([P, HH, N])
                pool.wait_ge(late_in[half], s.loaded())
                pool.wait_ge(bonus_ready, s.nth(1, 2))
                link(1, nc.gpsimd.tensor_tensor(heads(bonus_v[:]), heads(late[:, half, VV, :]),
                                                per_head(BONUS + half), ALU.mult))
                pool.wait_ge(yr_ready, s.nth(1, 1))
                link(2, nc.gpsimd.tensor_tensor(heads(yc[:]), heads(yc[:]), per_head(YR), ALU.mult))
                link(3, nc.gpsimd.tensor_tensor(yc[:], yc[:], gn[:, 0, col], ALU.mult))
                link(4, nc.gpsimd.tensor_tensor(yc[:], yc[:], gn[:, 1, col], ALU.add))
                link(5, nc.gpsimd.tensor_tensor(yc[:], yc[:], bonus_v[:], ALU.add))
                nc.gpsimd.tensor_tensor(y_tok[:, s.t, col], yc[:], late[:, half, GG, :], ALU.mult
                                        ).then_inc(late_used, 1)

            def iteration(q, s, n):
                level_of(q, 0)
                level_of(q, 1)
                if n:
                    scale_k(n)
                level_of(q, 2)
                level_of(q, 3)
                if s:
                    finish(s)
                if n:
                    bonus_terms(n)
            pool.wait_ge(a_lo_ready, first_act["value"] + KT)
            scale_k(Step(0, 0))
            for z in range(2):
                pool.wait_ge(stage_out[z], 16 * 6 * TT // 2)
            bonus_terms(Step(0, 0))
            steps(pool, iteration)
            pool.wait_ge(y_summed, STEPS)
            low_groups(first_slab["rw_out"] // SLOTS, SLABS // SLOTS)

        @block.scalar
        def _(act):
            def load_gains(q, g, b):
                act.wait_ge(x_ready if q > 1 else v_ready, max(q - 1, 1) * TT)
                nc.scalar.dma_start(gains[:, 0, :], g.partition_broadcast(P).rearrange("p a n -> p (a n)")
                                    ).then_inc(gains_in, 16)
                nc.scalar.dma_start(gains[:, 1, :], b.partition_broadcast(P).rearrange("p a n -> p (a n)")
                                    ).then_inc(gains_in, 16)

            def round_weights(i, j, n0):
                n0, j = n0 + j // SLOTS * SLOTS, j % SLOTS
                act.wait_ge(raw_in[j], i * 16 + 16 * (n0 // SLOTS + 1))
                if not isinstance(i, int) or n0 + i * SLOTS >= SLOTS:
                    act.wait_ge(slab_used, i * SLOTS + (n0 + j - SLOTS + 1))
                nc.scalar.activation(w_hi[:, j, :], raw[:, j, :], ACT.Copy).then_inc(w_hi_ready, 1)

            AHEAD = 2

            def ahead(i, j, n0):
                if isinstance(i, int) and n0 + i * SLOTS + j + AHEAD >= SLABS:
                    return
                round_weights(i, j + AHEAD, n0)

            def row_product(name, count, source, wait_source=None, begun=0):
                n0 = first_slab[name]

                def left(i, j):
                    if isinstance(i, int) and i * SLOTS + j < begun:
                        return
                    if wait_source is not None:
                        wait_source(i * SLOTS + j)
                    nc.scalar.activation(a_hi[:, j, :], source(i * SLOTS + j), ACT.Copy).then_inc(a_hi_ready, 1)

                def group(i):
                    for j in range(SLOTS):
                        ahead(i, j, n0)
                        left(i, j)
                group(0)
                if count > 2 * SLOTS:
                    with act.Fori(1, count // SLOTS - 1) as i:
                        group(i)
                i = count // SLOTS - 1
                ahead(i, 0, n0)
                for j in range(SLOTS):
                    left(i, j)
                    if j == SLOTS - 2:
                        ahead(i, 1, n0)

            def next_weights(name, count):
                for j in range(AHEAD, SLOTS):
                    ahead(count // SLOTS - 1, j, first_slab[name])

            def turned(times, t, rounded=False):
                for h in range(2):
                    b = 2 * t + h
                    act.wait_ge(x_turned, times * 2 * TT + b + 1)
                    dst = (xT_hi[:, 4 * h:4 * h + 4, t * P:(t + 1) * P] if rounded
                           else xT[:, 4 * h:4 * h + 4, PAD + t * P:PAD + (t + 1) * P])
                    nc.scalar.activation(dst, bank[b][:].rearrange("p (k t) -> p k t", t=P), ACT.Copy
                                         ).then_inc(xT_ready, 1)

            def std_of(norm, t):
                act.wait_ge(var_ready, norm * TT + t + 1)
                nc.scalar.activation(std[:], mean_var[:, 1:2], ACT.Sqrt).then_inc(std_ready, 1)

            def finish_norm(name, count, norm, times, rounded=False):
                last = count // SLOTS - 1
                for t in range(TT):
                    if t == 2 and times is not None:
                        turned(times, 0, rounded)
                        ahead(last, AHEAD, first_slab[name])
                        turned(times, 1, rounded)
                    if t == TT - 1 and times is not None:
                        ahead(last, AHEAD + 1, first_slab[name])
                        if rounded:
                            for j in range(SLOTS - AHEAD, SLOTS):
                                round_weights(last + 1, j, first_slab[name])
                    std_of(norm, t)
                if times is not None:
                    for t in range(2, TT):
                        turned(times, t, rounded)

            round_weights(0, 0, 0)
            for t in range(TT):
                turned(0, t)
            act.wait_ge(xT_ready, 2 * TT)
            nc.scalar.activation(a_hi[:, 0, :], xT[:, 0, PAD:], ACT.Copy).then_inc(a_hi_ready, 1)
            round_weights(0, 1, 0)
            row_product("v", KT, lambda k: xT[:, k, PAD:], begun=1)
            for t in range(TT):
                if t < TT - 1:
                    act.wait_ge(tile_summed, t + 1)
                else:
                    next_weights("v", KT)
                    act.wait_ge(slab_used, first_slab["u"])
                for h in range(2):
                    nc.scalar.activation(v_tok[:, t, h * HALF:(h + 1) * HALF], bank[2 * t + h][:], ACT.Gelu
                                         ).then_inc(v_read, 1)

            for f in range(KT):
                n0 = first_slab["u"]
                if f in (1, 2, 3, 4):
                    std_of(0, f - 1)
                ahead(f // SLOTS, f % SLOTS, n0)
                if f == KT - 1:
                    for k in range(2):
                        act.wait_ge(gated, 2 * k + 2)
                        nc.scalar.activation(a_hi[:, k, :], gatedT[:, k, :], ACT.Copy).then_inc(a_hi_ready, 1)
                act.wait_ge(slab_used, n0 + f + 1)
                nc.scalar.activation(uT[:, f, :], bank[f % SLOTS][:], ACT.Gelu).then_inc(bank_read, 1)
                if f == 3:
                    for h in range(2):
                        act.wait_ge(wsT_summed, h + 1)
                        nc.scalar.activation(wsT[:, 4 * h:4 * h + 4, :], bank[6 + h][:].rearrange("p (g t) -> p g t", t=P),
                                             ACT.Copy).then_inc(wsT_ready, 1)
                    act.wait_ge(mu_turned, 1)
                    nc.scalar.activation(mu[:].rearrange("p m k -> p (m k)"), bank[5][:, 0:6 * KT], ACT.Copy
                                         ).then_inc(mu_ready, 1)
            load_gains(1, ln1_g[0:1], ln1_b[0:1])
            row_product("gm_out", KT, lambda k: gatedT[:, k, :], lambda k: act.wait_ge(gated, 2 * k + 2), begun=2)
            finish_norm("gm_out", KT, 1, 1, True)

            def mlp(layer):
                n0 = first_slab[f"up{layer}"]

                def up_body(i, j, further=True):
                    act.wait_ge(slab_used, i * SLOTS + (n0 + j + 1))
                    if layer or not (isinstance(i, int) and i == 0 and j < 2):
                        act.wait_ge(squared, i * SLOTS + (FT * layer + j + 1))
                    nc.scalar.activation(relu[:, j % 2, :], bank[j][:], ACT.Relu).then_inc(bank_read, 1)
                    if further:
                        round_weights(i, j + SLOTS, n0)
                with act.Fori(0, FT // SLOTS - 1) as i:
                    for j in range(SLOTS):
                        up_body(i, j)
                for j in range(SLOTS):
                    up_body(FT // SLOTS - 1, j, j < AHEAD)
                    if j < 2:
                        nc.scalar.activation(a_hi[:, j, :], big[:, j, :], ACT.Copy).then_inc(a_hi_ready, 1)
                act.wait_ge(squared, FT * (layer + 1) + 2)
                row_product(f"down{layer}", FT, lambda k: big[:, k, :], begun=2)

            load_gains(2, ln2_g[0:1], ln2_b[0:1])
            mlp(0)
            finish_norm("down0", FT, 2, 2)

            act.wait_ge(lora_summed, 1)
            nc.scalar.activation(low_w[0:LORA, :], bank[4][0:LORA, :], ACT.Tanh).then_inc(low_ready, 1)
            nc.scalar.activation(low_a[0:LORA, :], bank[5][0:LORA, :], ACT.Copy).then_inc(low_ready, 1)
            nc.scalar.activation(low_g[:], bank[6][:], ACT.Sigmoid).then_inc(low_ready, 1)
            nc.scalar.activation(low_gb[:], bank[7][0:GLORA - P, :], ACT.Sigmoid).then_inc(low_ready, 1)

            def projected(u, t, function, weights=None):
                z = u * TT + t
                if z >= 2:
                    act.wait_ge(stage_out[z % 2], 16 * (z // 2))
                for h in range(2):
                    nc.scalar.activation(stage[:, z % 2, h * HALF:(h + 1) * HALF], bank[2 * t + h][:], function
                                         ).then_inc(proj_read, 1)
                act.wait_ge(proj_read, 2 * z + 2)
                nc.scalar.dma_start(proj[(SIG, AA, 4 + GG, KK, RR, 4 + VV)[u], t], stage[:, z % 2, :]).then_inc(stage_out[z % 2], 16)

            def square_kk(n):
                act.wait_ge(kk_scaled, n.nth(1, 1))
                nc.scalar.activation(scratch[:], kkn[:], ACT.Square).then_inc(kk_squared, 1)

            def norm_of(n):
                act.wait_ge(ss_ready, n.nth(1, 1))
                nc.scalar.activation(small[:, NORM, :], small[:, SQ, :], ACT.Sqrt).then_inc(norm_ready, 1)

            products = ("key", "receptance", "value")

            def left_operand(u, k):
                act.wait_ge(x_mixed, u * KT + k + 1)
                nc.scalar.activation(a_hi[:, k % SLOTS, :], mix[:, k % SLOTS, :], ACT.Copy).then_inc(a_hi_ready, 1)

            for u, function in enumerate((ACT.Sigmoid, ACT.Sigmoid, ACT.Copy)):
                for t in range(TT):
                    if (u, t) == (2, 0):
                        left_operand(0, 0)
                    act.wait_ge(bank_projected, TT * u + t + 1)
                    projected(u, t, function)
            for u, name in enumerate(products):
                n0 = first_slab[name]
                for k in range(KT):
                    if k <= KT - SLOTS:
                        ahead(k // SLOTS, k % SLOTS, n0)
                    if k > 0:
                        left_operand(u, k)
                    if k == KT - 2:
                        ahead(1, 1, n0)
                if name == "value":
                    square_kk(Step(0, 0))
                    norm_of(Step(0, 0))
                for t in range(TT):
                    if t < TT - 1:
                        act.wait_ge(tile_summed, row_products.index(name) * (TT - 1) + t + 1)
                    else:
                        if name != "value":
                            next_weights(name, KT)
                            left_operand(u + 1, 0)
                        act.wait_ge(slab_used, n0 + KT)
                    projected(3 + u, t, ACT.Copy)

            def decays_of(n):
                act.wait_ge(lx_ready, n.nth(1, 1))
                nc.scalar.activation(decays[:, n.half], bank[5][:, 0:2 * PAIRS].rearrange("p (a b) -> p a b", b=2),
                                     ACT.Exp).then_inc(exp_ready, 1)
                nc.scalar.activation(p_prev[:], p_prev[:], ACT.Exp).then_inc(exp_ready, 1)
                nc.scalar.activation(p_inv[:], bank[4][:], ACT.Exp, scale=-1.0).then_inc(exp_ready, 1)
                nc.scalar.activation(p_mid[:], bank[4][:], ACT.Exp).then_inc(exp_ready, 1)

            def copy_x(s):
                act.wait_ge(x_summed, s.nth(1, 1))
                nc.scalar.activation(xs[:], bank[4][:], ACT.Copy).then_inc(xs_ready, 1)

            def copy_u(s):
                act.wait_ge(u_summed, s.nth(1, 1))
                nc.scalar.activation(us[:], bank[5][:], ACT.Copy).then_inc(us_ready, 1)

            def square_y(s):
                act.wait_ge(yc_ready, s.nth(1, 1))
                nc.scalar.activation(xs[:], yc[:], ACT.Square).then_inc(yq_ready, 1)

            def std_y(s):
                act.wait_ge(yvar_ready, s.nth(1, 1))
                nc.scalar.activation(small[:, YSTD, :], small[:, YVAR, :], ACT.Sqrt).then_inc(ystd_ready, 1)

            def iteration(q, s, n):
                for p in range(PAIRS):
                    act.wait_ge(turned_summed, q.nth(PAIRS, p + 1))
                    nc.scalar.activation(turned4[:, q.half, p].rearrange("p a t -> p (a t)"), bank[4 + p][:],
                                         ACT.Copy).then_inc(turned_ready, 1)
                for z in range(STAGES):
                    if z in ON_ACT:
                        for g in range(2):
                            act.wait_ge(inv_summed, q.nth(2 * STAGES, 2 * z + g + 1))
                            nc.scalar.activation(inverse[q.half][z][3][:, 4 * g:4 * g + 4, :],
                                                 bank[2 * (z % 2) + g][:].rearrange("p (h t) -> p h t", t=P), ACT.Copy
                                                 ).then_inc(inv_copied, 1)
                    if s and z == 0:
                        copy_x(s)
                        copy_u(s)
                    if n and z == 0:
                        square_kk(n)
                    if s and z == 2:
                        square_y(s)
                    if n and z == 5:
                        decays_of(n)
                    if n and z == 8:
                        norm_of(n)
                    if s and z == 8:
                        std_y(s)
            decays_of(Step(0, 0))
            for z in range(2):
                act.wait_ge(stage_out[z], 16 * 6 * TT // 2)
            steps(act, iteration)
            last_step = Step(0, STEPS - 1)

            def turned_y(t, h):
                act.wait_ge(y_turned[h], t + 1)
                nc.scalar.activation(yT[:, 4 * h:4 * h + 4, t * P:(t + 1) * P],
                                     bank[2 * t + h][:].rearrange("p (k t) -> p k t", t=P), ACT.Copy
                                     ).then_inc(yT_ready[h], 1)
            copy_x(last_step)
            ahead(KT // SLOTS - 1, AHEAD, first_slab["value"])
            turned_y(0, 0)
            turned_y(0, 1)
            copy_u(last_step)
            turned_y(1, 0)
            turned_y(1, 1)
            turned_y(2, 0)
            turned_y(2, 1)
            turned_y(3, 0)
            act.wait_ge(yT_ready[0], TT)
            act.wait_ge(y_summed, STEPS)

            def left_y(k):
                nc.scalar.activation(a_hi[:, k % SLOTS, :], yT[:, k, :], ACT.Copy).then_inc(a_hi_ready, 1)
            left_y(0)
            square_y(last_step)
            ahead(KT // SLOTS - 1, AHEAD + 1, first_slab["value"])
            left_y(1)
            std_y(last_step)
            ahead(0, 0, first_slab["rw_out"])
            left_y(2)
            ahead(0, 1, first_slab["rw_out"])
            left_y(3)
            turned_y(3, 1)
            act.wait_ge(yT_ready[1], TT)
            ahead(0, 2, first_slab["rw_out"])
            ahead(0, 3, first_slab["rw_out"])
            act.wait_ge(late_used, STEPS)
            load_gains(3, ln1_g[1:2], ln1_b[1:2])
            ahead(1, 0, first_slab["rw_out"])
            left_y(4)
            left_y(5)
            left_y(6)
            ahead(1, 1, first_slab["rw_out"])
            left_y(7)
            finish_norm("rw_out", KT, 3, 3, True)
            load_gains(4, ln2_g[1:2], ln2_b[1:2])
            mlp(1)
            finish_norm("down1", FT, 4, None)

        @block.vector
        def _(dve):
            done = Tally(dve_done)

            def then(instruction):
                dve.wait_ge(dve_done, done.inc(instruction))

            then(nc.vector.memset(xT[:, :, 0:PAD], 0.0))
            then(nc.vector.memset(relu[:], 0.0))
            nc.vector.memset(stats[:, 0, :], 0.0).then_inc(squared, 1)
            nc.vector.memset(stats[:, 1, :], 0.0).then_inc(squared, 1)

            def low_of(i, j, m0, source):
                dve.wait_ge(a_hi_ready, i * SLOTS + (m0 + j + 1))
                nc.vector.tensor_tensor(a_lo[:, j, :], source(i * SLOTS + j), a_hi[:, j, :].bitcast(F32),
                                        ALU.subtract).then_inc(a_lo_ready, 1)

            def groups(count, body):
                if count == KT:
                    for i in range(count // SLOTS):
                        for j in range(SLOTS):
                            body(i, j)
                else:
                    with dve.Fori(0, count // SLOTS) as i:
                        for j in range(SLOTS):
                            body(i, j)

            def normalise(y, var_before, result, between=None):
                for h in range(2):
                    last = done.inc(nc.vector.bn_stats(stats[:, h, :], y[:, h * HALF:(h + 1) * HALF]))
                dve.wait_ge(dve_done, last)
                then(nc.vector.bn_aggr(mean_var[:], stats[:].rearrange("p h s -> p (h s)")))
                nc.vector.tensor_scalar(mean_var[:, 1:2], mean_var[:, 1:2], LN_EPS, None, ALU.add
                                        ).then_inc(var_ready, 1)
                if between is not None:
                    between()
                dve.wait_ge(std_ready, var_before + 1)
                then(nc.vector.reciprocal(rstd[:], std[:]))
                then(nc.vector.scalar_tensor_tensor(y, y, mean_var[:, 0:1], gains[:, 0, :],
                                                    ALU.subtract, ALU.mult))
                nc.vector.scalar_tensor_tensor(y, y, rstd[:, 0:1], gains[:, 1, :],
                                               ALU.mult, ALU.add).then_inc(result, 1)

            def residual_norm(name, which, times, split=True):
                dve.wait_ge(gains_in, 32 * (which + 2))
                product = row_products.index(name)
                for t in range(TT):
                    if t < TT - 1:
                        dve.wait_ge(tile_summed, product * (TT - 1) + t + 1)
                    else:
                        dve.wait_ge(slab_used, first_slab[name] + COUNT[name])
                    for h in range(2):
                        y = x_tok[:, t, h * HALF:(h + 1) * HALF]
                        last = done.inc(nc.vector.scalar_tensor_tensor(y, y, ALPHA, bank[2 * t + h][:],
                                                                       ALU.mult, ALU.add))
                    dve.wait_ge(dve_done, last)

                    def low_first():
                        low_x(0, times)
                        low_x(1, times)
                    splits_now = t == 2 and times is not None and split
                    normalise(x_tok[:, t, :], (which + 1) * TT + t, x_ready, low_first if splits_now else None)
                if times is not None and split:
                    for t in range(2, TT):
                        low_x(t, times)

            def low_x(t, times):
                for h in range(2):
                    k = slice(4 * h, 4 * h + 4)
                    dve.wait_ge(xT_ready, times * 2 * TT + 2 * t + h + 1)
                    nc.vector.tensor_tensor(xT_lo[:, k, t * P:(t + 1) * P],
                                            bank[2 * t + h][:].rearrange("p (k t) -> p k t", t=P),
                                            xT_hi[:, k, t * P:(t + 1) * P].bitcast(F32), ALU.subtract
                                            ).then_inc(xT_split, 1)

            def split_x(t, times):
                dve.wait_ge(xT_ready, times * 2 * TT + 2 * (t + 1))
                here = slice(t * P, (t + 1) * P)
                src = xT[:, :, PAD + t * P:PAD + (t + 1) * P]
                then(nc.vector.tensor_copy(xT_hi[:, :, here], src))
                for h in range(2):
                    k = slice(4 * h, 4 * h + 4)
                    nc.vector.tensor_tensor(xT_lo[:, k, here], src[:, k, :], xT_hi[:, k, here].bitcast(F32),
                                            ALU.subtract).then_inc(xT_split, 1)

            groups(KT, lambda i, j: low_of(i, j, first_act["v"], lambda k: xT[:, k, PAD:]))
            for t in range(TT):
                split_x(t, 0)
            dve.wait_ge(gains_in, 32)
            for t in range(TT):
                dve.wait_ge(v_read, 2 * t + 2)
                normalise(v_tok[:, t, :], t, v_ready)
            dve.wait_ge(bs_arrived, 16)
            def low_gated(k):
                low_of(k // SLOTS, k % SLOTS, first_act["gm_out"], lambda k: gatedT[:, k, :])

            for g in range(GROUPS):
                dve.wait_ge(mixed, g + 1)
                chunk = gatedT[:, g, :].rearrange("p (c t) -> p c t", t=P)
                dve.wait_ge(bank_read, g + 1)
                nc.vector.tensor_tensor(chunk, bank[4 + g % 4][:].rearrange("p (c t) -> p c t", t=P),
                                        bs_all[:, g:g + 1, :].broadcast_to([P, TT, P]), ALU.add
                                        ).then_inc(gated, 1)
                dve.wait_ge(gated, 2 * g + 1)
                nc.vector.tensor_tensor(gatedT[:, g, :], gatedT[:, g, :], uT[:, g, :], ALU.mult
                                        ).then_inc(gated, 1)
                if g in (GROUPS - 3, GROUPS - 2):
                    low_gated(g - (GROUPS - 3))
            for k in range(2, KT):
                low_gated(k)
            residual_norm("gm_out", 0, 1)

            def mlp(layer, up_before):
                def square(i, j):
                    dve.wait_ge(bank_read, i * SLOTS + (up_before + j + 1))
                    nc.vector.tensor_tensor(big[:, i * SLOTS + j, :], relu[:, j % 2, :], relu[:, j % 2, :],
                                            ALU.mult).then_inc(squared, 1)

                def low(i, j):
                    low_of(i, j, first_act[f"down{layer}"], lambda k: big[:, k, :])
                last = FT // SLOTS - 1
                with dve.Fori(0, last) as i:
                    for j in range(SLOTS):
                        square(i, j)
                for j in range(SLOTS):
                    square(last, j)
                    if j < 2:
                        low(0, j)
                for j in range(2, SLOTS):
                    low(0, j)
                with dve.Fori(1, last + 1) as i:
                    for j in range(SLOTS):
                        low(i, j)
            mlp(0, KT)
            residual_norm("down0", 1, 2, False)

            dve.wait_ge(mu_ready, 1)
            R_MIX, W_MIX, K_MIX, V_MIX, A_MIX, G_MIX = range(6)

            def mix_into(dst, k, m):
                return nc.vector.scalar_tensor_tensor(dst, xxT[:, k, :], mu[:, m, k:k + 1], xT[:, k, PAD:],
                                                      ALU.mult, ALU.add)
            for k in range(KT):
                dve.wait_ge(xT_ready, 3 * 2 * TT - (1 if k < KT // 2 else 0))
                then(nc.vector.tensor_tensor(xxT[:, k, :], xT[:, k, PAD - 1:PAD - 1 + S], xT[:, k, PAD:],
                                             ALU.subtract))
                if k >= 2:
                    dve.wait_ge(lora_used, k - 1)
                for m, which in enumerate((W_MIX, A_MIX, G_MIX)):
                    mix_into(lora_mix[:, k % 2, m, :], k, which).then_inc(lora_mixed, 1)
            then(nc.vector.memset(low_w[LORA:LORA + 1, :], 1.0))
            nc.vector.memset(low_a[LORA:LORA + 1, :], 1.0).then_inc(ones_ready, 1)
            for u, (name, which) in enumerate((("key", K_MIX), ("receptance", R_MIX), ("value", V_MIX))):
                m0 = first_act[name]

                def mix_slab(k):
                    if u * KT + k >= SLOTS:
                        dve.wait_ge(a_lo_ready, m0 + k - SLOTS + 1)
                    mix_into(mix[:, k % SLOTS, :], k, which).then_inc(x_mixed, 1)
                mix_slab(0)
                mix_slab(1)
                for k in range(KT):
                    low_of(k // SLOTS, k % SLOTS, m0, lambda k: mix[:, k % SLOTS, :])
                    if k + 2 < KT:
                        mix_slab(k + 2)

            dve.wait_ge(rw_in, 48)
            dve.wait_ge(masks_ready, 1)

            def by_head(ap):
                return ap.rearrange("p (h n) -> p h n", n=N)

            def per_head(k):
                return small[:, k, :].unsqueeze(2).broadcast_to([P, HH, N])

            def prep_link(n, k, instruction):
                instruction.then_inc(prep_linked, 1)
                dve.wait_ge(prep_linked, n.nth(4, k))

            def end_link(s, k, instruction):
                instruction.then_inc(end_linked, 1)
                dve.wait_ge(end_linked, s.nth(3, k))

            def scale_kk(n):
                dve.wait_ge(early_in[n.half], n.loaded())
                nc.vector.tensor_tensor(kkn[:], early[:, n.half, KK, :], k_k[:, n.half * HALF:(n.half + 1) * HALF],
                                        ALU.mult).then_inc(kk_scaled, 1)

            def sum_kk(n):
                dve.wait_ge(kk_squared, n.nth(1, 1))
                nc.vector.tensor_reduce(small[:, SQ, :], by_head(scratch[:]), AX.X, ALU.add).then_inc(ss_ready, 1)

            def decay_before(n):
                dve.wait_ge(cum_summed, n.nth(1, 1))
                nc.vector.scalar_tensor_tensor(p_prev[:], early[:, n.half, SIG, :], -DECAY, bank[4][:],
                                               ALU.mult, ALU.add).then_inc(lx_ready, 1)

            def normalise_kk(n):
                dve.wait_ge(norm_ready, n.nth(1, 1))
                prep_link(n, 1, nc.vector.tensor_scalar(small[:, NORM, :], small[:, NORM, :], 1e-12, None, ALU.max))
                prep_link(n, 2, nc.vector.reciprocal(small[:, RNORM, :], small[:, NORM, :]))
                prep_link(n, 3, nc.vector.tensor_tensor(by_head(kkn[:]), by_head(kkn[:]), per_head(RNORM), ALU.mult))

            def scale_b(n):
                prep_link(n, 4, nc.vector.scalar_tensor_tensor(scratch[:], kkn[:], -1.0, early[:, n.half, AA, :],
                                                               ALU.mult, ALU.mult))

            def decay_ab(n):
                dve.wait_ge(exp_ready, n.nth(4, 2))
                nc.vector.tensor_tensor(tok_ar[:, A_, :], kkn[:], p_prev[:], ALU.mult).then_inc(tok_ready, 1)
                dve.wait_ge(exp_ready, n.nth(4, 3))
                nc.vector.tensor_tensor(tok_bk[:, n.half, 0, :], scratch[:], p_inv[:], ALU.mult).then_inc(tok_ready, 1)

            def decay_kr(n):
                now = early[:, n.half]
                dve.wait_ge(k_ready, n.nth(1, 1))
                dve.wait_ge(exp_ready, n.nth(4, 3))
                nc.vector.tensor_tensor(tok_bk[:, n.half, 1, :], now[:, KK, :], p_inv[:], ALU.mult).then_inc(tok_ready, 1)
                dve.wait_ge(exp_ready, n.nth(4, 4))
                nc.vector.tensor_tensor(tok_ar[:, R_, :], now[:, RR, :], p_mid[:], ALU.mult).then_inc(tok_ready, 1)

            def sum_bonus(n):
                dve.wait_ge(rk_ready, n.nth(1, 1))
                nc.vector.tensor_reduce(small[:, BONUS + n.half, :], by_head(rk[:]), AX.X, ALU.add
                                        ).then_inc(bonus_ready, 1)

            def start_of(s):
                for e in range(2):
                    rows_, cols_ = slice(e * N, (e + 1) * N), slice(e * N, (e + 1) * N)
                    nc.vector.tensor_tensor(start[rows_, :, cols_], state[rows_, s.half, :, cols_],
                                            decays[rows_, s.half, :, 0:1].broadcast_to([N, PAIRS, N]), ALU.mult
                                            ).then_inc(start_ready, 1)

            def state_behind(s):
                dve.wait_ge(s_summed, s.nth(1, 1))
                for e in range(2):
                    rows_, cols_ = slice(e * N, (e + 1) * N), slice(e * N, (e + 1) * N)
                    now = state[rows_, s.half, :, cols_]
                    nc.vector.tensor_tensor(now, bank[6][rows_, :].rearrange("p (a v) -> p a v", v=P)[:, :, cols_],
                                            start[rows_, :, cols_], ALU.add).then_inc(state_moved, 1)
                    dve.wait_ge(state_moved, s.nth(2, e + 1))
                    nc.vector.tensor_tensor(now, now, decays[rows_, s.half, :, 1:2].broadcast_to([N, PAIRS, N]),
                                            ALU.mult).then_inc(state_ready, 1)
                dve.wait_ge(state_ready, s.nth(2, 2))

            def centre_y(s):
                dve.wait_ge(y_summed, s.nth(1, 1))
                end_link(s, 1, nc.vector.tensor_reduce(small[:, YSUM, :], by_head(bank[7][:]), AX.X, ALU.add))
                end_link(s, 2, nc.vector.tensor_scalar(small[:, YSUM, :], small[:, YSUM, :], 1.0 / N, None, ALU.mult))
                nc.vector.tensor_tensor(by_head(yc[:]), by_head(bank[7][:]), per_head(YSUM), ALU.subtract
                                        ).then_inc(yc_ready, 1)

            def variance_y(s):
                dve.wait_ge(yq_ready, s.nth(1, 1))
                end_link(s, 3, nc.vector.tensor_reduce(small[:, YVAR, :], by_head(xs[:]), AX.X, ALU.add))
                nc.vector.tensor_scalar(small[:, YVAR, :], small[:, YVAR, :], 1.0 / N, GN_EPS, ALU.mult, ALU.add
                                        ).then_inc(yvar_ready, 1)

            def rstd_y(s):
                dve.wait_ge(ystd_ready, s.nth(1, 1))
                nc.vector.reciprocal(small[:, YR, :], small[:, YSTD, :]).then_inc(yr_ready, 1)

            def four_heads(mask):
                return mask[:].unsqueeze(1).broadcast_to([P, 4, P])

            def iteration(q, s, n):
                if s:
                    start_of(s)
                for h in range(HH):
                    dve.wait_ge(gram_summed, q.nth(HH, h + 1))
                    nc.vector.tensor_tensor(gram[:, q.half, h, :, :].rearrange("p (g a) t -> p g a t", a=2),
                                            bank[4 + h % 4][:].rearrange("p (g a t) -> p g a t", g=2, a=2),
                                            keep_before[:].unsqueeze(1).broadcast_to([P, 2, 2, P]),
                                            ALU.mult).then_inc(gram_ready, 1)
                def link(k, instruction):
                    instruction.then_inc(base_linked, 1)
                    dve.wait_ge(base_linked, q.nth(4 + 2 * (BASE - 1), k))
                for g in range(2):
                    four = slice(4 * g, 4 * g + 4)
                    dve.wait_ge(gram_ready, q.nth(HH, 4 * g + 4))
                    link(2 * g + 1, nc.vector.tensor_tensor(in_block[:, four, :], gram[:, q.half, four, B_A, :],
                                                            four_heads(keep_block), ALU.mult))
                    link(2 * g + 2, nc.vector.tensor_reduce(
                        block_n[:, four, :], in_block[:, four, :].rearrange("p h (m c) -> p h c m", c=BASE),
                        AX.X, ALU.add))
                nc.vector.tensor_tensor(spread[:].rearrange("p j h c -> p j (h c)"),
                                        block_n[:].rearrange("p h c -> p (h c)").unsqueeze(1).broadcast_to([P, BASE, HH * BASE]),
                                        select[:].unsqueeze(2).broadcast_to([P, BASE, HH * BASE]), ALU.mult
                                        ).then_inc(spread_ready, 1)
                if n:
                    scale_kk(n)
                sum_bonus(q)
                dve.wait_ge(replicated, q.nth(1, 1))
                block_rows = bank[2][:].rearrange("p (j h c) -> p h j c", j=BASE, h=HH)
                for c in range(1, BASE):
                    link(2 * c + 3, nc.vector.tensor_tensor(terms[:, :, c, 0:c], block_inv[:, :, 0:c],
                                                            block_rows[:, :, 0:c, c], ALU.mult))
                    link(2 * c + 4, nc.vector.tensor_reduce(block_inv[:, :, c:c + 1], terms[:, :, c, 0:c + 1],
                                                            AX.X, ALU.add))
                for g in range(2):
                    four = slice(4 * g, 4 * g + 4)
                    nc.vector.tensor_tensor(
                        inv_t[:, q.half, four, :].rearrange("p h (m c) -> p h m c", c=BASE),
                        block_inv[:, four, :].unsqueeze(2).broadcast_to([P, 4, P // BASE, BASE]),
                        keep_block[:].rearrange("p (m c) -> p m c", c=BASE).unsqueeze(1).broadcast_to([P, 4, P // BASE, BASE]),
                        ALU.mult).then_inc(base_ready, 1)
                if s:
                    state_behind(s)
                if n:
                    decay_before(n)
                if s:
                    centre_y(s)
                if n:
                    sum_kk(n)
                for g in range(2):
                    dve.wait_ge(base_ready, q.nth(2, g + 1))
                for z in ON_DVE:
                    result = inverse[q.half][z][3]
                    for g in range(2):
                        dve.wait_ge(inv_summed, q.nth(2 * STAGES, 2 * z + g + 1))
                        four = slice(4 * g, 4 * g + 4)
                        product = bank[2 * (z % 2) + g][:].rearrange("p (h t) -> p h t", t=P)
                        nc.vector.tensor_tensor(result[:, four, :], product, result[:, four, :], ALU.add
                                                ).then_inc(inv_added, 1)
                    if s and z == 3:
                        variance_y(s)
                    if n and z == 6:
                        decay_kr(n)
                    if n and z == 9:
                        normalise_kk(n)
                        scale_b(n)
                        decay_ab(n)
                    if s and z == 9:
                        rstd_y(s)
            first_step, last_step = Step(0, 0), Step(0, STEPS - 1)
            scale_kk(first_step)
            sum_kk(first_step)
            normalise_kk(first_step)
            scale_b(first_step)
            decay_before(first_step)
            decay_ab(first_step)
            decay_kr(first_step)
            dve.wait_ge(slab_used, first_slab["rw_out"])
            then(nc.vector.memset(state[:], 0.0))
            then(nc.vector.memset(start[:], 0.0))
            then(nc.vector.tensor_reduce(select[:], ident[:].rearrange("p (m j) -> p j m", j=BASE), AX.X, ALU.add))
            for c in range(BASE):
                here = select[:, c:c + 1].broadcast_to([P, HH])
                then(nc.vector.tensor_copy(terms[:, :, c, c], here))
                if c == 0:
                    then(nc.vector.tensor_copy(block_inv[:, :, 0], here))
            for z in range(2):
                dve.wait_ge(stage_out[z], 16 * 6 * TT // 2)
            steps(dve, iteration)
            start_of(last_step)

            def low_y(k):
                low_of(k // SLOTS, k % SLOTS, first_act["rw_out"], lambda k: yT[:, k, :])
            dve.wait_ge(late_used, STEPS - 1)
            centre_y(last_step)
            half, col = last_step.half, slice(last_step.half * HALF, (last_step.half + 1) * HALF)
            dve.wait_ge(gn_in, 32)
            then(nc.vector.tensor_tensor(by_head(bonus_v[:]), by_head(late[:, half, VV, :]), per_head(BONUS + half),
                                         ALU.mult))
            low_y(0)
            variance_y(last_step)
            low_y(1)
            rstd_y(last_step)
            dve.wait_ge(yr_ready, STEPS)
            then(nc.vector.tensor_tensor(by_head(yc[:]), by_head(yc[:]), per_head(YR), ALU.mult))
            then(nc.vector.tensor_tensor(yc[:], yc[:], gn[:, 0, col], ALU.mult))
            then(nc.vector.tensor_tensor(yc[:], yc[:], gn[:, 1, col], ALU.add))
            then(nc.vector.tensor_tensor(yc[:], yc[:], bonus_v[:], ALU.add))
            nc.vector.tensor_tensor(y_tok[:, TT - 1, col], yc[:], late[:, half, GG, :], ALU.mult).then_inc(late_used, 1)
            for k in range(2, KT):
                low_y(k)
            residual_norm("rw_out", 2, 3)
            mlp(1, KT + FT)
            residual_norm("down1", 3, None)

        @block.tensor
        def _(pe):
            def slab_arrived(n):
                pe.wait_ge(w_hi_ready, n + 1)
                pe.wait_ge(w_lo_ready, n + 1)

            def row_tile(j, t, start, stop):
                tok = slice(t * P, (t + 1) * P)
                for a, ws in ((a_hi, (w_hi, w_lo)), (a_lo, (w_hi,))):
                    for w in ws:
                        for h in range(2):
                            last = nc.tensor.matmul(bank[2 * t + h][:], a[:, j, tok], w[:, j, h * HALF:(h + 1) * HALF],
                                                    start=start and a is a_hi and w is w_hi,
                                                    stop=stop and a is a_lo)
                return last

            def row_product(name, count, turning=None, bank_free=None, split_turns=False,
                            first_tiles=range(TT), begun=False):
                n0, m0 = first_slab[name], first_act[name]

                def arrived(i, j):
                    pe.wait_ge(w_hi_ready, i * SLOTS + (n0 + j + 1))
                    pe.wait_ge(w_lo_ready, i * SLOTS + (n0 + j + 1))
                    pe.wait_ge(a_hi_ready, i * SLOTS + (m0 + j + 1))
                    pe.wait_ge(a_lo_ready, i * SLOTS + (m0 + j + 1))

                def group(i, start):
                    for j in range(SLOTS):
                        arrived(i, j)
                        for t in first_tiles if start and j == 0 else range(TT):
                            if start and j == 0 and bank_free is not None:
                                bank_free(t)
                            last = row_tile(j, t, start and j == 0, False)
                        last.then_inc(slab_used, 1)
                if not begun:
                    group(0, True)
                if count > 2 * SLOTS:
                    with pe.Fori(1, count // SLOTS - 1) as i:
                        group(i, False)
                for t in range(TT):
                    for j in range(SLOTS):
                        if t == 0:
                            arrived(count // SLOTS - 1, j)
                        last = row_tile(j, t, False, j == SLOTS - 1)
                        if t == TT - 1:
                            last.then_inc(slab_used, 1)
                        if turning is not None and t >= 2 and j == 0:
                            turn_x(turning, t - 2)
                    if t < TT - 1:
                        last.then_inc(tile_summed, 1)
                if turning is not None and not split_turns:
                    for t in range(2, TT):
                        turn_x(turning, t)

            def column_slab(i, j, n0, tokens=slice(0, S), used=True):
                pe.wait_ge(w_hi_ready, i * SLOTS + (n0 + j + 1))
                pe.wait_ge(w_lo_ready, i * SLOTS + (n0 + j + 1))
                for k in range(KT):
                    col = slice(k * P, (k + 1) * P)
                    dst = bank[j][:, tokens]
                    nc.tensor.matmul(dst, w_hi[:, j, col], xT_hi[:, k, tokens], start=k == 0, stop=False)
                    nc.tensor.matmul(dst, w_hi[:, j, col], xT_lo[:, k, tokens], start=False, stop=False)
                    last = nc.tensor.matmul(dst, w_lo[:, j, col], xT_hi[:, k, tokens], start=False,
                                            stop=k == KT - 1)
                if used:
                    last.then_inc(slab_used, 1)

            def turn_x(norms, t):
                if norms is not None:
                    pe.wait_ge(x_ready, norms * TT + t + 1)
                for h in range(2):
                    for k in range(4):
                        last = nc.tensor.transpose(bank[2 * t + h][:, k * P:(k + 1) * P],
                                                   x_tok[:, t, (4 * h + k) * P:(4 * h + k + 1) * P], ident[:])
                    last.then_inc(x_turned, 1)

            pe.wait_ge(ident_ready, 1)
            for t in range(TT):
                pe.wait_ge(x_in[t], 16)
                turn_x(None, t)
            pe.wait_ge(xT_ready, 2 * TT)
            row_product("v", KT)
            pe.wait_ge(xT_split, 2 * TT)
            def mix_tokens(g):
                pe.wait_ge(v_ready, TT)
                pe.wait_ge(wsT_ready, 2)
                pe.wait_ge(mu_ready, 1)
                if g >= 4:
                    pe.wait_ge(gated, 2 * (g - 4) + 1)
                for c in range(TT):
                    last = nc.tensor.matmul(bank[4 + g % 4][:, c * P:(c + 1) * P], v_tok[:, c, g * P:(g + 1) * P],
                                            wsT[:, g, :], start=True, stop=True)
                last.then_inc(mixed, 1)

            for f in range(KT):
                if f < 4:
                    pe.wait_ge(v_read, f + 1)
                else:
                    pe.wait_ge(bank_read, f - 3)
                column_slab(f // SLOTS, f % SLOTS, first_slab["u"])
                if f == 2:
                    pe.wait_ge(v_read, 2 * TT)
                    pe.wait_ge(ws_masked, 1)
                    for h in range(2):
                        for g in range(4):
                            last = nc.tensor.transpose(bank[6 + h][:, g * P:(g + 1) * P], ws_in[:, 4 * h + g, :], ident[:])
                        last.then_inc(wsT_summed, 1)
                    pe.wait_ge(mu_in, 16)
                    nc.tensor.transpose(bank[5][:, 0:6 * KT], mu_rows[:], ident[0:6 * KT, 0:6 * KT]).then_inc(mu_turned, 1)
                if f >= KT // 2:
                    for g in (2 * f - KT, 2 * f - KT + 1):
                        mix_tokens(g)
            def gelu_or_gate_read(t):
                if t < 2:
                    pe.wait_ge(bank_read, KT - 4 + 2 * t + 2)
                else:
                    pe.wait_ge(gated, 2 * (GROUPS - 8 + 2 * t + 1) + 1)
            row_product("gm_out", KT, 0, split_turns=True, bank_free=gelu_or_gate_read)

            def mlp(layer, norms, splits, up_before, turning):
                n0 = first_slab[f"up{layer}"]
                pe.wait_ge(xT_split, splits + TT)
                for f in range(SLOTS):
                    column_slab(0, f, n0, slice(0, 2 * P), False)
                    if f in (1, 2):
                        turn_x(norms, f + 1)
                pe.wait_ge(xT_split, splits + 2 * TT)
                for f in range(SLOTS):
                    column_slab(0, f, n0, slice(2 * P, S))
                with pe.Fori(1, FT // SLOTS) as i:
                    for j in range(SLOTS):
                        pe.wait_ge(bank_read, i * SLOTS + (up_before + j - SLOTS + 1))
                        column_slab(i, j, n0)
                def relu_read(t):
                    if t < 2:
                        pe.wait_ge(bank_read, up_before + FT - 4 + 2 * t + 2)
                row_product(f"down{layer}", FT, turning, first_tiles=(2, 3, 0, 1), bank_free=relu_read)
            mlp(0, 0, 2 * TT, KT, 1)

            pe.wait_ge(xT_ready, 3 * 2 * TT)
            pe.wait_ge(lora_in, 16 * 9)
            for k in range(KT):
                for m, products in enumerate((((4, lw1[:, k, :]),), ((5, la1[:, k, :]),),
                                              ((6, lg1[:, k, 0:P]), (7, lg1[:, k, P:GLORA])))):
                    pe.wait_ge(lora_mixed, 3 * k + m + 1)
                    for b, w in products:
                        last = nc.tensor.matmul(bank[b][0:w.shape[1], :], w, lora_mix[:, k % 2, m, :],
                                                start=k == 0, stop=k == KT - 1)
                if k < KT - 1:
                    last.then_inc(lora_used, 1)
                else:
                    last.then_inc(lora_summed, 1)
            pe.wait_ge(ones_ready, 1)
            pe.wait_ge(low_ready, 1)
            for u, terms in enumerate((((low_w, lw2),), ((low_a, la2),), ((low_g, lg2), (low_gb, lg2b)))):
                for t in range(TT):
                    if (u, t) == (0, 2):
                        pe.wait_ge(low_ready, 4)
                    for h in range(2):
                        if u:
                            pe.wait_ge(proj_read, 8 * (u - 1) + 2 * t + h + 1)
                        for n, (a, w) in enumerate(terms):
                            last = nc.tensor.matmul(bank[2 * t + h][:], a[:, t * P:(t + 1) * P],
                                                    w[:, h * HALF:(h + 1) * HALF], start=n == 0,
                                                    stop=n == len(terms) - 1)
                    last.then_inc(bank_projected, 1)
            for u, name in enumerate(("key", "receptance", "value")):
                row_product(name, KT, None, lambda t: pe.wait_ge(proj_read, 8 * (u + 2) + 2 * t + 2))

            pe.wait_ge(masks_ready, 1)
            def head(ap, h):
                return ap[:, h * N:(h + 1) * N]

            def log_decays(n):
                sig = early[:, n.half, SIG, :]
                pe.wait_ge(early_in[n.half], n.loaded())
                nc.tensor.matmul(bank[4][:], cumulate[:], sig, start=True, stop=True)
                for p in range(PAIRS):
                    last = nc.tensor.matmul(bank[5][:, 2 * p:2 * p + 2], sig[:, p * P:(p + 1) * P],
                                            halves[:], start=True, stop=True)
                last.then_inc(cum_summed, 1)

            def interactions(q):
                pe.wait_ge(exp_ready, q.nth(4, 4))
                pe.wait_ge(tok_ready, q.nth(4, 4))
                for p in range(PAIRS):
                    c = slice(p * P, (p + 1) * P)
                    for a, source in enumerate((tok_ar[:, A_, c], tok_ar[:, R_, c],
                                                tok_bk[:, q.half, 0, c], tok_bk[:, q.half, 1, c])):
                        last = nc.tensor.transpose(bank[4 + p][:, a * P:(a + 1) * P], source, ident[:])
                    last.then_inc(turned_summed, 1)
                for p in range(PAIRS):
                    pe.wait_ge(turned_ready, q.nth(PAIRS, p + 1))
                    for e in range(2):
                        h = 2 * p + e
                        pe.wait_ge(turned_ready, q.nth(PAIRS, h % 4 + 1))
                        if h >= 4:
                            pe.wait_ge(gram_ready, q.nth(HH, h - 3))
                        r = slice(e * N, (e + 1) * N)
                        for g, left in enumerate((B_, K_)):
                            last = nc.tensor.matmul(bank[4 + h % 4][:, g * 2 * P:(g + 1) * 2 * P],
                                                    turned4[r, q.half, p, left, :],
                                                    turned4[r, q.half, p, 0:2, :].rearrange("p a t -> p (a t)"),
                                                    start=True, stop=True)
                        last.then_inc(gram_summed, 1)

            def evacuated(q, z, g):
                if z in ON_ACT:
                    pe.wait_ge(inv_copied, q.nth(2 * len(ON_ACT), 2 * ON_ACT.index(z) + g + 1))
                else:
                    pe.wait_ge(inv_added, q.nth(2 * len(ON_DVE), 2 * ON_DVE.index(z) + g + 1))

            def x_product(s):
                pe.wait_ge(start_ready, s.nth(2, 2))
                pe.wait_ge(late_in[s.half], s.loaded())
                for p in range(PAIRS):
                    nc.tensor.matmul(bank[4][:, p * P:(p + 1) * P], turned4[:, s.half, p, A_, :], start[:, p, :],
                                     start=p == 0, stop=False, skip_group_check=True)
                    for h in (2 * p, 2 * p + 1):
                        last = nc.tensor.matmul(head(bank[4], h), gram[:, s.half, h, K_A, :],
                                                head(late[:, s.half, VV, :], h), start=False, stop=True,
                                                skip_group_check=True)
                last.then_inc(x_summed, 1)

            def u_product(s):
                pe.wait_ge(inv_added, s.nth(2 * len(ON_DVE), 2 * len(ON_DVE)))
                pe.wait_ge(xs_ready, s.nth(1, 1))
                for h in range(HH):
                    last = nc.tensor.matmul(head(bank[5], h), inv_t[:, s.half, h, :], head(xs, h),
                                            start=True, stop=True)
                last.then_inc(u_summed, 1)

            def state_change(s):
                pe.wait_ge(us_ready, s.nth(1, 1))
                for p in range(PAIRS):
                    c = slice(p * P, (p + 1) * P)
                    nc.tensor.matmul(bank[6][:, c], tok_bk[:, s.half, 0, c], us[:, c], start=p == 0, stop=False,
                                     skip_group_check=True)
                    last = nc.tensor.matmul(bank[6][:, c], tok_bk[:, s.half, 1, c], late[:, s.half, VV, c],
                                            start=False, stop=True, skip_group_check=True)
                last.then_inc(s_summed, 1)

            def y_product(s):
                for p in range(PAIRS):
                    nc.tensor.matmul(bank[7][:, p * P:(p + 1) * P], turned4[:, s.half, p, R_, :], start[:, p, :],
                                     start=p == 0, stop=False, skip_group_check=True)
                    for h in (2 * p, 2 * p + 1):
                        nc.tensor.matmul(head(bank[7], h), gram[:, s.half, h, B_R, :], head(us, h), start=False,
                                         stop=False, skip_group_check=True)
                        last = nc.tensor.matmul(head(bank[7], h), gram[:, s.half, h, K_R, :],
                                                head(late[:, s.half, VV, :], h), start=False,
                                                stop=True, skip_group_check=True)
                last.then_inc(y_summed, 1)

            def iteration(q, s, n):
                interactions(q)
                for z, (what, left, right, _, _, next_to_last) in enumerate(inverse[q.half]):
                    for g in range(2):
                        if z == 0:
                            pe.wait_ge(gram_ready, q.nth(HH, 4 * g + 4))
                        elif z == 1:
                            pe.wait_ge(base_ready, q.nth(2, 2))
                        if z in LEFT:
                            pe.wait_ge(level_ready, q.nth(2 * len(LEVELS), 2 * LEFT.index(z) + g + 1))
                        if next_to_last:
                            evacuated(q, z - 1, g)
                        if z >= 2:
                            evacuated(q, z - 2, g)
                        elif s:
                            pe.wait_ge(inv_added, q.nth(2 * len(ON_DVE), 0))
                        for h in range(4 * g, 4 * g + 4):
                            dst = bank[2 * (z % 2) + g][:, (h % 4) * P:(h % 4 + 1) * P]
                            if what == "turn":
                                last = nc.tensor.transpose(dst, left[:, h, :], ident[:])
                            else:
                                last = nc.tensor.matmul(dst, left[:, h, :], right[:, h, :], start=True, stop=True)
                        last.then_inc(inv_summed, 1)
                    if z > 0:
                        continue
                    if s:
                        x_product(s)
                    pe.wait_ge(spread_ready, q.nth(1, 1))
                    nc.tensor.matmul(bank[2][:], keep_block[:], spread[:].rearrange("p j h c -> p (j h c)"),
                                     start=True, stop=True).then_inc(replicated, 1)
                    if s:
                        u_product(s)
                        state_change(s)
                    if n:
                        log_decays(n)
                    if s:
                        y_product(s)
            pe.wait_ge(proj_read, 8 * 5 + 6)
            log_decays(Step(0, 0))
            pe.wait_ge(proj_read, 8 * 6)
            steps(pe, iteration)
            last_step = Step(0, STEPS - 1)

            def turn_y(t, h):
                pe.wait_ge(late_used, 2 * t + h + 1)
                for k in range(4):
                    last = nc.tensor.transpose(bank[2 * t + h][:, k * P:(k + 1) * P],
                                               y_tok[:, t, (4 * h + k) * P:(4 * h + k + 1) * P], ident[:])
                last.then_inc(y_turned[h], 1)
            x_product(last_step)
            pe.wait_ge(inv_added, 2 * len(ON_DVE) * STEPS)
            turn_y(0, 0)
            turn_y(0, 1)
            u_product(last_step)
            turn_y(1, 0)
            turn_y(1, 1)
            pe.wait_ge(us_ready, STEPS)
            turn_y(2, 0)
            turn_y(2, 1)
            y_product(last_step)
            turn_y(3, 0)
            for j in range(SLOTS):
                slab_arrived(first_slab["rw_out"] + j)
                pe.wait_ge(a_hi_ready, first_act["rw_out"] + j + 1)
                pe.wait_ge(a_lo_ready, first_act["rw_out"] + j + 1)
                for t in range(TT - 1):
                    if j == 0:
                        pe.wait_ge(yT_ready[0], t + 1)
                        pe.wait_ge(yT_ready[1], t + 1)
                    row_tile(j, t, j == 0, False)
            turn_y(3, 1)
            pe.wait_ge(yT_ready[1], TT)
            for j in range(SLOTS):
                row_tile(j, TT - 1, j == 0, False).then_inc(slab_used, 1)
            row_product("rw_out", KT, 2, split_turns=True, begun=True)
            mlp(1, 2, 4 * TT, KT + FT, None)


_INS = ["x", "ln1_g", "ln1_b", "ln2_g", "ln2_b", "ffn_w1", "ffn_w2", "gm_w_in", "gm_vn_g", "gm_vn_b", "gm_ws",
        "gm_bs", "gm_w_out", "rw_mu", "rw_w_rkv", "rw_w0", "rw_w1", "rw_w2", "rw_a0", "rw_a1", "rw_a2", "rw_g1",
        "rw_g2", "rw_k_k", "rw_k_a", "rw_r_k", "rw_gn_g", "rw_gn_b", "rw_w_o"]


def kernel(**inputs):
    import numpy as np
    import concourse.bacc as bacc
    from concourse.bass_utils import run_bass_kernel_spmd

    nc = bacc.Bacc("TRN2", target_bir_lowering=False, num_devices=1)
    arrays, args = {}, []
    for name in _INS:
        a = np.ascontiguousarray(inputs[name])
        arrays[f"in_{name}"] = a
        args.append(nc.dram_tensor(f"in_{name}", a.shape, mybir.dt.from_np(a.dtype), kind="ExternalInput").ap())
    out = nc.dram_tensor("out_0", inputs["x"].shape, F32, kind="ExternalOutput").ap()
    trunk(nc, *args, out)
    r = run_bass_kernel_spmd(nc, [arrays], core_ids=[0])
    return r.results[0]["out_0"]
```
